# Optimizing a Trainium2 kernel written in Bass

```python
import jax, jax.numpy as jnp
from jax import lax
import numpy as np

D_MODEL = 1024
BATCH = 1
SEQ = 1024
DEPTH = 2
DEC_BATCH = 8
DEC_SEQ = 1
PAST_LEN = 4096
PAGE_SIZE = 128

N_A_LAYERS = DEPTH // 2
N_B_LAYERS = DEPTH - N_A_LAYERS
HEAD_DIM = 64
A_GROUPS = ((128, 1), (512, 4), (2048, 16))
N_GROUPS = len(A_GROUPS)
A_HEADS = D_MODEL // (2 * HEAD_DIM)
B_HEADS = D_MODEL // HEAD_DIM
B_KV_HEADS = 2
B_WINDOW = 128
D_FF = 2816
CONV_W = 3
ROPE_THETA = 10000.0
EPS = 1e-6
BLOCK = 128

kernel_name = "yoco_dilated_swa_sink_convffn_step"

def rms_norm(x, g):
    xf = x.astype(jnp.float32)
    y = xf * lax.rsqrt(jnp.mean(xf * xf, axis=-1, keepdims=True) + EPS)
    return (y * g.astype(jnp.float32)).astype(x.dtype)

def rope(x, pos):
    half = HEAD_DIM // 2
    inv_freq = ROPE_THETA ** (-jnp.arange(half, dtype=jnp.float32) / half)
    ang = pos.astype(jnp.float32)[:, None] * inv_freq[None, :]
    cos = jnp.cos(ang)[:, None, :]
    sin = jnp.sin(ang)[:, None, :]
    xf = x.astype(jnp.float32)
    x1, x2 = xf[..., :half], xf[..., half:]
    return jnp.concatenate([x1 * cos - x2 * sin, x2 * cos + x1 * sin], axis=-1).astype(x.dtype)

def softmax_lse(s):
    m = jnp.max(s, axis=-1, keepdims=True)
    e = jnp.exp(s - m)
    den = jnp.sum(e, axis=-1, keepdims=True)
    return e / den, (m + jnp.log(den))[..., 0]

def banded_attention(q, k, v, max_dist):
    n, L, H, hd = q.shape
    kvh = k.shape[2]
    rep = H // kvh
    blk = min(BLOCK, L)
    nb = -(-L // blk)
    pad = nb * blk - L
    qb = jnp.pad(q, ((0, 0), (0, pad), (0, 0), (0, 0))).reshape(n, nb, blk, kvh, rep, hd)
    span = max_dist + blk
    idx = jnp.arange(nb)[:, None] * blk + jnp.arange(span)[None, :]
    kpad = ((0, 0), (max_dist, pad), (0, 0), (0, 0))
    kb = jnp.pad(k, kpad)[:, idx]
    vb = jnp.pad(v, kpad)[:, idx]
    kpos = idx - max_dist
    qpos = jnp.arange(nb)[:, None] * blk + jnp.arange(blk)[None, :]
    dist = qpos[:, :, None] - kpos[:, None, :]
    valid = (dist >= 0) & (dist <= max_dist) & (kpos[:, None, :] >= 0)
    s = jnp.einsum('nbqgrd,nbkgd->nbgrqk', qb, kb).astype(jnp.float32) * (hd ** -0.5)
    s = jnp.where(valid[None, :, None, None], s, -jnp.inf)
    p, lse = softmax_lse(s)
    o = jnp.einsum('nbgrqk,nbkgd->nbqgrd', p.astype(v.dtype), vb)
    o = o.reshape(n, nb * blk, H, hd)[:, :L]
    lse = lse.transpose(0, 1, 4, 2, 3).reshape(n, nb * blk, H)[:, :L]
    return o, lse

def dilated_attention_prompt(q, k, v, window, dil):
    n, S, H, hd = q.shape
    L = S // dil
    def split(t):
        return t.reshape(n, L, dil, H, hd).transpose(0, 2, 1, 3, 4).reshape(n * dil, L, H, hd)
    o, lse = banded_attention(split(q), split(k), split(v), window // dil)
    o = o.reshape(n, dil, L, H, hd).transpose(0, 2, 1, 3, 4).reshape(n, S, H, hd)
    lse = lse.reshape(n, dil, L, H).transpose(0, 2, 1, 3).reshape(n, S, H)
    return o, lse

def dilated_attention_sample(q, k_new, v_new, kv_cache, window, dil):
    n, T, H, hd = q.shape
    wb = kv_cache.shape[2]
    kc = jnp.concatenate([kv_cache[:, 0].astype(k_new.dtype), k_new], axis=1)
    vc = jnp.concatenate([kv_cache[:, 1].astype(v_new.dtype), v_new], axis=1)
    m = jnp.arange(window // dil + 1)
    idx = wb + jnp.arange(T)[:, None] - m[None, :] * dil
    valid = idx >= 0
    idxc = jnp.maximum(idx, 0)
    kg = kc[:, idxc]
    vg = vc[:, idxc]
    s = jnp.einsum('nthd,ntmhd->nthm', q, kg).astype(jnp.float32) * (hd ** -0.5)
    s = jnp.where(valid[None, :, None, :], s, -jnp.inf)
    p, lse = softmax_lse(s)
    o = jnp.einsum('nthm,ntmhd->nthd', p.astype(vc.dtype), vg)
    new_cache = jnp.stack([kc[:, T:], vc[:, T:]], axis=1)
    return o, lse, new_cache

def a_mixer(hn, pos, caches, w_in, q_g, k_g, w_out):
    n, T, _ = hn.shape
    qkv = (hn @ w_in).reshape(n, T, 3, N_GROUPS, A_HEADS, HEAD_DIM)
    outs, lses, rows = [], [], []
    for g, (window, dil) in enumerate(A_GROUPS):
        q = rope(rms_norm(qkv[:, :, 0, g], q_g[g]), pos)
        k = rope(rms_norm(qkv[:, :, 1, g], k_g[g]), pos)
        v = qkv[:, :, 2, g]
        if caches is None:
            o, lse = dilated_attention_prompt(q, k, v, window, dil)
            keep = min(window, T)
            new = jnp.stack([k[:, T - keep:], v[:, T - keep:]], axis=1)
        else:
            o, lse, new = dilated_attention_sample(q, k, v, caches[g], window, dil)
        outs.append(o)
        lses.append(lse)
        rows.append(new)
    wts = jax.nn.softmax(jnp.stack(lses, axis=0), axis=0)
    o = jnp.einsum('gnthd,gnth->nthd', jnp.stack(outs, axis=0), wts.astype(outs[0].dtype))
    return o.reshape(n, T, A_HEADS * HEAD_DIM) @ w_out, rows

def shared_kv(h, pos, kv_norm_g, w_kv, k_norm_g):
    n, T, _ = h.shape
    kv = (rms_norm(h, kv_norm_g) @ w_kv).reshape(n, T, 2, B_KV_HEADS, HEAD_DIM)
    k = rope(rms_norm(kv[:, :, 0], k_norm_g), pos)
    return k, kv[:, :, 1]

def b_attention_sample(q, kc, vc, pos):
    n, T, H, hd = q.shape
    K = kc.shape[1]
    kpos = PAST_LEN + T - K + jnp.arange(K)
    dist = pos[:, None] - kpos[None, :]
    valid = (dist >= 0) & (dist < B_WINDOW)
    qg = q.reshape(n, T, B_KV_HEADS, H // B_KV_HEADS, hd)
    s = jnp.einsum('ntgrd,nkgd->ntgrk', qg, kc).astype(jnp.float32) * (hd ** -0.5)
    s = jnp.where(valid[None, :, None, None, :], s, -jnp.inf)
    p, lse = softmax_lse(s)
    o = jnp.einsum('ntgrk,nkgd->ntgrd', p.astype(vc.dtype), vc)
    return o.reshape(n, T, H, hd), lse.reshape(n, T, H)

def conv_ffn(hn, conv_state, w_up, conv_w, conv_b, w_down):
    T = hn.shape[1]
    u = hn @ w_up
    uc = jnp.concatenate([conv_state.astype(u.dtype), u], axis=1)
    c = sum((conv_w[j] * uc[:, j:j + T] for j in range(CONV_W)), conv_b)
    gate, val = jnp.split(c, 2, axis=-1)
    return (jax.nn.silu(gate) * val) @ w_down, uc[:, T:]

def trunk(x, sample, a_caches, b_cache, conv_state, attn_norm_g, ffn_norm_g, a_w_in, a_q_norm_g,
          a_k_norm_g, a_w_out, b_kv_norm_g, b_w_kv, b_k_norm_g, b_w_q, b_q_norm_g, b_sinks, b_w_out,
          ffn_w_up, ffn_conv_w, ffn_conv_b, ffn_w_down):
    n, T, _ = x.shape
    pos = (PAST_LEN if sample else 0) + jnp.arange(T)
    h = x
    new_a = [[] for _ in A_GROUPS]
    new_conv = []
    k_sh = v_sh = new_b = None
    for layer in range(DEPTH):
        hn = rms_norm(h, attn_norm_g[layer])
        if layer < N_A_LAYERS:
            caches = [c[layer] for c in a_caches] if sample else None
            mix, rows = a_mixer(hn, pos, caches, a_w_in[layer], a_q_norm_g[layer],
                                a_k_norm_g[layer], a_w_out[layer])
            for g in range(N_GROUPS):
                new_a[g].append(rows[g])
        else:
            if layer == N_A_LAYERS:
                k_sh, v_sh = shared_kv(h, pos, b_kv_norm_g, b_w_kv, b_k_norm_g)
                if sample:
                    k_sh = jnp.concatenate([b_cache[:, 0].astype(k_sh.dtype), k_sh], axis=1)
                    v_sh = jnp.concatenate([b_cache[:, 1].astype(v_sh.dtype), v_sh], axis=1)
                    new_b = jnp.stack([k_sh[:, T:], v_sh[:, T:]], axis=1)
                else:
                    keep = min(B_WINDOW, T)
                    new_b = jnp.stack([k_sh[:, T - keep:], v_sh[:, T - keep:]], axis=1)
            j = layer - N_A_LAYERS
            q = (hn @ b_w_q[j]).reshape(n, T, B_HEADS, HEAD_DIM)
            q = rope(rms_norm(q, b_q_norm_g[j]), pos)
            if sample:
                o, lse = b_attention_sample(q, k_sh, v_sh, pos)
            else:
                o, lse = banded_attention(q, k_sh, v_sh, B_WINDOW - 1)
            o = o * jax.nn.sigmoid(lse - b_sinks[j].astype(jnp.float32))[..., None].astype(o.dtype)
            mix = o.reshape(n, T, B_HEADS * HEAD_DIM) @ b_w_out[j]
        h = h + mix
        cs = conv_state[layer] if sample else jnp.zeros((n, CONV_W - 1, 2 * D_FF), h.dtype)
        f, ncs = conv_ffn(rms_norm(h, ffn_norm_g[layer]), cs, ffn_w_up[layer], ffn_conv_w[layer],
                          ffn_conv_b[layer], ffn_w_down[layer])
        h = h + f
        new_conv.append(ncs)
    a_out = [jnp.stack(r, axis=0) for r in new_a]
    return h, a_out, new_b, jnp.stack(new_conv, axis=0)

def setup_inputs(seed: int = 0) -> dict:
    key = jax.random.key(seed)
    ks = iter(jax.random.split(key, 40))

    def nrm(shape, scale):
        return scale * jax.random.normal(next(ks), shape, jnp.float32)

    def gain(shape):
        return 1.0 + 0.05 * jax.random.normal(next(ks), shape, jnp.float32)

    def a_cache(window):
        return nrm((N_A_LAYERS, DEC_BATCH, 2, min(window, PAST_LEN), A_HEADS, HEAD_DIM), 1.0)

    tap_bias = (jnp.arange(CONV_W) == CONV_W - 1).astype(jnp.float32)[None, :, None]
    return {
        "x_prompt": nrm((BATCH, SEQ, D_MODEL), 1.0),
        "x_sample": nrm((DEC_BATCH, DEC_SEQ, D_MODEL), 1.0),
        "cache_a_kv_w128": a_cache(A_GROUPS[0][0]),
        "cache_a_kv_w512": a_cache(A_GROUPS[1][0]),
        "cache_a_kv_w2048": a_cache(A_GROUPS[2][0]),
        "cache_b_kv": nrm((DEC_BATCH, 2, min(B_WINDOW, PAST_LEN), B_KV_HEADS, HEAD_DIM), 1.0),
        "state_ffn_conv": nrm((DEPTH, DEC_BATCH, CONV_W - 1, 2 * D_FF), 1.0),
        "attn_norm_g": gain((DEPTH, D_MODEL)),
        "ffn_norm_g": gain((DEPTH, D_MODEL)),
        "a_w_in": nrm((N_A_LAYERS, D_MODEL, 3 * N_GROUPS * A_HEADS * HEAD_DIM), D_MODEL ** -0.5),
        "a_q_norm_g": gain((N_A_LAYERS, N_GROUPS, HEAD_DIM)),
        "a_k_norm_g": gain((N_A_LAYERS, N_GROUPS, HEAD_DIM)),
        "a_w_out": nrm((N_A_LAYERS, A_HEADS * HEAD_DIM, D_MODEL), (A_HEADS * HEAD_DIM) ** -0.5),
        "b_kv_norm_g": gain((D_MODEL,)),
        "b_w_kv": nrm((D_MODEL, 2 * B_KV_HEADS * HEAD_DIM), D_MODEL ** -0.5),
        "b_k_norm_g": gain((HEAD_DIM,)),
        "b_w_q": nrm((N_B_LAYERS, D_MODEL, B_HEADS * HEAD_DIM), D_MODEL ** -0.5),
        "b_q_norm_g": gain((N_B_LAYERS, HEAD_DIM)),
        "b_sinks": nrm((N_B_LAYERS, B_HEADS), 1.0),
        "b_w_out": nrm((N_B_LAYERS, B_HEADS * HEAD_DIM, D_MODEL), (B_HEADS * HEAD_DIM) ** -0.5),
        "ffn_w_up": nrm((DEPTH, D_MODEL, 2 * D_FF), D_MODEL ** -0.5),
        "ffn_conv_w": nrm((DEPTH, CONV_W, 2 * D_FF), 0.3) + tap_bias,
        "ffn_conv_b": nrm((DEPTH, 2 * D_FF), 0.02),
        "ffn_w_down": nrm((DEPTH, D_FF, D_MODEL), D_FF ** -0.5),
    }

def reference(x_prompt, x_sample, cache_a_kv_w128, cache_a_kv_w512, cache_a_kv_w2048, cache_b_kv,
              state_ffn_conv, attn_norm_g, ffn_norm_g, a_w_in, a_q_norm_g, a_k_norm_g, a_w_out,
              b_kv_norm_g, b_w_kv, b_k_norm_g, b_w_q, b_q_norm_g, b_sinks, b_w_out,
              ffn_w_up, ffn_conv_w, ffn_conv_b, ffn_w_down):
    weights = (attn_norm_g, ffn_norm_g, a_w_in, a_q_norm_g, a_k_norm_g, a_w_out, b_kv_norm_g,
               b_w_kv, b_k_norm_g, b_w_q, b_q_norm_g, b_sinks, b_w_out,
               ffn_w_up, ffn_conv_w, ffn_conv_b, ffn_w_down)
    y_prompt, a_p, b_p, conv_p = trunk(x_prompt, False, None, None, None, *weights)
    y_sample, a_s, b_s, conv_s = trunk(
        x_sample, True, (cache_a_kv_w128, cache_a_kv_w512, cache_a_kv_w2048),
        cache_b_kv, state_ffn_conv, *weights)
    return (y_prompt, y_sample, a_p[0], a_s[0], a_p[1], a_s[1], a_p[2], a_s[2], b_p, b_s, conv_p, conv_s)


_drawn_inputs = setup_inputs


def setup_inputs(seed=0):
    import zlib

    import numpy as np

    out = dict(_drawn_inputs(seed))
    spreads = {}
    factors = {'a_q_norm_g': 7.068, 'b_q_norm_g': 8.0, 'b_sinks': 7.785}
    for name, (base, spread) in spreads.items():
        noise = np.random.default_rng([zlib.crc32(name.encode()), seed]).standard_normal(out[name].shape)
        drawn = base * np.exp(spread * noise) if base else spread * noise
        out[name] = __import__('jax').numpy.asarray(drawn.astype(out[name].dtype))
    for name, factor in factors.items():
        out[name] = (out[name] * factor).astype(out[name].dtype)
    return out
```

```python
from contextlib import ExitStack

import numpy as np

import concourse.bass as bass
from concourse import mybir

F32 = mybir.dt.float32
F32R = mybir.dt.float32r
BF16 = mybir.dt.bfloat16
ALU = mybir.AluOpType
ACT = mybir.ActivationFunctionType
AX_X = mybir.AxisListType.X

P = 128
D = 1024
KC = D // P
SEQ = 1024
NS = 8
T = SEQ + NS
NT = 3
TH = T // NT
HD = 64
DFF = 2816
FC = DFF // P
PAST = 4096
GROUPS = ((128, 1), (512, 4), (2048, 16))
NG = len(GROUPS)
A_PAIRS = 4
B_CHUNKS = 8
EPS = 1e-6
SCALE = HD ** -0.5
MASKED = -1e30
RING = 3
BODY = 6
A_CHUNKS = 36
NTILE = SEQ // P

U_QKV = RING
U_AOUT = U_QKV + A_CHUNKS
U_FFN0 = U_AOUT + 4
FFN_TURNS = FC // 2
FFN_UNITS = 6 * FFN_TURNS
U_KV = U_FFN0 + FFN_UNITS
U_BQ = U_KV + 2
U_BOUT = U_BQ + B_CHUNKS
U_FFN1 = U_BOUT + 8
U_END = U_FFN1 + FFN_UNITS

C_ID, C_ONES, C_BLK, C_ROT, C_E64, C_E128 = 0, 128, 256, 384, 512, 520
C_MQ, C_MK = 528, 1040
C_COS, C_SIN = 1552, 1552 + T
C_END = C_SIN + T
CUR, PREV_A, BOTH, PREV_B = range(4)


def shape_constants():
    c = np.zeros((P, C_END), np.float32)
    i = np.arange(P)
    c[:, C_ID:C_ID + P] = np.eye(P)
    c[:, C_ONES:C_ONES + P] = 1.0
    c[:, C_BLK:C_BLK + P] = i[:, None] // HD == i[None, :] // HD
    for m in range(P):
        half = m % HD < HD // 2
        c[m + HD // 2 if half else m - HD // 2, C_ROT + m] = -1.0 if half else 1.0
    c[:, C_E64:C_E64 + NS] = i[:, None] % NS == np.arange(NS)
    c[:, C_E128:C_E128 + NS] = i[:, None] % NS == np.arange(NS)
    q, k = i[:, None], i[None, :]
    valid = [k <= q, k >= q, (k <= q) & (k % 2 == q % 2), k > q]
    for n, v in enumerate(valid):
        m = np.where(v, 0.0, MASKED)
        c[:, C_MQ + n * P:C_MQ + (n + 1) * P] = m
        c[:, C_MK + n * P:C_MK + (n + 1) * P] = m.T
    pos = np.concatenate([np.arange(SEQ), np.full(NS, PAST)]).astype(np.float32)
    inv = (10000.0 ** (-np.arange(HD // 2) / (HD // 2))).astype(np.float32)
    ang = (pos[None, :] * inv[i % (HD // 2), None]).astype(np.float32)
    c[:, C_COS:C_COS + T] = np.cos(ang.astype(np.float64))
    c[:, C_SIN:C_SIN + T] = np.sin(ang.astype(np.float64))
    return c


class Mixer:

    def __init__(self, groups):
        self.ng = groups
        b = []
        prev = PREV_A if groups > 1 else PREV_B
        cols = 8 * groups
        for g in range(groups):
            kind = BOTH if g == 2 else CUR
            for t in (0, 4):
                b.append((g, kind, [(t + e, t + e, 8 * g + t + e) for e in range(4)]))
        b.append((0, prev, [(t, t - 1, cols + t - 1) for t in range(1, 5)]))
        b.append((0, prev, [(t, t - 1, cols + t - 1) for t in range(5, 8)]))
        if groups > 1:
            b.append((1, prev, [(2 * r + 1, 2 * r, cols + 7 + r) for r in range(4)]))
        self.batches = b
        self.cols = cols + 7 + (4 if groups > 1 else 0)


def tile_tokens(x, g, tile):
    if g == 0:
        return x[:, P * tile:P * tile + P]
    if g == 1:
        r, b = divmod(tile, 2)
        return x.rearrange("p (n s) -> p s n", s=4)[:, r, P * b:P * b + P]
    return x.rearrange("p (n s) -> p s n", s=8)[:, tile, :]


def batch_tokens(x, g, kind, blocks):
    t0 = blocks[0][0]
    if g == 0:
        return x[:, P * t0:P * (t0 + len(blocks))]
    if g == 1:
        s = x.rearrange("p (n s) -> p s n", s=4)
        return s[:, 0:4, P:2 * P] if kind == PREV_A else s[:, t0 // 2:t0 // 2 + 2, :]
    return x.rearrange("p (n s) -> p s n", s=8)[:, t0:t0 + 4, :]


def build(nc, a, outs):
    with ExitStack() as ctx:
        def sb(name, shape, dt=F32):
            return ctx.enter_context(nc.sbuf_tensor(name, shape, dt))

        def sem(name):
            return ctx.enter_context(nc.semaphore(name))

        hT = sb("hT", [P, KC, T])
        xh = sb("xh", [P, KC, T], F32R)
        xl = sb("xl", [P, KC, T], F32R)
        w_raw = sb("w_raw", [P, RING, 1024])
        w_hi = sb("w_hi", [P, RING, 1024], F32R)
        w_lo = sb("w_lo", [P, RING, 1024], F32R)
        f_hi = sb("f_hi", [P, 2, T], F32R)
        f_lo = sb("f_lo", [P, 2, T], F32R)
        cst = sb("cst", [P, 528])
        rope = sb("rope", [P, 2, T])
        masks = sb("masks", [P, 2, 4, P], BF16)
        ident_b = sb("ident_b", [P, P], BF16)
        sel = sb("sel", [2, 2, P], F32R)
        sel_den = sb("sel_den", [2, 2, P])
        neg_max = sb("neg_max", [2, SEQ], F32R)
        rinv = sb("rinv", [P, T])
        norm_g = sb("norm_g", [P, 5, KC])
        head_g = sb("head_g", [P, 46])
        eps = sb("eps", [P, 1])
        cw = sb("cw", [P, 2, 4, 2 * FC])
        st_T = sb("st_T", [P, 2, NS, 4 * FC])
        u_tail = sb("u_tail", [P, 10, 2 * FC])
        sink8 = sb("sink8", [2, B_CHUNKS])
        sink = sb("sink", [2, B_CHUNKS])
        sink_now = sb("sink_now", [2, 1])
        sink_col = sb("sink_col", [P, 1])
        ARENA = 10800
        arena = sb("arena", [P, ARENA])
        acc = ctx.enter_context(nc.psum_tensor("acc", [P, 6, 512], F32))
        aux = ctx.enter_context(nc.psum_tensor("aux", [P, 2, 512], F32))

        ident = cst[:, C_ID:C_ID + P]
        ones = cst[:, C_ONES:C_ONES + P]
        blk = cst[:, C_BLK:C_BLK + P]
        rot = cst[:, C_ROT:C_ROT + P]

        def carve(*sizes):
            at, views = 0, []
            for s in sizes:
                views.append(arena[:, at:at + s])
                at += s
            assert at <= ARENA, at
            return views

        scratch = nc.dram_tensor("scratch", [46, P, T], F32).ap()

        ident_in = sem("ident_in")
        const_in = sem("const_in")
        const_set = sem("const_set")
        x_in = [sem(f"x_in{i}") for i in range(2)]
        x_turned = sem("x_turned")
        h_set = sem("h_set")
        tab_in = sem("tab_in")
        gain_rows_set = sem("gain_rows_set")
        gains_turned = sem("gains_turned")
        gains_set = sem("gains_set")
        tab_turned = sem("tab_turned")
        tab_set = sem("tab_set")
        w_landed = [sem(f"w_landed{i}") for i in range(RING)]
        hi_ready = sem("hi_ready")
        lo_ready = sem("lo_ready")
        w_used = sem("w_used")
        n_sq = sem("n_sq")
        n_mm = sem("n_mm")
        n_stat = sem("n_stat")
        n_x = sem("n_x")
        n_hi = sem("n_hi")
        n_lo = sem("n_lo")
        third_full = sem("third_full")
        acc_evac = sem("acc_evac")
        ssq_ready = sem("ssq_ready")
        rot_ready = sem("rot_ready")
        ln_done = sem("ln_done")
        r_ready = sem("r_ready")
        rot_used = sem("rot_used")
        qk_step = sem("qk_step")
        chunk_out = sem("chunk_out")
        stored = [sem(f"stored{i}") for i in range(2)]
        res_full = sem("res_full")
        h_added = sem("h_added")
        up_evac = sem("up_evac")
        conv_step = sem("conv_step")
        conv_out = sem("conv_out")
        e_ready = sem("e_ready")
        f_raw = sem("f_raw")
        fhi_ready = sem("fhi_ready")
        flo_ready = sem("flo_ready")
        d_done = sem("d_done")
        tail_turned = sem("tail_turned")
        tail_set = sem("tail_set")
        tail_out = sem("tail_out")
        y_turned = sem("y_turned")
        y_set = sem("y_set")
        y_out = [sem(f"y_out{i}") for i in range(2)]
        copied = sem("copied")
        chain = sem("chain")

        class Attn:
            def __init__(self, p):
                self.loaded = sem(f"{p}_loaded")
                self.moved = sem(f"{p}_moved")
                self.copied = sem(f"{p}_copied")
                self.exported = sem(f"{p}_exported")
                self.scored = sem(f"{p}_scored")
                self.maxed = sem(f"{p}_maxed")
                self.merged = sem(f"{p}_merged")
                self.turned = sem(f"{p}_turned")
                self.rowed = sem(f"{p}_rowed")
                self.shift = sem(f"{p}_shift")
                self.sc_full = sem(f"{p}_sc_full")
                self.sc_exp = sem(f"{p}_sc_exp")
                self.pv = sem(f"{p}_pv")
                self.o_rec = sem(f"{p}_o_rec")
                self.o_norm = sem(f"{p}_o_norm")
                self.o_hi = sem(f"{p}_o_hi")
                self.o_lo = sem(f"{p}_o_lo")
        SA, SB = Attn("a"), Attn("b")

        class Sample:
            def __init__(self, p):
                self.cols = sem(f"{p}_cols")
                self.cache = [sem(f"{p}_cache{i}") for i in range(4)]
                self.prep = sem(f"{p}_prep")
                self.moved = sem(f"{p}_moved")
                self.kt = sem(f"{p}_kt")
                self.scored = sem(f"{p}_scored")
                self.step = sem(f"{p}_step")
                self.act = sem(f"{p}_act")
                self.pe = sem(f"{p}_pe")
                self.out = sem(f"{p}_out")
                self.fin = sem(f"{p}_fin")
        ZA, ZB = Sample("sa"), Sample("sb")

        MA, MB = Mixer(NG), Mixer(1)

        def unit_at(u0, m=0, i=0):
            assert m % RING == 0
            if m:
                return u0 % RING, u0 + m * i, u0 // RING + (m // RING) * i
            return u0 % RING, u0, u0 // RING

        def load(sp, src, u0, m=0, i=0):
            slot, u, _ = unit_at(u0, m, i)
            sp.wait_ge(lo_ready, u - RING + 1)
            sp.dma_start(w_raw[:, slot, :].rearrange("p (k n) -> p k n", n=src.shape[-1]), src) \
                .then_inc(w_landed[slot], 16)

        def split_hi(act, u0, m=0, i=0):
            slot, u, use = unit_at(u0, m, i)
            act.wait_ge(w_landed[slot], 16 * use)
            act.wait_ge(w_used, u - RING + 1)
            act.copy(w_hi[:, slot, :], w_raw[:, slot, :]).then_inc(hi_ready, 1)

        def split_ahead(act, u0, m=0, i=0):
            if m or u0 + 2 < U_END:
                split_hi(act, u0 + 2, m, i)

        def split_lo(pool, u0, m=0, i=0):
            slot, u, _ = unit_at(u0, m, i)
            pool.wait_ge(hi_ready, u + 1)
            pool.tensor_tensor(w_lo[:, slot, :], w_raw[:, slot, :], w_hi[:, slot, :].bitcast(F32),
                               ALU.subtract).then_inc(lo_ready, 1)

        def product(pe, out, whi, wlo, ahi, alo, first, last):
            pe.matmul(out, whi, ahi, start=first, stop=False)
            pe.matmul(out, whi, alo, start=False, stop=False)
            return pe.matmul(out, wlo, ahi, start=False, stop=last)

        def thirds(x):
            return x.rearrange("p (t n) -> p t n", n=TH)

        def acc_set(n):
            return acc[:, 3 * (n % 2):3 * (n % 2) + 3, 0:TH]

        def wcols(w, c, width=P):
            return w.rearrange("(k p) (c n) -> p k c n", p=P, n=width)[:, :, c, :]

        w_in = a["a_w_in"].rearrange("l k n -> (l k) n")
        w_aout = a["a_w_out"].rearrange("l k n -> (l k) n")
        w_q = a["b_w_q"].rearrange("l k n -> (l k) n")
        w_bout = a["b_w_out"].rearrange("l k n -> (l k) n")

        xs = carve(1024, 1024, 512, 512, 1024, 1024)
        x_stage, cw_stage, st_stage = xs[0:2], xs[2:4], xs[4:6]
        y_stage = xs[0:2]
        xp = a["x_prompt"].rearrange("b s d -> (b s) d")
        xsm = a["x_sample"].rearrange("b s d -> (b s) d")

        def rows_in_sp(sp):
            sp.dma_start(cst[:], a["consts"][:, 0:528]).then_inc(ident_in, 16)
            for n in range(NTILE + 1):
                if n >= 2:
                    sp.wait_ge(x_turned, n - 1)
                if n < NTILE:
                    sp.dma_start(x_stage[n % 2], xp[P * n:P * n + P, :]).then_inc(x_in[n % 2], 16)
                else:
                    sp.dma_start(x_stage[n % 2][0:NS], xsm).then_inc(x_in[n % 2], 16)
                if n == 1:
                    for u in range(U_QKV, U_QKV + 3):
                        load(sp, wcols(w_in, u - U_QKV), u)

        def tables_sp(sp):
            gains = [a["attn_norm_g"][0], a["ffn_norm_g"][0], a["b_kv_norm_g"], a["attn_norm_g"][1],
                     a["ffn_norm_g"][1]]
            for n, g in enumerate(gains):
                sp.dma_start(norm_rows[KC * n:KC * n + KC, :], g.rearrange("(k p) -> k p", p=P)).then_inc(tab_in, 16)
            sp.wait_ge(gain_rows_set, 1)
            for half in (0, HD):
                for c0, n, g in [(4 * e, 4, a["a_q_norm_g"][0, e]) for e in range(NG)] + \
                        [(12 + 4 * e, 4, a["a_k_norm_g"][0, e]) for e in range(NG)] + \
                        [(36, 1, a["b_k_norm_g"]), (38, 8, a["b_q_norm_g"][0])]:
                    sp.dma_start(head_rows[c0:c0 + n, half:half + HD],
                                 g.unsqueeze(0).to_broadcast([n, HD])).then_inc(tab_in, 16)
            sp.dma_start(sink_rows, a["b_sinks"][0].rearrange("(c h) -> c h", h=2)).then_inc(tab_in, 16)
            sp.dma_start(sink_col[:], a["b_sinks"][0].unsqueeze(1).to_broadcast([16, NS]).unsqueeze(2)) \
                .then_inc(const_in, 16)
            sp.dma_start(rope[:], a["consts"][:, C_COS:C_END].rearrange("p (a t) -> p a t", a=2)) \
                .then_inc(const_in, 16)
            m_raw = f_stage
            sp.dma_start(m_raw, a["consts"][:, C_MQ:C_COS]).then_inc(const_in, 16)
            for l in range(2):
                for t in range(3):
                    sp.dma_start(cw_stage[l][0:2 * FC, P * t:P * t + P],
                                 a["ffn_conv_w"][l, t].rearrange("(c f) -> c f", f=P)).then_inc(tab_in, 16)
                sp.dma_start(cw_stage[l][0:2 * FC, 3 * P:4 * P],
                             a["ffn_conv_b"][l].rearrange("(c f) -> c f", f=P)).then_inc(tab_in, 16)
                for t in range(2):
                    sp.dma_start(st_stage[l][2 * FC * t:2 * FC * (t + 1), :].rearrange("c (s f) -> c s f", f=P),
                                 a["state_ffn_conv"][l, :, t, :].rearrange("s (c f) -> c s f", f=P)) \
                        .then_inc(tab_in, 16)

        CONSTS_IN = 16 * 3
        TABLES_IN = 16 * (5 + 16 + 1 + 2 * 6)
        f_stage = arena[:, 6144:7168]
        head_rows, norm_rows = arena[0:46, 7168:7296], arena[0:5 * KC, 7296:7424]
        sink_rows = arena[0:B_CHUNKS, 7424:7426]

        def rows_in_pe(pe):
            pe.wait_ge(ident_in, 16)
            for n in range(NTILE + 1):
                pe.wait_ge(x_in[n % 2], 16 * (n // 2 + 1))
                if n >= 3:
                    pe.wait_ge(h_set, 2 * (n - 3) + 2)
                rows = P if n < NTILE else NS
                for c in range(KC):
                    mm = pe.transpose(acc[:, (2 * n + c // 4) % 6, P * (c % 4):P * (c % 4) + rows],
                                      x_stage[n % 2][0:rows, P * c:P * c + P], ident[0:rows, 0:rows])
                mm.then_inc(x_turned, 1)
            pe.wait_ge(tab_in, TABLES_IN)
            pe.transpose(aux[:, 1, 0:46], head_rows, ident[0:46, 0:46])
            pe.transpose(aux[:, 1, 64:64 + 5 * KC], norm_rows, ident[0:5 * KC, 0:5 * KC])
            pe.transpose(aux[0:2, 1, 128:128 + B_CHUNKS], sink_rows, ident[0:B_CHUNKS, 0:B_CHUNKS]) \
                .then_inc(gains_turned, 1)
            pe.wait_ge(gains_set, 3)
            for l in range(2):
                if l:
                    pe.wait_ge(tab_set, 2)
                for t in range(4):
                    mm = pe.transpose(aux[:, 0, 2 * FC * t:2 * FC * (t + 1)], cw_stage[l][0:2 * FC, P * t:P * t + P],
                                      ident[0:2 * FC, 0:2 * FC])
                mm.then_inc(tab_turned, 1)
                for half in range(2):
                    pe.wait_ge(tab_set, 3 * l + half) if l or half else None
                    for s in range(4):
                        q = 4 * half + s
                        mm = pe.transpose(aux[:, 1, 4 * FC * s:4 * FC * (s + 1)],
                                          st_stage[l][0:4 * FC, P * q:P * q + P], ident[0:4 * FC, 0:4 * FC])
                    mm.then_inc(tab_turned, 1)
                    pe.wait_ge(tab_set, 3 * l + half + 2)

        def rows_in_dve(v):
            v.memset(head_rows, 1.0).then_inc(gain_rows_set, 1)
            for n in range(NTILE + 1):
                v.wait_ge(x_turned, n + 1)
                rows = P if n < NTILE else NS
                for b in range(2):
                    v.tensor_copy(hT[:, 4 * b:4 * b + 4, P * n:P * n + rows],
                                  acc[:, (2 * n + b) % 6, :].rearrange("p (c n) -> p c n", n=P)[:, :, 0:rows]) \
                        .then_inc(h_set, 1)
            v.wait_ge(gains_turned, 1)
            v.tensor_copy(head_g[:], aux[:, 1, 0:46]).then_inc(gains_set, 1)
            v.tensor_copy(norm_g[:].rearrange("p n k -> p (n k)"), aux[:, 1, 64:64 + 5 * KC]).then_inc(gains_set, 1)
            v.tensor_copy(sink[:], aux[0:2, 1, 128:128 + B_CHUNKS]).then_inc(gains_set, 1)
            for l in range(2):
                v.wait_ge(tab_turned, 3 * l + 1)
                v.tensor_copy(cw[:, l, :, :], aux[:, 0, 0:8 * FC].rearrange("p (t c) -> p t c", t=4)).then_inc(tab_set, 1)
                for half in range(2):
                    v.wait_ge(tab_turned, 3 * l + half + 2)
                    v.tensor_copy(st_T[:, l, 4 * half:4 * half + 4, :],
                                  aux[:, 1, 0:16 * FC].rearrange("p (s c) -> p s c", s=4)) \
                        .then_inc(tab_set, 1)

        def consts_dve(v):
            v.memset(eps[:], EPS).then_inc(const_set, 1)
            v.memset(sel_den[:], 0.0).then_inc(const_set, 1)
            v.wait_ge(ident_in, 16)
            v.wait_ge(const_in, CONSTS_IN)
            v.tensor_copy(masks[:].rearrange("p a m n -> p (a m n)"), f_stage).then_inc(const_set, 1)
            v.tensor_copy(ident_b[:], ident).then_inc(const_set, 1)
            for h in range(2):
                v.tensor_scalar(sel[:, h, :], ones[0:2, :], cst[0:2, C_ID + h:C_ID + h + 1], None, ALU.mult) \
                    .then_inc(const_set, 1)
            v.wait_ge(gains_set, 3)
            v.tensor_scalar(sink8[:], sink[:], 1.0 / SCALE, None, ALU.mult).then_inc(const_set, 1)
            v.wait_ge(const_set, 7)
            for h in range(2):
                half = HD * (1 - h)
                v.tensor_copy(sel_den[:, h, half:half + HD], sel[:, h, half:half + HD].bitcast(F32)) \
                    .then_inc(const_set, 1)
            v.wait_ge(const_set, 9)
            v.tensor_scalar(sink_col[:], sink_col[:], 1.0 / SCALE, None, ALU.mult).then_inc(const_set, 1)

        CONSTS_SET = 10

        n_bufs = carve(5 * T, T, T, T, T)[1:]
        sq_n, xf_n = n_bufs[0:2], n_bufs[2:4]
        SQ0 = {0: 0, 1: 8, 2: 16, 4: 24}
        ST0 = {0: 0, 1: 2, 2: 4, 4: 6}

        def norm_act(act, n, before, stat=True):
            before(act)
            if stat:
                for k in range(KC):
                    if k >= 2:
                        act.wait_ge(n_mm, SQ0[n] + k - 1)
                    act.activation(sq_n[k % 2], hT[:, k, :], ACT.Square).then_inc(n_sq, 1)
                act.wait_ge(n_mm, SQ0[n] + KC)
                act.activation(thirds(rinv[:]), acc_set(0), ACT.Ln, bias=eps[:], scale=1.0 / D).then_inc(n_stat, 1)
                act.wait_ge(n_stat, ST0[n] + 1)
                act.activation(rinv[:], rinv[:], ACT.Exp, scale=-0.5).then_inc(n_stat, 1)
            for k in range(KC):
                act.wait_ge(n_x, 8 * n + k + 1)
                act.copy(xh[:, k, :], xf_n[k % 2]).then_inc(n_hi, 1)

        def norm_pe(pe, n):
            for k in range(KC):
                pe.wait_ge(n_sq, SQ0[n] + k + 1)
                for t in range(NT):
                    mm = pe.matmul(acc_set(0)[:, t, :], ones, sq_n[k % 2][:, TH * t:TH * t + TH],
                                   start=(k == 0), stop=(k == KC - 1))
                mm.then_inc(n_mm, 1)

        def norm_dve(v, n, before, stat=True):
            before(v)
            if stat:
                v.wait_ge(n_stat, ST0[n] + 2)
            def lo(k):
                v.wait_ge(n_hi, 8 * n + k + 1)
                v.tensor_tensor(xl[:, k, :], xf_n[k % 2], xh[:, k, :].bitcast(F32), ALU.subtract).then_inc(n_lo, 1)
            for k in range(KC):
                if k >= 2:
                    lo(k - 2)
                    v.wait_ge(n_lo, 8 * n + k - 1)
                v.scalar_tensor_tensor(xf_n[k % 2], hT[:, k, :], norm_g[:, n, k:k + 1], rinv[:],
                                       ALU.mult, ALU.mult).then_inc(n_x, 1)
            lo(KC - 2)
            lo(KC - 1)

        CH = 2
        CH_B = CH + A_CHUNKS
        Q_B = 24
        qg, sq_p, rr, ob0, ob1, t1b, t2b, lnb = carve(T, T, T, T, T, 2 * TH, 2 * TH, 2 * TH)
        outb = [ob0, ob1]

        def third(x, t):
            return x[:, TH * t:TH * t + TH]

        def counts_pe(pe):
            pe.sem_inc(w_used, RING)
            pe.sem_inc(third_full, 2 * CH)

        def counts_act(act):
            act.sem_inc(hi_ready, RING)
            act.sem_inc(acc_evac, 3 * CH)

        def proj_main(pe, c, k, u0, m, i, t, norm=None):
            slot, u, _ = unit_at(u0, m, i)
            if t == 0:
                pe.wait_ge(lo_ready, u + 1)
                pe.wait_ge(acc_evac, 3 * c - 3)
            w1 = w_hi[:, slot, :].rearrange("p (k n) -> p k n", n=P)
            w2 = w_lo[:, slot, :].rearrange("p (k n) -> p k n", n=P)
            for j in range(KC):
                if norm is not None and t == 0:
                    pe.wait_ge(n_lo, 8 * norm + j + 1)
                mm = product(pe, acc_set(k)[:, t, :], w1[:, j, :], w2[:, j, :], third(xh[:, j, :], t),
                             third(xl[:, j, :], t), j == 0, j == KC - 1)
            mm.then_inc(w_used if t == NT - 1 else third_full, 1)

        def proj_aux(pe, c, q, t):
            pe.wait_ge(acc_evac, 3 * c + t + 1)
            pe.wait_ge(ln_done, 3 * q + t)
            pe.matmul(aux[:, 0, 0:TH], blk, third(sq_p, t), start=True, stop=True).then_inc(ssq_ready, 1)
            pe.wait_ge(rot_used, 3 * q + t)
            pe.matmul(aux[:, 1, 0:TH], rot, third(qg, t), start=True, stop=True).then_inc(rot_ready, 1)

        def proj_evac(act, c, k, u0, m, i, t, gain):
            _, u, _ = unit_at(u0, m, i)
            if t < NT - 1:
                act.wait_ge(third_full, 2 * c + t + 1)
            else:
                act.wait_ge(w_used, u + 1)
            act.wait_ge(chunk_out, 3 * c + t - 2)
            if gain is not None:
                act.activation(third(sq_p, t), acc_set(k)[:, t, :], ACT.Square)
                act.activation(third(qg, t), acc_set(k)[:, t, :], ACT.Copy, scale=gain).then_inc(acc_evac, 1)
            else:
                act.copy(third(qg, t), acc_set(k)[:, t, :]).then_inc(acc_evac, 1)

        def proj_stat(act, q, t):
            s = third(lnb, t % 2)
            act.wait_ge(ssq_ready, 3 * q + t + 1)
            act.wait_ge(r_ready, 3 * q + t)
            act.activation(s, aux[:, 0, 0:TH], ACT.Ln, bias=eps[:], scale=1.0 / HD).then_inc(ln_done, 1)
            act.wait_ge(ln_done, 3 * q + t + 1)
            act.activation(third(rr, t), s, ACT.Exp, scale=-0.5).then_inc(r_ready, 1)

        def proj_dve(v, c, k, q, t):
            v.wait_ge(acc_evac, 3 * c + t + 1)
            if t == 0:
                v.wait_ge(stored[k], 8 * (c - k) - 16)
            if q is None:
                v.tensor_copy(third(outb[k], t), third(qg, t)).then_inc(chunk_out, 1)
                return
            s1, s2 = third(t1b, t % 2), third(t2b, t % 2)
            v.wait_ge(chunk_out, 3 * c + t)
            v.tensor_tensor(s1, third(qg, t), third(rope[:, 0, :], t), ALU.mult).then_inc(qk_step, 1)
            v.wait_ge(rot_ready, 3 * q + t + 1)
            v.tensor_tensor(s2, aux[:, 1, 0:TH], third(rope[:, 1, :], t), ALU.mult).then_inc(rot_used, 1)
            v.wait_ge(qk_step, 2 * (3 * q + t) + 1)
            v.wait_ge(rot_used, 3 * q + t + 1)
            v.tensor_tensor(s1, s1, s2, ALU.add).then_inc(qk_step, 1)
            v.wait_ge(qk_step, 2 * (3 * q + t) + 2)
            v.wait_ge(r_ready, 3 * q + t + 1)
            v.tensor_tensor(third(outb[k], t), s1, third(rr, t), ALU.mult).then_inc(chunk_out, 1)

        def proj_a(eng, main, aux_of, aux_first):
            def step(one, other):
                for f in (other, one) if aux_first else (one, other):
                    f()
            for t in range(NT):
                main(0, 0, 0, t)
            with eng.Fori(0, 3) as i:
                for e in range(BODY):
                    for t in range(NT):
                        step(lambda: main(e + 1, BODY, i, t), lambda: aux_of(e, BODY, i, t))
            for n in range(3 * BODY + 1, A_CHUNKS):
                for t in range(NT):
                    step(lambda: main(n, 0, 0, t), lambda: aux_of(n - 1, 0, 0, t) if n <= 24 else None)

        def proj_a_pe(pe):
            proj_a(pe,
                   lambda n, m, i, t: proj_main(pe, CH + n + m * i, n % 2, U_QKV + n, m, i, t,
                                                norm=0 if n == 0 else None),
                   lambda n, m, i, t: proj_aux(pe, CH + n + m * i, n + m * i, t), False)

        def proj_a_act(act):
            def main(n, m, i, t):
                if t == 0:
                    split_ahead(act, U_QKV + n, m, i)
                gain = None if m == 0 and n >= 24 else head_g[:, bass.ds(n + m * i, 1)] if m else head_g[:, n:n + 1]
                proj_evac(act, CH + n + m * i, n % 2, U_QKV + n, m, i, t, gain)
            proj_a(act, main, lambda n, m, i, t: proj_stat(act, n + m * i, t), True)

        def proj_a_dve(v):
            with v.Fori(0, 24 // BODY) as i:
                for e in range(BODY):
                    for t in range(NT):
                        proj_dve(v, CH + e + BODY * i, e % 2, e + BODY * i, t)
            with v.Fori(0, 12 // BODY) as i:
                for e in range(BODY):
                    for t in range(NT):
                        proj_dve(v, CH + 24 + e + BODY * i, e % 2, None, t)

        def store_chunk(sp, c, k, to):
            sp.wait_ge(chunk_out, 3 * c + 3)
            sp.dma_start(to, outb[k]).then_inc(stored[k], 16)

        def proj_a_sp(sp):
            with sp.Fori(0, A_CHUNKS // BODY - 1) as i:
                for e in range(BODY):
                    load(sp, wcols(w_in, e + 3 + BODY * i), U_QKV + 3 + e, BODY, i)
                    store_chunk(sp, CH + e + BODY * i, e % 2, scratch[e + BODY * i])
            for n in range(A_CHUNKS - BODY, A_CHUNKS):
                if n + 3 < A_CHUNKS:
                    load(sp, wcols(w_in, n + 3), U_QKV + n + 3)
                else:
                    load(sp, wcols(w_aout, n + 3 - A_CHUNKS, 2 * P), U_QKV + n + 3)
                store_chunk(sp, CH + n, n % 2, scratch[n])

        def proj_b_pe(pe):
            norm_pe(pe, 2)
            for t in range(NT):
                proj_main(pe, CH_B, 0, U_KV, 0, 0, t, norm=2)
            for t in range(NT):
                proj_main(pe, CH_B + 1, 1, U_KV + 1, 0, 0, t)
                proj_aux(pe, CH_B, Q_B, t)
            for n in range(B_CHUNKS):
                for t in range(NT):
                    proj_main(pe, CH_B + 2 + n, n % 2, U_BQ + n, 0, 0, t, norm=3 if n == 0 else None)
                    if n:
                        proj_aux(pe, CH_B + 1 + n, Q_B + n, t)
            for t in range(NT):
                proj_aux(pe, CH_B + 1 + B_CHUNKS, Q_B + B_CHUNKS, t)

        def proj_b_act(act):
            split_ahead(act, U_KV)
            for t in range(NT):
                proj_evac(act, CH_B, 0, U_KV, 0, 0, t, head_g[:, 36:37])
            split_ahead(act, U_KV + 1)
            for t in range(NT):
                proj_stat(act, Q_B, t)
                proj_evac(act, CH_B + 1, 1, U_KV + 1, 0, 0, t, None)
            norm_act(act, 3, lambda e: e.wait_ge(w_used, U_BQ), stat=False)
            for n in range(B_CHUNKS):
                split_ahead(act, U_BQ + n)
                for t in range(NT):
                    if n:
                        proj_stat(act, Q_B + n, t)
                    proj_evac(act, CH_B + 2 + n, n % 2, U_BQ + n, 0, 0, t, head_g[:, 38 + n:39 + n])
            for t in range(NT):
                proj_stat(act, Q_B + B_CHUNKS, t)

        def proj_b_dve(v):
            for t in range(NT):
                proj_dve(v, CH_B, 0, Q_B, t)
            for t in range(NT):
                proj_dve(v, CH_B + 1, 1, None, t)
            norm_dve(v, 3, lambda e: e.wait_ge(w_used, U_BQ), stat=False)
            for n in range(B_CHUNKS):
                for t in range(NT):
                    proj_dve(v, CH_B + 2 + n, n % 2, Q_B + 1 + n, t)

        def proj_b_sp(sp):
            for n in range(2 + B_CHUNKS):
                if n + 3 < 2 + B_CHUNKS:
                    load(sp, wcols(w_q, n + 1), U_KV + n + 3)
                else:
                    load(sp, wcols(w_bout, n + 3 - 2 - B_CHUNKS), U_KV + n + 3)
                store_chunk(sp, CH_B + n, n % 2, scratch[A_CHUNKS + n])

        ADDED = {"a": 0, 0: KC, "b": KC + KC * FFN_TURNS, 1: 2 * KC + KC * FFN_TURNS}

        def out_main(pe, n, k, u0, half, kcs, last_of_unit):
            slot, u, _ = unit_at(u0)
            pe.wait_ge(lo_ready, u + 1)
            w1 = w_hi[:, slot, :].rearrange("p (k n) -> p k n", k=kcs)
            w2 = w_lo[:, slot, :].rearrange("p (k n) -> p k n", k=kcs)
            for t in range(NT):
                for j in range(kcs):
                    mm = product(pe, acc_set(k)[:, t, :], w1[:, j, P * half:P * half + P],
                                 w2[:, j, P * half:P * half + P], third(xh[:, j, :], t), third(xl[:, j, :], t),
                                 j == 0, j == kcs - 1)
            mm.then_inc(w_used if last_of_unit else res_full, 1)

        def add_to_h(v, n, k):
            v.tensor_tensor(thirds(hT[:, n, :]), thirds(hT[:, n, :]), acc_set(k), ALU.add).then_inc(h_added, 1)

        def aout_pe(pe):
            pe.wait_ge(ZA.fin, 1)
            for n in range(KC):
                if n >= 2:
                    pe.wait_ge(h_added, n - 1)
                out_main(pe, n, n % 2, U_AOUT + n // 2, n % 2, 4, n % 2 == 1)

        def aout_act(act):
            for n in range(4):
                split_ahead(act, U_AOUT + n)

        def aout_dve(v):
            for n in range(KC):
                if n % 2 == 0:
                    v.wait_ge(res_full, n // 2 + 1)
                else:
                    v.wait_ge(w_used, U_AOUT + n // 2 + 1)
                add_to_h(v, n, n % 2)

        def bout_pe(pe):
            pe.wait_ge(ZB.fin, 1)
            for n in range(KC):
                if n >= 2:
                    pe.wait_ge(h_added, ADDED["b"] + n - 1)
                out_main(pe, n, n % 2, U_BOUT + n, 0, KC, True)

        def bout_act(act):
            for n in range(KC):
                split_ahead(act, U_BOUT + n)

        def bout_dve(v):
            for n in range(KC):
                v.wait_ge(w_used, U_BOUT + n + 1)
                add_to_h(v, n, n % 2)

        U1 = T + 2
        ug, uv, cg, cv, ebuf, fbuf, tail_sb = carve(U1, U1, T, T, T, T, 640)
        GATE, VAL = 0, 1
        u_ext, c_out = [ug, uv], [cg, cv]
        UPS = 4 * FFN_TURNS
        CONV_STEPS, GATE_STEPS = 4, 3
        TURN_STEPS = 4 * CONV_STEPS + 2 * GATE_STEPS
        LAST = FFN_TURNS - 1

        class Turn:
            def __init__(self, l, i, last):
                self.l, self.i, self.last = l, i, last
                self.m = 0 if last else 6
                self.off = 6 * i if last else 0
                self.ii = 0 if last else i
                self.unit0 = [U_FFN0, U_FFN1][l]
                self.up = UPS * l + 4 * i
                self.added = ADDED[l] + KC * i
                self.res = 4 + 7 * FFN_TURNS * l + 7 * i
                self.f = 2 * FFN_TURNS * l + 2 * i
                self.steps = TURN_STEPS * FFN_TURNS * l + CONV_STEPS + TURN_STEPS * i
                self.d0 = 4 if last else 5

            def unit(self, o):
                return self.unit0 + self.off + o, self.m, self.ii

            def no(self, o):
                return unit_at(*self.unit(o))[1]

        def turns(eng, l, body, *extra):
            with eng.Fori(0, LAST) as i:
                body(eng, Turn(l, i, False))
            body(eng, Turn(l, LAST, True))

        def up_pe(pe, unit, k, norm=None):
            slot, u, _ = unit_at(*unit)
            pe.wait_ge(lo_ready, u + 1)
            w1 = w_hi[:, slot, :].rearrange("p (k n) -> p k n", n=P)
            w2 = w_lo[:, slot, :].rearrange("p (k n) -> p k n", n=P)
            for t in range(NT):
                for j in range(KC):
                    if norm is not None and t == 0:
                        pe.wait_ge(n_lo, 8 * norm + j + 1)
                    mm = product(pe, acc_set(k)[:, t, :], w1[:, j, :], w2[:, j, :], third(xh[:, j, :], t),
                                 third(xl[:, j, :], t), j == 0, j == KC - 1)
            mm.then_inc(w_used, 1)

        def ffn_turn_pe(pe, z):
            pe.wait_ge(h_added, z.added - 1)
            up_pe(pe, z.unit(1), 1)
            pe.wait_ge(h_added, z.added)
            pe.wait_ge(up_evac, z.up + 1)
            up_pe(pe, z.unit(2), 0)
            pe.wait_ge(up_evac, z.up + 2)
            up_pe(pe, z.unit(3), 1)
            if not z.last:
                pe.wait_ge(up_evac, z.up + 3)
                up_pe(pe, z.unit(4), 0)
            k0 = 0 if z.last else 1
            slots = [unit_at(*z.unit(z.d0 + e))[0] for e in range(2)]
            pe.wait_ge(lo_ready, z.no(z.d0 + 1) + 1)
            pe.wait_ge(flo_ready, z.f + 2)
            for n in range(KC):
                if n == 0:
                    pe.wait_ge(up_evac, z.up + (3 if z.last else 4))
                elif n == 1:
                    pe.wait_ge(up_evac, z.up + (4 if z.last else 5))
                else:
                    pe.wait_ge(h_added, z.added + n - 1)
                for t in range(NT):
                    for e, s in enumerate(slots):
                        mm = product(pe, acc_set(k0 + n)[:, t, :], w_hi[:, s, P * n:P * n + P],
                                     w_lo[:, s, P * n:P * n + P], third(f_hi[:, e, :], t),
                                     third(f_lo[:, e, :], t), e == 0, e == 1)
                        if n == KC - 1 and t == NT - 1:
                            mm.then_inc(w_used, 1)
                if n < KC - 1:
                    mm.then_inc(res_full, 1)

        def ffn_pe(pe, l):
            norm_pe(pe, 1 + 3 * l)
            up_pe(pe, ([U_FFN0, U_FFN1][l], 0, 0), 0, norm=1 + 3 * l)
            turns(pe, l, ffn_turn_pe)
            pe.wait_ge(conv_out, UPS * (l + 1))
            pe.wait_ge(tail_set, 2 * l)
            for s in range(5):
                mm = pe.transpose(aux[0:4 * FC, s // 4, P * (s % 4):P * (s % 4) + P],
                                  u_tail[:, 2 * s:2 * s + 2, :].rearrange("p a c -> p (a c)"), ident)
            mm.then_inc(tail_turned, 1)

        def up_evac_act(act, z, o, which, k):
            split_ahead(act, *z.unit(o))
            act.wait_ge(w_used, z.no(o) + 1)
            act.wait_ge(conv_out, z.up + o - 1)
            act.copy(thirds(u_ext[which][:, 2:U1]), acc_set(k)).then_inc(up_evac, 1)

        def gate_act(act, z, e):
            act.wait_ge(conv_out, z.up + 2 * e + 1)
            act.wait_ge(f_raw, z.f + e)
            act.activation(ebuf, cg, ACT.Exp, scale=-1.0).then_inc(e_ready, 1)
            act.wait_ge(f_raw, z.f + e + 1)
            act.wait_ge(w_used, z.no(1))
            act.copy(f_hi[:, e, :], fbuf).then_inc(fhi_ready, 1)

        def ffn_turn_act(act, z):
            up_evac_act(act, z, 1, VAL, 1)
            gate_act(act, z, 0)
            up_evac_act(act, z, 2, GATE, 0)
            up_evac_act(act, z, 3, VAL, 1)
            gate_act(act, z, 1)
            if not z.last:
                up_evac_act(act, z, 4, GATE, 0)
            split_ahead(act, *z.unit(z.d0))
            split_ahead(act, *z.unit(z.d0 + 1))

        def ffn_act(act, l):
            norm_act(act, 1 + 3 * l, lambda e: e.wait_ge(h_added, ADDED[l]))
            u0 = [U_FFN0, U_FFN1][l]
            split_ahead(act, u0)
            act.wait_ge(w_used, u0 + 1)
            act.copy(thirds(u_ext[GATE][:, 2:U1]), acc_set(0)).then_inc(up_evac, 1)
            turns(act, l, ffn_turn_act)

        def conv_dve(v, l, n, which, ch, s, products):
            u, c = u_ext[which], c_out[which]
            w = [cw[:, l, t, bass.ds(ch, 1)] for t in range(4)]
            state = [st_T[:, l, :, bass.ds(ch + 2 * FC * t, 1)] for t in range(2)]
            cs = c[:, SEQ:T].unsqueeze(2)
            v.wait_ge(up_evac, n + 1)
            v.wait_ge(f_raw, products)
            v.tensor_scalar(c[:, 0:T], u[:, 2:U1], w[2], w[3], ALU.mult, ALU.add).then_inc(conv_step, 1)
            v.tensor_copy(u_tail[:, :, bass.ds(ch, 1)], u[:, SEQ:U1].unsqueeze(2))
            v.wait_ge(conv_step, s + 1)
            v.scalar_tensor_tensor(c[:, 0:SEQ], u[:, 1:SEQ + 1], w[1], c[:, 0:SEQ], ALU.mult, ALU.add) \
                .then_inc(conv_step, 1)
            v.scalar_tensor_tensor(cs, state[1], w[1], cs, ALU.mult, ALU.add).then_inc(conv_step, 1)
            v.wait_ge(conv_step, s + 2)
            v.scalar_tensor_tensor(c[:, 0:SEQ], u[:, 0:SEQ], w[0], c[:, 0:SEQ], ALU.mult, ALU.add) \
                .then_inc(conv_step, 1)
            v.wait_ge(conv_step, s + 3)
            v.scalar_tensor_tensor(cs, state[0], w[0], cs, ALU.mult, ALU.add).then_inc(conv_out, 1)

        def gated_dve(v, z, e, s):
            v.wait_ge(conv_out, z.up + 2 * e + 2)
            v.wait_ge(conv_step, s)
            v.tensor_tensor(cv, cg, cv, ALU.mult).then_inc(conv_step, 1)
            v.wait_ge(e_ready, z.f + e + 1)
            v.tensor_scalar(ebuf, ebuf, 1.0, None, ALU.add).then_inc(conv_step, 1)
            v.wait_ge(conv_step, s + 2)
            v.reciprocal(ebuf, ebuf).then_inc(conv_step, 1)
            v.wait_ge(conv_step, s + 3)
            v.wait_ge(flo_ready, z.f + e)
            v.tensor_tensor(fbuf, cv, ebuf, ALU.mult).then_inc(f_raw, 1)
            v.wait_ge(fhi_ready, z.f + e + 1)
            v.tensor_tensor(f_lo[:, e, :], fbuf, f_hi[:, e, :].bitcast(F32), ALU.subtract).then_inc(flo_ready, 1)

        def ffn_turn_dve(v, z):
            s, l, g = z.steps, z.l, 2 * z.i
            conv_dve(v, l, z.up + 1, VAL, FC + g, s, z.f)
            gated_dve(v, z, 0, s + CONV_STEPS)
            s += CONV_STEPS + GATE_STEPS
            conv_dve(v, l, z.up + 2, GATE, g + 1, s, z.f + 1)
            conv_dve(v, l, z.up + 3, VAL, FC + g + 1, s + CONV_STEPS, z.f + 1)
            gated_dve(v, z, 1, s + 2 * CONV_STEPS)
            s += 2 * CONV_STEPS + GATE_STEPS
            if not z.last:
                conv_dve(v, l, z.up + 4, GATE, g + 2, s, z.f + 2)
            k0 = 0 if z.last else 1
            for n in range(KC):
                if n < KC - 1:
                    v.wait_ge(res_full, z.res + n + 1)
                else:
                    v.wait_ge(w_used, z.no(z.d0 + 1) + 1)
                add_to_h(v, n, k0 + n)

        def ffn_dve(v, l):
            norm_dve(v, 1 + 3 * l, lambda e: e.wait_ge(h_added, ADDED[l]))
            for n in range(2):
                v.memset(u_ext[n][:, 0:2], 0.0).then_inc(chain, 1)
            v.wait_ge(chain, 2 * (l + 1))
            conv_dve(v, l, UPS * l, GATE, 0, TURN_STEPS * FFN_TURNS * l, 2 * FFN_TURNS * l)
            turns(v, l, ffn_turn_dve)
            v.wait_ge(tail_turned, l + 1)
            v.wait_ge(tail_out, 16 * TAILS * l)
            v.tensor_copy(tail_sb[0:4 * FC, 0:512], aux[0:4 * FC, 0, :]).then_inc(tail_set, 1)
            v.tensor_copy(tail_sb[0:4 * FC, 512:640], aux[0:4 * FC, 1, 0:P]).then_inc(tail_set, 1)

        TAILS = 1 + NS
        up_w = [a["ffn_w_up"][l] for l in range(2)]

        def down_unit(l, c):
            return a["ffn_w_down"][l].rearrange("(c p) (k n) -> c p k n", p=P, k=1)[c]

        CACHE_PIECES = 23
        w2048 = [a["cache_a_kv_w2048"], outs["a_w2048_sample"]]
        c_from = w2048[0][0].rearrange("s x w h d -> (s x) (w h d)")
        c_to = w2048[1][0].rearrange("s x w h d -> (s x) (w h d)")
        ROW = 8 * HD
        PIECE = (GROUPS[2][0] - 1) * ROW // CACHE_PIECES

        def copy_piece(sp, n):
            src = c_from[:, ROW:].rearrange("r (n e) -> r n e", e=PIECE)
            dst = c_to[:, 0:PIECE * CACHE_PIECES].rearrange("r (n e) -> r n e", e=PIECE)
            sp.dma_start(dst[:, n, :], src[:, n, :]).then_inc(copied, 16)

        def ffn_turn_sp(sp, z):
            l, g = z.l, 2 * z.i
            load(sp, wcols(up_w[l], g + FC), *z.unit(1))
            load(sp, wcols(up_w[l], g + 1), *z.unit(2))
            load(sp, wcols(up_w[l], g + 1 + FC), *z.unit(3))
            copy_piece(sp, FFN_TURNS * l + z.i)
            if not z.last:
                load(sp, wcols(up_w[l], g + 2), *z.unit(4))
            for e in range(2):
                load(sp, down_unit(l, g + e), *z.unit(z.d0 + e))

        def ffn_sp(sp, l):
            load(sp, wcols(up_w[l], 0), [U_FFN0, U_FFN1][l])
            turns(sp, l, ffn_turn_sp)

        def tails_sp(sp, l):
            sp.wait_ge(tail_set, 2 * l + 2)
            sp.dma_start(outs["ffn_conv_prompt"][l, 0].rearrange("t (c f) -> (t c) f", f=P),
                         tail_sb[0:4 * FC, 0:P]).then_inc(tail_out, 16)
            for s in range(NS):
                r = 2 * FC * (s % 2)
                sp.dma_start(outs["ffn_conv_sample"][l, s, 1].rearrange("(c f) -> c f", f=P),
                             tail_sb[r:r + 2 * FC, P * (1 + s // 2):P * (2 + s // 2)]).then_inc(tail_out, 16)

        ones_col = ones[:, 0:1]

        def buffers(M):
            if M.ng > 1:
                v2, vt, pt, mrow, bm, stg = carve(SEQ, 24 * 192, 3 * 512, SEQ, 2 * M.cols, 4 * 512)
                q = [xh[:, 4 + g, 0:SEQ] for g in range(3)]
                k = [xl[:, 4 + g, 0:SEQ] for g in range(3)]
                v = [xh[:, 7, 0:SEQ], xl[:, 7, 0:SEQ], None]
                q, k = [x.bitcast(F32) for x in q], [x.bitcast(F32) for x in k]
                v = [v[0].bitcast(F32), v[1].bitcast(F32), v2]
                erow = None
            else:
                q0, k0, v0, vt, pt, mrow, bm, erow = carve(SEQ, SEQ, SEQ, 8 * 192, 3 * 512, SEQ, 2 * M.cols, SEQ)
                q, k, v, stg = [q0], [k0], [v0], None
            vt = vt.rearrange("p (t c) -> p t c", c=192)
            bm = bm.rearrange("p (h c) -> p h c", h=2)
            return q, k, v, vt, pt, mrow, bm, stg, mrow, erow

        BUF = {id(M): buffers(M) for M in (MA, MB)}
        LOADS = {id(MA): 9, id(MB): 5}
        EXPORTS = [(0, 7, 1), (1, 4, 4), (2, 0, 4), (2, 4, 4)]

        def moves(M):
            vt = [("t", g, t, 4) for g in range(M.ng) for t in (0, 4)]
            if M.ng == 1:
                return vt
            return [("k", *e) for e in EXPORTS] + vt + [("v", *e) for e in EXPORTS]

        def attn_pe(pe, M, S, it):
            q, k, v, vt, pt, mrow, bm, stg, of, erow = BUF[id(M)]
            nb, mv = len(M.batches), moves(M)
            NM = len(mv)
            pe.wait_ge(S.loaded, 16 * LOADS[id(M)] * (it + 1))
            for n, (what, g, t0, cnt) in enumerate(mv):
                if n < 6:
                    pe.wait_ge(S.sc_exp, 2 * nb * it)
                else:
                    pe.wait_ge(S.copied, NM * it + n - 5)
                src = k[g] if what == "k" else v[g]
                for e in range(cnt):
                    x = tile_tokens(src, g, t0 + e) if what == "t" else src[:, P * (t0 + e):P * (t0 + e) + P]
                    mm = pe.transpose(acc[:, n % 6, P * e:P * e + P], x, ident)
                mm.then_inc(S.moved, 1)
            for hh in range(2):
                rows = slice(HD * hh, HD * hh + HD)
                for b, (g, kind, blocks) in enumerate(M.batches):
                    n = nb * hh + b
                    if n < 6:
                        pe.wait_ge(S.copied, NM * (it + 1))
                    else:
                        pe.wait_ge(S.maxed, 2 * nb * it + n - 5)
                    w = len(blocks) * P
                    pe.matmul(acc[:, n % 6, 0:w], ident_b[:],
                              masks[:, 0, kind, :].unsqueeze(1).to_broadcast([P, len(blocks), P]),
                              start=True, stop=False)
                    for e, (tq, tk, _) in enumerate(blocks):
                        mm = pe.matmul(acc[:, n % 6, P * e:P * e + P], tile_tokens(q[g][rows, :], g, tq),
                                       tile_tokens(k[g][rows, :], g, tk), start=False, stop=e == len(blocks) - 1)
                    mm.then_inc(S.scored, 1)
            pe.wait_ge(S.merged, it + 1)
            for g in range(M.ng):
                for t in range(NTILE):
                    mm = pe.transpose(acc[0:2, 2 * g + t // 4, P * (t % 4):P * (t % 4) + P],
                                      bm[:, :, 8 * g + t], ident)
                mm.then_inc(S.turned, 1)

            def scores(n):
                hh, b = divmod(n, nb)
                g, kind, blocks = M.batches[b]
                rows = slice(HD * hh, HD * hh + HD)
                if n < 6:
                    pe.wait_ge(S.shift, it + 1)
                else:
                    pe.wait_ge(S.sc_exp, 2 * nb * it + n - 5)
                w = len(blocks) * P
                pe.matmul(acc[:, n % 6, 0:w], ident_b[:],
                          masks[:, 1, kind, :].unsqueeze(1).to_broadcast([P, len(blocks), P]),
                          start=True, stop=False)
                pe.matmul(acc[:, n % 6, 0:w], sel[:, hh, :], batch_tokens(neg_max[:, :], g, kind, blocks),
                          start=False, stop=False)
                for e, (tq, tk, _) in enumerate(blocks):
                    mm = pe.matmul(acc[:, n % 6, P * e:P * e + P], tile_tokens(k[g][rows, :], g, tk),
                                   tile_tokens(q[g][rows, :], g, tq), start=False, stop=e == len(blocks) - 1)
                mm.then_inc(S.sc_full, 1)

            def values(n):
                hh, b = divmod(n, nb)
                g, kind, blocks = M.batches[b]
                pe.wait_ge(S.sc_exp, 2 * nb * it + n + 1)
                if b == 0:
                    pe.wait_ge(S.o_norm, 2 * it + hh)
                o = aux[:, :, :].rearrange("p a n -> p (a n)")
                vc = slice(HD * hh, HD * hh + P)
                probs = pt[:, 512 * (n % 3):512 * (n % 3) + 512]
                if erow is not None and b == nb - 1:
                    for half in range(2):
                        pe.matmul(aux[:, half, :], sel_den[:, hh, :], erow[0:2, 512 * half:512 * half + 512],
                                  start=False, stop=False, skip_group_check=True)
                for e, (tq, tk, _) in enumerate(blocks):
                    pe_ = probs[:, P * e:P * e + P]
                    kw = dict(start=b < 2 and e == 0, stop=b == nb - 1, skip_group_check=True)
                    if g < 2:
                        mm = pe.matmul(tile_tokens(o, g, tq), vt[:, 8 * g + tk, vc], pe_, **kw)
                    else:
                        for half in range(0, P, HD):
                            mm = pe.matmul(tile_tokens(o, g, tq)[:, half:half + HD], vt[:, 8 * g + tk, vc],
                                           pe_[:, half:half + HD], **kw)
                mm.then_inc(S.pv, 1)

            scores(0)
            for n in range(1, 2 * nb):
                scores(n)
                values(n - 1)
            values(2 * nb - 1)

        def attn_act(act, M, S, it):
            q, k, v, vt, pt, mrow, bm, stg, of, erow = BUF[id(M)]
            nb = len(M.batches)
            if erow is not None:
                act.wait_ge(S.shift, it + 1)
                act.wait_ge(S.pv, 2 * nb * it)
                act.activation(erow[0:2, :], neg_max[:, :].bitcast(F32), ACT.Exp, bias=sink_now[:],
                               scale=SCALE)
            for n in range(2 * nb):
                w = len(M.batches[n % nb][2]) * P
                act.wait_ge(S.sc_full, 2 * nb * it + n + 1)
                act.wait_ge(S.pv, 2 * nb * it + max(0, n - 2))
                act.activation(pt[:, 512 * (n % 3):512 * (n % 3) + w], acc[:, n % 6, 0:w], ACT.Exp, scale=SCALE) \
                    .then_inc(S.sc_exp, 1)
            act.wait_ge(S.o_norm, 2 * it + 2)
            act.copy(xh[:, it, 0:SEQ], of).then_inc(S.o_hi, 1)

        def attn_dve(v_, M, S, it):
            q, k, v, vt, pt, mrow, bm, stg, of, erow = BUF[id(M)]
            nb, mv = len(M.batches), moves(M)
            NM = len(mv)
            for n, (what, g, t0, cnt) in enumerate(mv):
                v_.wait_ge(S.moved, NM * it + n + 1)
                if what == "t":
                    v_.wait_ge(S.pv, 2 * nb * it)
                    v_.tensor_copy(vt[:, 8 * g + t0:8 * g + t0 + 4, :]
                                   .rearrange("p t (a b) -> p t a b", b=HD)[:, :, 0:3:2, :],
                                   acc[:, n % 6, :].rearrange("p (t a b) -> p t a b", t=4, a=2)).then_inc(S.copied, 1)
                else:
                    v_.wait_ge(S.exported, 64 * (2 * it + (what == "v")))
                    s = [e[0:2] for e in EXPORTS].index((g, t0))
                    v_.tensor_copy(stg[:, 512 * s:512 * s + P * cnt], acc[:, n % 6, 0:P * cnt]).then_inc(S.copied, 1)
            for hh in range(2):
                for b, (g, kind, blocks) in enumerate(M.batches):
                    n = nb * hh + b
                    c0 = blocks[0][2]
                    v_.wait_ge(S.scored, 2 * nb * it + n + 1)
                    if n == 0:
                        v_.wait_ge(S.turned, M.ng * it)
                    v_.tensor_reduce(bm[:, hh, c0:c0 + len(blocks)],
                                     acc[:, n % 6, 0:P * len(blocks)].rearrange("p (e n) -> p e n", n=P),
                                     AX_X, ALU.max).then_inc(S.maxed, 1)
            v_.wait_ge(S.maxed, 2 * nb * (it + 1))
            c1 = 8 * M.ng
            if M.ng > 1:
                v_.tensor_tensor(bm[:, :, 9:16:2], bm[:, :, 9:16:2], bm[:, :, c1 + 7:c1 + 11], ALU.max)
            v_.tensor_tensor(bm[:, :, 1:8], bm[:, :, 1:8], bm[:, :, c1:c1 + 7], ALU.max).then_inc(S.merged, 1)
            m = mrow[0:2, :]
            NR = M.ng + (erow is not None)
            for g in range(M.ng):
                v_.wait_ge(S.turned, M.ng * it + g + 1)
                src = acc[0:2, 2 * g:2 * g + 2, :].rearrange("p a n -> p (a n)")
                if g == 0:
                    v_.tensor_copy(m, src).then_inc(S.rowed, 1)
                else:
                    v_.wait_ge(S.rowed, NR * it + g)
                    st = 4 * g
                    mv_ = m.rearrange("p (n s) -> p s n", s=st)
                    v_.tensor_tensor(mv_, mv_, src.rearrange("p (s n) -> p s n", s=st), ALU.max).then_inc(S.rowed, 1)
            if erow is not None:
                v_.wait_ge(S.rowed, NR * it + 1)
                v_.wait_ge(S.pv, 2 * nb * it)
                v_.tensor_copy(sink_now[:], sink[:, bass.ds(it, 1)])
                v_.tensor_scalar(m, m, sink8[:, bass.ds(it, 1)], None, ALU.max).then_inc(S.rowed, 1)
            v_.wait_ge(S.rowed, NR * (it + 1))
            v_.wait_ge(S.pv, 2 * nb * it)
            v_.tensor_scalar(neg_max[:, :], m, -1.0, None, ALU.mult).then_inc(S.shift, 1)
            o = aux[:, :, :].rearrange("p a n -> p (a n)")
            for hh in range(2):
                rows, den = slice(HD * hh, HD * hh + HD), slice(HD * (1 - hh), HD * (1 - hh) + HD)
                v_.wait_ge(S.pv, 2 * nb * it + nb * (hh + 1))
                v_.reciprocal(rinv[rows, 0:SEQ], o[den, :]).then_inc(S.o_rec, 1)
                v_.wait_ge(S.o_rec, 2 * it + hh + 1)
                v_.tensor_tensor(of[rows, :], o[rows, :], rinv[rows, 0:SEQ], ALU.mult).then_inc(S.o_norm, 1)
            v_.wait_ge(S.o_hi, it + 1)
            v_.tensor_tensor(xl[:, it, 0:SEQ], of, xh[:, it, 0:SEQ].bitcast(F32), ALU.subtract).then_inc(S.o_lo, 1)
            v_.wait_ge(S.o_lo, it + 1)

        def attn_sp(sp, M, S, it, i, kv):
            q, k, v, vt, pt, mrow, bm, stg, of, erow = BUF[id(M)]
            nb, NM = len(M.batches), len(moves(M))
            sp.wait_ge(S.pv, 2 * nb * it)
            if M.ng > 1:
                for g in range(M.ng):
                    for w, x in enumerate((q, k, v)):
                        sp.dma_start(x[g], scratch[12 * w + 4 * g:12 * w + 4 * g + 4].rearrange("c p t -> p c t")
                                     [:, i, 0:SEQ]).then_inc(S.loaded, 16)
                outs_g = [outs["a_w128_prompt"], outs["a_w512_prompt"], outs["a_w2048_prompt"]]
                for w in range(2):
                    for s, (g, t0, cnt) in enumerate(EXPORTS):
                        sp.wait_ge(S.copied, NM * it + 10 * w + s + 1)
                        kept = min(GROUPS[g][0], SEQ)
                        first = t0 - (SEQ - kept) // P
                        dst = outs_g[g][0, 0, w].rearrange("(t p) (j h) d -> p t j (h d)", p=P, j=A_PAIRS)
                        sp.dma_start(dst[:, first:first + cnt, i, :],
                                     stg[:, 512 * s:512 * s + P * cnt].rearrange("p (t c) -> p t c", c=P)) \
                            .then_inc(S.exported, 16)
            else:
                qs = scratch[A_CHUNKS + 2 + 4 * kv:A_CHUNKS + 6 + 4 * kv].rearrange("c p t -> p c t")
                sp.dma_start(q[0], qs[:, i, 0:SEQ]).then_inc(S.loaded, 16)
                for w, x in enumerate((k[0], v[0])):
                    for half in (0, HD):
                        sp.dma_start(x[half:half + HD, :], scratch[A_CHUNKS + w, HD * kv:HD * kv + HD, 0:SEQ]) \
                            .then_inc(S.loaded, 16)

        CROW = A_PAIRS * P
        s_ring, s_kt, s_kvn, s_stc, s_all, s_pT, s_cols, s_qb, s_prod, s_dg, s_D, s_red, s_of = carve(
            4 * 1024, 2 * 512, 24 * P, 192, 387, 192, 36 * NS, 192, 96, 192, 192, 8, 32)
        s_ring = s_ring.rearrange("p (r a n) -> p r a n", r=4, a=2)
        s_cols = s_cols.rearrange("p (c s) -> p c s", s=NS)
        s_qb = s_qb.rearrange("p (c s h) -> p c s h", s=NS, h=2)
        caches = [a["cache_a_kv_w128"], a["cache_a_kv_w512"], a["cache_a_kv_w2048"]]
        out_caches = [outs["a_w128_sample"], outs["a_w512_sample"], outs["a_w2048_sample"]]
        STEPS_A = NG * NS // 2

        def sample_a_sp(sp):
            nb = len(MA.batches)
            sp.wait_ge(SA.pv, 2 * nb * A_PAIRS)
            sp.wait_ge(SA.exported, 16 * 8 * A_PAIRS)
            sp.wait_ge(SA.o_lo, A_PAIRS)
            sp.dma_start(s_cols, scratch[0:A_CHUNKS, :, SEQ:T].rearrange("c p t -> p c t")).then_inc(ZA.cols, 16)
            for n in range(2 * STEPS_A):
                w, (g, s2) = n // STEPS_A, divmod(n % STEPS_A, NS // 2)
                if 4 <= n < STEPS_A + 4:
                    sp.wait_ge(ZA.moved, 2 * (n - 4) + 2 + 6)
                elif n >= STEPS_A + 4:
                    sp.wait_ge(ZA.pe, n - STEPS_A - 3)
                src = caches[g][0, 2 * s2:2 * s2 + 2, w].rearrange("s (n d) h e -> n d s (h e)", d=GROUPS[g][1])
                sp.dma_start(s_ring[:, n % 4, :, :], src[:, 0]).then_inc(ZA.cache[n % 4], 16)
                if n == 4:
                    sp.wait_ge(ZA.kt, 6)
                    for w2 in range(2):
                        for g2 in range(NG):
                            W = GROUPS[g2][0]
                            sp.dma_start(out_caches[g2][0, :, w2, W - 1].rearrange("s h d -> s (h d)"),
                                         s_kvn[0:NS, CROW * (3 * w2 + g2):CROW * (3 * w2 + g2) + CROW]) \
                                .then_inc(ZA.out, 16)

        def sample_a_pe(pe):
            nb = len(MA.batches)
            pe.wait_ge(SA.sc_exp, 2 * nb * A_PAIRS)
            pe.wait_ge(SA.o_norm, 2 * A_PAIRS)
            pe.wait_ge(ZA.cols, 16)
            for b in range(6):
                for e in range(4):
                    mm = pe.transpose(acc[0:NS, b, P * e:P * e + P], s_cols[:, 12 + 4 * b + e, :], ident)
                mm.then_inc(ZA.moved, 1)
            pe.wait_ge(ZA.prep, 4)
            for g in range(NG):
                for h in range(2):
                    mm = pe.matmul(aux[32 * h:32 * h + 32, 1, g:g + 1],
                                   s_prod[HD * h:HD * h + HD, 32 * g:32 * g + 32], ones[HD * h:HD * h + HD, 0:1],
                                   start=True, stop=True)
            pe.wait_ge(ZA.kt, 6)

            def turn(m):
                n, e = divmod(m, 2)
                if e == 0:
                    pe.wait_ge(ZA.cache[n % 4], 16 * (n // 4 + 1))
                if m >= 4:
                    pe.wait_ge(ZA.kt, m - 3 + 6)
                for c in range(4):
                    mm = pe.transpose(acc[:, m % 4, P * c:P * c + P], s_ring[:, n % 4, e, P * c:P * c + P], ident)
                mm.then_inc(ZA.moved, 1)

            def score(m):
                n, e = divmod(m, 2)
                g, s2 = divmod(n, NS // 2)
                s = 2 * s2 + e
                pe.wait_ge(ZA.kt, m + 1 + 6)
                for c in range(4):
                    at0 = 64 * g + 8 * c + s
                    mm = pe.matmul(aux[:, 0, at0:at0 + 33:32], s_kt[:, 512 * (m % 2) + P * c:512 * (m % 2) + P * c + P],
                                   s_qb[:, 4 * g + c, s, :], start=True, stop=True)
                mm.then_inc(ZA.scored, 1)

            turn(0)
            for m in range(1, 2 * STEPS_A):
                turn(m)
                score(m - 1)
            score(2 * STEPS_A - 1)
            pe.wait_ge(ZA.step, 1)
            for g in range(NG):
                mm = pe.transpose(acc[0:64, 0, P * g:P * g + P], s_stc[:, 64 * g:64 * g + 64], ident)
            mm.then_inc(ZA.moved, 1)
            pe.wait_ge(ZA.step, 9)
            for g in range(NG):
                pe.transpose(acc[:, 1, 64 * g:64 * g + 64], s_all[0:64, P * g:P * g + P], ident[0:64, 0:64])
            pe.matmul(acc[0:NS, 2, 0:192], cst[0:64, C_E64:C_E64 + NS], s_dg[0:64, :], start=True, stop=True) \
                .then_inc(ZA.moved, 1)
            pe.wait_ge(ZA.step, 11)
            for n in range(STEPS_A):
                g, s2 = divmod(n, NS // 2)
                r = STEPS_A + n
                pe.wait_ge(ZA.cache[r % 4], 16 * (r // 4 + 1))
                for e in range(2):
                    s = 2 * s2 + e
                    for c in range(4):
                        mm = pe.matmul(acc[:, 3, 16 * c + 2 * s:16 * c + 2 * s + 2],
                                       s_ring[:, r % 4, e, P * c:P * c + P],
                                       s_pT[:, 64 * g + 8 * c + s:64 * g + 8 * c + s + 33:32],
                                       start=(n == 0 and e == 0 and c == 0), stop=False, skip_group_check=True)
                mm.then_inc(ZA.pe, 1)
            for g in range(NG):
                for c in range(4):
                    mm = pe.matmul(acc[:, 3, 16 * c:16 * c + 16].rearrange("p (s h) -> p s h", h=2),
                                   s_kvn[0:NS, CROW * (3 + g) + P * c:CROW * (3 + g) + P * c + P],
                                   s_D[0:NS, 64 * g:64 * g + 64].rearrange("p (h c s) -> p c s h", h=2, c=4)[:, c],
                                   start=False, stop=True, skip_group_check=True)
            mm.then_inc(ZA.pe, 1)

        def sample_a_dve(v):
            v.wait_ge(ZA.cols, 16)
            v.memset(s_qb, 0.0).then_inc(ZA.prep, 1)
            v.tensor_tensor(s_prod.rearrange("p (c s) -> p c s", s=NS), s_cols[:, 0:12, :], s_cols[:, 12:24, :],
                            ALU.mult).then_inc(ZA.prep, 1)
            v.wait_ge(ZA.prep, 1)
            for h in range(2):
                v.tensor_copy(s_qb[HD * h:HD * h + HD, :, :, h], s_cols[HD * h:HD * h + HD, 0:12, :]) \
                    .then_inc(ZA.prep, 1)
            for b in range(6):
                v.wait_ge(ZA.moved, b + 1)
                v.tensor_copy(s_kvn[0:NS, 512 * b:512 * b + 512], acc[0:NS, b, :]).then_inc(ZA.kt, 1)
            for m in range(2 * STEPS_A):
                v.wait_ge(ZA.moved, m + 1 + 6)
                if m >= 2:
                    v.wait_ge(ZA.scored, m - 1)
                v.tensor_copy(s_kt[:, 512 * (m % 2):512 * (m % 2) + 512], acc[:, m % 4, :]).then_inc(ZA.kt, 1)
            v.wait_ge(ZA.scored, 2 * STEPS_A)
            v.tensor_copy(s_stc, aux[:, 0, 0:192]).then_inc(ZA.step, 1)
            v.wait_ge(ZA.moved, 2 * STEPS_A + 7)
            v.tensor_copy(s_all[0:64, 0:384], acc[0:64, 0, 0:384]).then_inc(ZA.step, 1)
            v.tensor_copy(s_all[0:64, 384:387], aux[0:64, 1, 0:NG]).then_inc(ZA.step, 1)
            v.wait_ge(ZA.step, 3)
            v.tensor_reduce(s_red[0:64, 0:1], s_all[0:64, :], AX_X, ALU.max).then_inc(ZA.step, 1)
            v.wait_ge(ZA.step, 4)
            v.tensor_scalar(s_red[0:64, 1:2], s_red[0:64, 0:1], -SCALE, None, ALU.mult).then_inc(ZA.step, 1)
            v.wait_ge(ZA.act, 1)
            v.reciprocal(s_red[0:64, 3:4], s_red[0:64, 2:3]).then_inc(ZA.step, 1)
            v.wait_ge(ZA.step, 6)
            v.tensor_scalar(s_all[0:64, :], s_all[0:64, :], s_red[0:64, 3:4], None, ALU.mult).then_inc(ZA.step, 1)
            v.wait_ge(ZA.step, 7)
            for g in range(NG):
                ins = v.tensor_scalar(s_dg[0:64, 64 * g:64 * g + 64], ident[0:64, 0:64],
                                      s_all[0:64, 384 + g:385 + g], None, ALU.mult)
                if g:
                    ins.then_inc(ZA.step, 1)
            v.wait_ge(ZA.moved, 2 * STEPS_A + 8)
            v.tensor_copy(s_pT, acc[:, 1, 0:192]).then_inc(ZA.step, 1)
            v.tensor_copy(s_D[0:NS, :], acc[0:NS, 2, 0:192]).then_inc(ZA.step, 1)
            v.wait_ge(ZA.pe, STEPS_A + 1)
            for h in range(2):
                v.tensor_copy(s_of[HD * h:HD * h + HD, :],
                              acc[HD * h:HD * h + HD, 3, 0:64].rearrange("p (n h) -> p n h", h=2)[:, :, h]) \
                    .then_inc(ZA.step, 1)
            v.wait_ge(ZA.step, 13)
            v.wait_ge(ZA.act, 2)
            v.tensor_tensor(xl[:, 0:4, SEQ:T], s_of.rearrange("p (c s) -> p c s", s=NS),
                            xh[:, 0:4, SEQ:T].bitcast(F32), ALU.subtract).then_inc(ZA.fin, 1)

        def sample_a_act(act):
            act.wait_ge(ZA.step, 5)
            act.activation(s_all[0:64, :], s_all[0:64, :], ACT.Exp, bias=s_red[0:64, 1:2], scale=SCALE,
                           accum_out=s_red[0:64, 2:3]).then_inc(ZA.act, 1)
            act.wait_ge(ZA.step, 13)
            act.copy(xh[:, 0:4, SEQ:T], s_of.rearrange("p (c s) -> p c s", s=NS)).then_inc(ZA.act, 1)

        NH = 2 * B_CHUNKS
        b_k, b_v, b_kt, b_cols, b_qb, b_prod, b_stc, b_all, b_pT, b_dg, b_D, b_kvn, b_red, b_of, b_new, b_rows = carve(
            NS * P, NS * P, NS * P, 10 * NS, P, P, P, 130, P, P, P, 256, 8, 64, 256, 256)
        b_cols = b_cols.rearrange("p (c s) -> p c s", s=NS)
        b_qb = b_qb.rearrange("p (h s) -> p h s", s=NS)
        b_of = b_of.rearrange("p (c s) -> p c s", s=NS)

        def sample_b_sp(sp):
            nb = len(MB.batches)
            sp.wait_ge(SB.pv, 2 * nb * B_CHUNKS)
            sp.wait_ge(SB.o_lo, B_CHUNKS)
            sp.dma_start(b_cols, scratch[A_CHUNKS:46, :, SEQ:T].rearrange("c p t -> p c t")).then_inc(ZB.cols, 16)
            sp.dma_start(b_new.rearrange("p (c t) -> p c t", c=2),
                         scratch[A_CHUNKS:A_CHUNKS + 2, :, SEQ - P:SEQ].rearrange("c p t -> p c t")) \
                .then_inc(ZB.cols, 16)
            for w, x in enumerate((b_k, b_v)):
                sp.dma_start(x.rearrange("p (s c) -> p s c", s=NS),
                             a["cache_b_kv"][:, w].rearrange("s w h d -> w s (h d)")).then_inc(ZB.cache[w], 16)
            sp.wait_ge(ZB.kt, 2)
            for w in range(2):
                sp.dma_start(outs["b_kv_sample"][:, w, P - 1].rearrange("s h d -> s (h d)"),
                             b_kvn[0:NS, P * w:P * w + P]).then_inc(ZB.out, 16)
                sp.dma_start(outs["b_kv_prompt"][0, w].rearrange("t h d -> t (h d)"),
                             b_rows[:, P * w:P * w + P]).then_inc(ZB.out, 16)

        def sample_b_pe(pe):
            nb = len(MB.batches)
            pe.wait_ge(SB.sc_exp, 2 * nb * B_CHUNKS)
            pe.wait_ge(SB.o_norm, 2 * B_CHUNKS)
            pe.wait_ge(ZB.cols, 32)
            for w in range(2):
                mm = pe.transpose(acc[0:NS, 5, P * w:P * w + P], b_cols[:, w, :], ident)
            mm.then_inc(ZB.moved, 1)
            for w in range(2):
                mm = pe.transpose(acc[:, 4, P * w:P * w + P], b_new[:, P * w:P * w + P], ident)
            mm.then_inc(ZB.moved, 1)
            pe.wait_ge(ZB.cache[0], 16)
            for s in range(NS):
                mm = pe.transpose(acc[:, s // 4, P * (s % 4):P * (s % 4) + P], b_k[:, P * s:P * s + P], ident)
            mm.then_inc(ZB.moved, 1)
            pe.wait_ge(ZB.prep, 6)
            pe.matmul(aux[:, 1, 0:1], b_prod, ones[:, 0:1], start=True, stop=True)
            pe.wait_ge(ZB.kt, 4)
            for s in range(NS):
                mm = pe.matmul(aux[:, 0, s:s + 8 * (NH - 1) + 1:8], b_kt[:, P * s:P * s + P], b_qb[:, :, s],
                               start=True, stop=True)
            mm.then_inc(ZB.scored, 1)
            pe.wait_ge(ZB.step, 1)
            pe.transpose(acc[:, 2, 0:P], b_stc, ident).then_inc(ZB.moved, 1)
            pe.wait_ge(ZB.step, 10)
            pe.transpose(acc[:, 3, 0:P], b_all[:, 0:P], ident)
            pe.matmul(acc[0:NS, 1, 0:P], cst[:, C_E128:C_E128 + NS], b_dg, start=True, stop=True).then_inc(ZB.moved, 1)
            pe.wait_ge(ZB.step, 12)
            pe.wait_ge(ZB.cache[1], 16)
            for s in range(NS):
                pe.matmul(acc[:, 0, s:s + 8 * (NH - 1) + 1:8], b_v[:, P * s:P * s + P],
                          b_pT[:, s:s + 8 * (NH - 1) + 1:8], start=(s == 0), stop=False, skip_group_check=True)
            pe.matmul(acc[:, 0, 0:P], b_kvn[0:NS, P:2 * P], b_D[0:NS, :], start=False, stop=True,
                      skip_group_check=True).then_inc(ZB.pe, 1)

        def sample_b_dve(v):
            v.wait_ge(ZB.cols, 32)
            v.memset(b_qb, 0.0).then_inc(ZB.prep, 1)
            v.wait_ge(ZB.prep, 1)
            for kv in range(2):
                for h in range(2):
                    v.tensor_copy(b_qb[HD * kv:HD * kv + HD, 8 * kv + h:8 * kv + 8:2, :],
                                  b_cols[HD * h:HD * h + HD, 2 + 4 * kv:6 + 4 * kv, :]).then_inc(ZB.prep, 1)
            v.wait_ge(ZB.prep, 5)
            v.tensor_tensor(b_prod.rearrange("p (h s) -> p h s", s=NS), b_qb,
                            b_cols[:, 0, :].unsqueeze(1).to_broadcast([P, NH, NS]), ALU.mult).then_inc(ZB.prep, 1)
            v.wait_ge(ZB.moved, 1)
            v.tensor_copy(b_kvn[0:NS, :], acc[0:NS, 5, 0:256]).then_inc(ZB.kt, 1)
            v.wait_ge(ZB.moved, 2)
            v.tensor_copy(b_rows, acc[:, 4, 0:256]).then_inc(ZB.kt, 1)
            v.wait_ge(ZB.moved, 3)
            for half in range(2):
                v.tensor_copy(b_kt[:, 512 * half:512 * half + 512], acc[:, half, :]).then_inc(ZB.kt, 1)
            v.wait_ge(ZB.scored, 1)
            v.tensor_copy(b_stc, aux[:, 0, 0:P]).then_inc(ZB.step, 1)
            v.wait_ge(ZB.moved, 4)
            v.tensor_copy(b_all[:, 0:P], acc[:, 2, 0:P]).then_inc(ZB.step, 1)
            v.tensor_copy(b_all[:, P:P + 1], aux[:, 1, 0:1]).then_inc(ZB.step, 1)
            v.tensor_copy(b_all[:, P + 1:P + 2], sink_col[:]).then_inc(ZB.step, 1)
            v.wait_ge(ZB.step, 2)
            v.memset(b_all[:, 0:1], MASKED).then_inc(ZB.step, 1)
            v.wait_ge(ZB.step, 5)
            v.tensor_reduce(b_red[:, 0:1], b_all, AX_X, ALU.max).then_inc(ZB.step, 1)
            v.wait_ge(ZB.step, 6)
            v.tensor_scalar(b_red[:, 1:2], b_red[:, 0:1], -SCALE, None, ALU.mult).then_inc(ZB.step, 1)
            v.wait_ge(ZB.act, 1)
            v.reciprocal(b_red[:, 3:4], b_red[:, 2:3]).then_inc(ZB.step, 1)
            v.wait_ge(ZB.step, 8)
            v.tensor_scalar(b_all, b_all, b_red[:, 3:4], None, ALU.mult).then_inc(ZB.step, 1)
            v.wait_ge(ZB.step, 9)
            v.tensor_scalar(b_dg, ident, b_all[:, P:P + 1], None, ALU.mult).then_inc(ZB.step, 1)
            v.wait_ge(ZB.moved, 5)
            v.tensor_copy(b_pT, acc[:, 3, 0:P]).then_inc(ZB.step, 1)
            v.tensor_copy(b_D[0:NS, :], acc[0:NS, 1, 0:P]).then_inc(ZB.step, 1)
            v.wait_ge(ZB.pe, 1)
            for kv in range(2):
                for h in range(2):
                    v.tensor_copy(b_of[HD * h:HD * h + HD, 4 * kv:4 * kv + 4, :],
                                  acc[HD * kv:HD * kv + HD, 0, 0:P].rearrange("p (h s) -> p h s", s=NS)
                                  [:, 8 * kv + h:8 * kv + 8:2, :]).then_inc(ZB.step, 1)
            v.wait_ge(ZB.step, 16)
            v.wait_ge(ZB.act, 2)
            v.tensor_tensor(xl[:, :, SEQ:T], b_of, xh[:, :, SEQ:T].bitcast(F32), ALU.subtract).then_inc(ZB.fin, 1)

        def sample_b_act(act):
            act.wait_ge(ZB.step, 7)
            act.activation(b_all, b_all, ACT.Exp, bias=b_red[:, 1:2], scale=SCALE,
                           accum_out=b_red[:, 2:3]).then_inc(ZB.act, 1)
            act.wait_ge(ZB.step, 16)
            act.copy(xh[:, :, SEQ:T], b_of).then_inc(ZB.act, 1)

        yp = outs["y_prompt"].rearrange("b s d -> (b s) d")
        ys = outs["y_sample"].rearrange("b s d -> (b s) d")

        def rows_out_pe(pe):
            pe.wait_ge(h_added, ADDED[1] + KC * FFN_TURNS)
            for n in range(NTILE + 1):
                rows = P if n < NTILE else NS
                if n >= 3:
                    pe.wait_ge(y_set, 2 * (n - 3) + 2)
                for c in range(KC):
                    mm = pe.transpose(acc[0:rows, (2 * n + c // 4) % 6, P * (c % 4):P * (c % 4) + P],
                                      hT[:, c, P * n:P * n + rows], ident)
                mm.then_inc(y_turned, 1)

        def rows_out_dve(v):
            for n in range(NTILE + 1):
                rows = P if n < NTILE else NS
                v.wait_ge(y_turned, n + 1)
                if n >= 2:
                    v.wait_ge(y_out[n % 2], 16 * (n // 2))
                for b in range(2):
                    v.tensor_copy(y_stage[n % 2][0:rows, 512 * b:512 * b + 512], acc[0:rows, (2 * n + b) % 6, :]) \
                        .then_inc(y_set, 1)

        def rows_out_sp(sp):
            for n in range(NTILE + 1):
                sp.wait_ge(y_set, 2 * n + 2)
                if n < NTILE:
                    sp.dma_start(yp[P * n:P * n + P, :], y_stage[n % 2]).then_inc(y_out[n % 2], 16)
                else:
                    sp.dma_start(ys, y_stage[n % 2][0:NS]).then_inc(y_out[n % 2], 16)

        def copies_sp(sp):
            sp.dma_start(c_to[:, PIECE * (CACHE_PIECES - 1):PIECE * CACHE_PIECES],
                         c_from[:, ROW + PIECE * (CACHE_PIECES - 1):ROW + PIECE * CACHE_PIECES]).then_inc(copied, 16)
            for g in range(2):
                W = GROUPS[g][0]
                sp.dma_start(out_caches[g][0, :, :, 0:W - 1].rearrange("s x w h d -> (s x) (w h d)"),
                             caches[g][0, :, :, 1:W].rearrange("s x w h d -> (s x) (w h d)")).then_inc(copied, 16)
            sp.dma_start(outs["b_kv_sample"][:, :, 0:P - 1].rearrange("s x w h d -> (s x) (w h d)"),
                         a["cache_b_kv"][:, :, 1:P].rearrange("s x w h d -> (s x) (w h d)")).then_inc(copied, 16)
            for l in range(2):
                sp.dma_start(outs["ffn_conv_sample"][l, :, 0], a["state_ffn_conv"][l, :, 1]).then_inc(copied, 16)
        COPIES = 2 * FFN_TURNS + 1 + 2 + 1 + 2

        block = ctx.enter_context(nc.Block())

        @block.sync
        def _(sp):
            rows_in_sp(sp)
            tables_sp(sp)
            proj_a_sp(sp)
            copies_sp(sp)
            for k in range(2):
                sp.wait_ge(stored[k], 16 * A_CHUNKS // 2)
            with sp.Fori(0, A_PAIRS) as i:
                attn_sp(sp, MA, SA, i, i, None)
            sample_a_sp(sp)
            load(sp, wcols(w_aout, 3, 2 * P), U_AOUT + 3)
            ffn_sp(sp, 0)
            for n in range(3):
                load(sp, wcols([a["b_w_kv"], a["b_w_kv"], w_q][n], [0, 1, 0][n]), U_KV + n)
            tails_sp(sp, 0)
            proj_b_sp(sp)
            for k in range(2):
                sp.wait_ge(stored[k], 16 * 46 // 2)
            for kv in range(2):
                with sp.Fori(0, 4) as i:
                    attn_sp(sp, MB, SB, 4 * kv + i, i, kv)
            sample_b_sp(sp)
            for n in range(3, KC):
                load(sp, wcols(w_bout, n), U_BOUT + n)
            ffn_sp(sp, 1)
            tails_sp(sp, 1)
            rows_out_sp(sp)
            sp.wait_ge(y_out[0], 16 * 5)
            sp.wait_ge(y_out[1], 16 * 4)
            sp.wait_ge(tail_out, 16 * TAILS * 2)
            sp.wait_ge(ZA.out, 16 * 6)
            sp.wait_ge(ZB.out, 16 * 4)
            sp.wait_ge(SA.exported, 16 * 8 * A_PAIRS)
            sp.wait_ge(copied, 16 * COPIES)

        @block.gpsimd
        def _(pool):
            pool.sem_inc(lo_ready, RING)
            with pool.Fori(0, (U_END - U_QKV) // RING) as i:
                for e in range(RING):
                    split_lo(pool, U_QKV + e, RING, i)
            for u in range(U_END - (U_END - U_QKV) % RING, U_END):
                split_lo(pool, u)

        @block.scalar
        def _(act):
            act.preload_act_table_set("natural_log_exp_and_others")
            counts_act(act)
            split_hi(act, U_QKV)
            split_hi(act, U_QKV + 1)
            act.wait_ge(const_set, CONSTS_SET)
            act.wait_ge(tab_set, 6)
            norm_act(act, 0, lambda e: e.wait_ge(h_set, 2 * (NTILE + 1)))
            proj_a_act(act)
            with act.Fori(0, A_PAIRS) as i:
                attn_act(act, MA, SA, i)
            sample_a_act(act)
            aout_act(act)
            ffn_act(act, 0)
            act.wait_ge(tail_out, 16 * TAILS)
            norm_act(act, 2, lambda e: e.wait_ge(h_added, ADDED["b"]))
            proj_b_act(act)
            with act.Fori(0, B_CHUNKS) as i:
                attn_act(act, MB, SB, i)
            sample_b_act(act)
            bout_act(act)
            ffn_act(act, 1)

        @block.vector
        def _(v):
            v.sem_inc(chunk_out, 3 * CH)
            rows_in_dve(v)
            consts_dve(v)
            norm_dve(v, 0, lambda e: None)
            proj_a_dve(v)
            for k in range(2):
                v.wait_ge(stored[k], 16 * A_CHUNKS // 2)
            v.memset(BUF[id(MA)][3][:, :, HD:2 * HD], 1.0)
            with v.Fori(0, A_PAIRS) as i:
                attn_dve(v, MA, SA, i)
            sample_a_dve(v)
            aout_dve(v)
            ffn_dve(v, 0)
            norm_dve(v, 2, lambda e: e.wait_ge(h_added, ADDED["b"]))
            proj_b_dve(v)
            for k in range(2):
                v.wait_ge(stored[k], 16 * 46 // 2)
            v.memset(BUF[id(MB)][3][:, :, HD:2 * HD], 1.0)
            with v.Fori(0, B_CHUNKS) as i:
                attn_dve(v, MB, SB, i)
            sample_b_dve(v)
            bout_dve(v)
            ffn_dve(v, 1)
            rows_out_dve(v)

        @block.tensor
        def _(pe):
            counts_pe(pe)
            rows_in_pe(pe)
            pe.wait_ge(const_set, CONSTS_SET)
            norm_pe(pe, 0)
            proj_a_pe(pe)
            pe.wait_ge(chunk_out, 3 * CH_B)
            with pe.Fori(0, A_PAIRS) as i:
                attn_pe(pe, MA, SA, i)
            sample_a_pe(pe)
            aout_pe(pe)
            ffn_pe(pe, 0)
            proj_b_pe(pe)
            pe.wait_ge(chunk_out, 3 * (CH_B + 2 + B_CHUNKS))
            with pe.Fori(0, B_CHUNKS) as i:
                attn_pe(pe, MB, SB, i)
            sample_b_pe(pe)
            bout_pe(pe)
            ffn_pe(pe, 1)
            rows_out_pe(pe)


INPUTS = ["x_prompt", "x_sample", "cache_a_kv_w128", "cache_a_kv_w512", "cache_a_kv_w2048", "cache_b_kv",
          "state_ffn_conv", "attn_norm_g", "ffn_norm_g", "a_w_in", "a_q_norm_g", "a_k_norm_g", "a_w_out",
          "b_kv_norm_g", "b_w_kv", "b_k_norm_g", "b_w_q", "b_q_norm_g", "b_sinks", "b_w_out",
          "ffn_w_up", "ffn_conv_w", "ffn_conv_b", "ffn_w_down"]
OUTPUTS = [
    ("y_prompt", (1, SEQ, D)), ("y_sample", (NS, 1, D)),
    ("a_w128_prompt", (1, 1, 2, 128, 8, HD)), ("a_w128_sample", (1, NS, 2, 128, 8, HD)),
    ("a_w512_prompt", (1, 1, 2, 512, 8, HD)), ("a_w512_sample", (1, NS, 2, 512, 8, HD)),
    ("a_w2048_prompt", (1, 1, 2, SEQ, 8, HD)), ("a_w2048_sample", (1, NS, 2, 2048, 8, HD)),
    ("b_kv_prompt", (1, 2, 128, 2, HD)), ("b_kv_sample", (NS, 2, 128, 2, HD)),
    ("ffn_conv_prompt", (2, 1, 2, 2 * DFF)), ("ffn_conv_sample", (2, NS, 2, 2 * DFF)),
]


def kernel(**inputs):
    import concourse.bacc as bacc
    from concourse.bass_utils import run_bass_kernel_spmd

    nc = bacc.Bacc("TRN2", target_bir_lowering=False, num_devices=1, dynamic_dma_scratch_size=1024)
    arrays, a, outs = {}, {}, {}
    for name in INPUTS:
        arrays["in_" + name] = np.ascontiguousarray(inputs[name])
    arrays["in_consts"] = shape_constants()
    for name, x in arrays.items():
        a[name[3:]] = nc.dram_tensor(name, x.shape, F32, kind="ExternalInput").ap()
    for name, shape in OUTPUTS:
        outs[name] = nc.dram_tensor("out_" + name, shape, F32, kind="ExternalOutput").ap()
    build(nc, a, outs)
    r = run_bass_kernel_spmd(nc, [arrays], core_ids=[0])
    return tuple(r.results[0]["out_" + name] for name, _ in OUTPUTS)
```

```python
from contextlib import ExitStack

import numpy as np

import concourse.bass as bass
from concourse import mybir

F32 = mybir.dt.float32
F32R = mybir.dt.float32r
BF16 = mybir.dt.bfloat16
ALU = mybir.AluOpType
ACT = mybir.ActivationFunctionType
AX_X = mybir.AxisListType.X

P = 128
D = 1024
KC = D // P
SEQ = 1024
NS = 8
T = SEQ + NS
NT = 3
TH = T // NT
HD = 64
DFF = 2816
FC = DFF // P
PAST = 4096
GROUPS = ((128, 1), (512, 4), (2048, 16))
NG = len(GROUPS)
A_PAIRS = 4
B_CHUNKS = 8
EPS = 1e-6
SCALE = HD ** -0.5
MASKED = -1e30
RING = 3
BODY = 6
A_CHUNKS = 36
NTILE = SEQ // P

U_QKV = RING
U_AOUT = U_QKV + A_CHUNKS
U_FFN0 = U_AOUT + 4
FFN_TURNS = FC // 2
FFN_UNITS = 6 * FFN_TURNS
U_KV = U_FFN0 + FFN_UNITS
U_BQ = U_KV + 2
U_BOUT = U_BQ + B_CHUNKS
U_FFN1 = U_BOUT + 8
U_END = U_FFN1 + FFN_UNITS

C_ID, C_ONES, C_E64, C_E128, C_BLK, C_ROT = 0, 128, 256, 264, 272, 400
C_MQ, C_MK = 528, 1040
C_COS, C_SIN = 1552, 1552 + T
C_END = C_SIN + T
CUR, PREV_A, BOTH, PREV_B = range(4)


def shape_constants():
    c = np.zeros((P, C_END), np.float32)
    i = np.arange(P)
    c[:, C_ID:C_ID + P] = np.eye(P)
    c[:, C_ONES:C_ONES + P] = 1.0
    c[:, C_BLK:C_BLK + P] = i[:, None] // HD == i[None, :] // HD
    for m in range(P):
        half = m % HD < HD // 2
        c[m + HD // 2 if half else m - HD // 2, C_ROT + m] = -1.0 if half else 1.0
    c[:, C_E64:C_E64 + NS] = i[:, None] % NS == np.arange(NS)
    c[:, C_E128:C_E128 + NS] = i[:, None] % NS == np.arange(NS)
    q, k = i[:, None], i[None, :]
    valid = [k <= q, k >= q, (k <= q) & (k % 2 == q % 2), k > q]
    for n, v in enumerate(valid):
        m = np.where(v, 0.0, MASKED)
        c[:, C_MQ + n * P:C_MQ + (n + 1) * P] = m
        c[:, C_MK + n * P:C_MK + (n + 1) * P] = m.T
    pos = np.concatenate([np.arange(SEQ), np.full(NS, PAST)]).astype(np.float32)
    inv = (10000.0 ** (-np.arange(HD // 2) / (HD // 2))).astype(np.float32)
    ang = (pos[None, :] * inv[i % (HD // 2), None]).astype(np.float32)
    c[:, C_COS:C_COS + T] = np.cos(ang.astype(np.float64))
    c[:, C_SIN:C_SIN + T] = np.sin(ang.astype(np.float64))
    return c


class Mixer:

    def __init__(self, groups):
        self.ng = groups
        b = []
        prev = PREV_A if groups > 1 else PREV_B
        cols = 8 * groups
        for g in range(groups):
            kind = BOTH if g == 2 else CUR
            for t in (0, 4):
                b.append((g, kind, [(t + e, t + e, 8 * g + t + e) for e in range(4)]))
        b.append((0, prev, [(t, t - 1, cols + t - 1) for t in range(1, 5)]))
        b.append((0, prev, [(t, t - 1, cols + t - 1) for t in range(5, 8)]))
        if groups > 1:
            b.append((1, prev, [(2 * r + 1, 2 * r, cols + 7 + r) for r in range(4)]))
        self.batches = b
        self.cols = cols + 7 + (4 if groups > 1 else 0)


def tile_tokens(x, g, tile):
    if g == 0:
        return x[:, P * tile:P * tile + P]
    if g == 1:
        r, b = divmod(tile, 2)
        return x.rearrange("p (n s) -> p s n", s=4)[:, r, P * b:P * b + P]
    return x.rearrange("p (n s) -> p s n", s=8)[:, tile, :]


def batch_tokens(x, g, kind, blocks):
    t0 = blocks[0][0]
    if g == 0:
        return x[:, P * t0:P * (t0 + len(blocks))]
    if g == 1:
        s = x.rearrange("p (n s) -> p s n", s=4)
        return s[:, 0:4, P:2 * P] if kind == PREV_A else s[:, t0 // 2:t0 // 2 + 2, :]
    return x.rearrange("p (n s) -> p s n", s=8)[:, t0:t0 + 4, :]


def build(nc, a, outs):
    with ExitStack() as ctx:
        def sb(name, shape, dt=F32):
            return ctx.enter_context(nc.sbuf_tensor(name, shape, dt))

        def sem(name):
            return ctx.enter_context(nc.semaphore(name))

        hT = sb("hT", [P, KC, T])
        xh = sb("xh", [P, KC, T], F32R)
        xl = sb("xl", [P, KC, T], F32R)
        w_raw = sb("w_raw", [P, RING, 1024])
        w_hi = sb("w_hi", [P, RING, 1024], F32R)
        w_lo = sb("w_lo", [P, RING, 1024], F32R)
        f_hi = sb("f_hi", [P, 2, T], F32R)
        f_lo = sb("f_lo", [P, 2, T], F32R)
        cst = sb("cst", [P, C_BLK])
        head_ops = sb("head_ops", [P, 2, P], F32R)
        rope = sb("rope", [P, 2, T])
        masks = sb("masks", [P, 2, 4, P], BF16)
        ident_b = sb("ident_b", [P, P], BF16)
        sel = sb("sel", [2, 2, P], F32R)
        sel_den = sb("sel_den", [2, 2, P])
        neg_max = sb("neg_max", [2, SEQ], F32R)
        rinv = sb("rinv", [P, T])
        norm_g = sb("norm_g", [P, 5, KC])
        head_g = sb("head_g", [P, 46])
        eps = sb("eps", [P, 1])
        cw = sb("cw", [P, 2, 4, 2 * FC])
        st_T = sb("st_T", [P, 2, NS, 4 * FC])
        u_tail = sb("u_tail", [P, 10, 2 * FC])
        sink8 = sb("sink8", [2, B_CHUNKS])
        sink = sb("sink", [2, B_CHUNKS])
        sink_now = sb("sink_now", [2, 1])
        sink_col = sb("sink_col", [P, 1])
        ARENA = 10800
        arena = sb("arena", [P, ARENA])
        acc = ctx.enter_context(nc.psum_tensor("acc", [P, 6, 512], F32))
        aux = ctx.enter_context(nc.psum_tensor("aux", [P, 2, 512], F32))

        ident = cst[:, C_ID:C_ID + P]
        ones = cst[:, C_ONES:C_ONES + P]
        blk, rot = head_ops[:, 0, :], head_ops[:, 1, :]

        def carve(*sizes):
            at, views = 0, []
            for s in sizes:
                views.append(arena[:, at:at + s])
                at += s
            assert at <= ARENA, at
            return views

        scratch = nc.dram_tensor("scratch", [46, P, T], F32).ap()

        ident_in = sem("ident_in")
        const_in = sem("const_in")
        const_set = sem("const_set")
        x_in = [sem(f"x_in{i}") for i in range(2)]
        x_turned = sem("x_turned")
        h_set = sem("h_set")
        tab_in = sem("tab_in")
        gain_rows_set = sem("gain_rows_set")
        gains_turned = sem("gains_turned")
        gains_set = sem("gains_set")
        tab_turned = sem("tab_turned")
        tab_set = sem("tab_set")
        w_landed = [sem(f"w_landed{i}") for i in range(RING)]
        hi_ready = sem("hi_ready")
        lo_ready = sem("lo_ready")
        w_used = sem("w_used")
        n_sq = sem("n_sq")
        n_mm = sem("n_mm")
        n_stat = sem("n_stat")
        n_add = sem("n_add")
        n_x = sem("n_x")
        n_hi = sem("n_hi")
        n_lo = sem("n_lo")
        third_full = sem("third_full")
        acc_evac = sem("acc_evac")
        sq_split = sem("sq_split")
        qg_split = sem("qg_split")
        aux_split = sem("aux_split")
        ssq_ready = sem("ssq_ready")
        rot_ready = sem("rot_ready")
        ln_done = sem("ln_done")
        r_ready = sem("r_ready")
        rot_used = sem("rot_used")
        qk_step = sem("qk_step")
        chunk_out = sem("chunk_out")
        stored = [sem(f"stored{i}") for i in range(2)]
        res_full = sem("res_full")
        h_added = sem("h_added")
        up_evac = sem("up_evac")
        conv_step = sem("conv_step")
        conv_out = sem("conv_out")
        e_ready = sem("e_ready")
        f_raw = sem("f_raw")
        fhi_ready = sem("fhi_ready")
        flo_ready = sem("flo_ready")
        d_done = sem("d_done")
        tail_turned = sem("tail_turned")
        tail_set = sem("tail_set")
        tail_out = sem("tail_out")
        y_turned = sem("y_turned")
        y_set = sem("y_set")
        y_out = [sem(f"y_out{i}") for i in range(2)]
        copied = sem("copied")
        chain = sem("chain")

        class Attn:
            def __init__(self, p):
                self.v_in = sem(f"{p}_v_in")
                self.k_in = sem(f"{p}_k_in")
                self.q_in = [sem(f"{p}_q_in{i}") for i in range(NG)]
                self.cleared = sem(f"{p}_cleared")
                self.moved = sem(f"{p}_moved")
                self.copied = sem(f"{p}_copied")
                self.exported = sem(f"{p}_exported")
                self.scored = sem(f"{p}_scored")
                self.maxed = sem(f"{p}_maxed")
                self.merged = sem(f"{p}_merged")
                self.turned = sem(f"{p}_turned")
                self.rowed = sem(f"{p}_rowed")
                self.shift = sem(f"{p}_shift")
                self.sc_full = sem(f"{p}_sc_full")
                self.sc_exp = sem(f"{p}_sc_exp")
                self.pv = sem(f"{p}_pv")
                self.o_out = sem(f"{p}_o_out")
                self.o_ln = sem(f"{p}_o_ln")
                self.o_rec = sem(f"{p}_o_rec")
                self.o_norm = sem(f"{p}_o_norm")
                self.o_hi = sem(f"{p}_o_hi")
                self.o_go = sem(f"{p}_o_go")
                self.seen = sem(f"{p}_seen")
                self.o_lo = sem(f"{p}_o_lo")
        SA, SB = Attn("a"), Attn("b")

        class Sample:
            def __init__(self, p):
                self.cols = sem(f"{p}_cols")
                self.cache = [sem(f"{p}_cache{i}") for i in range(4)]
                self.prep = sem(f"{p}_prep")
                self.moved = sem(f"{p}_moved")
                self.kt = sem(f"{p}_kt")
                self.scored = sem(f"{p}_scored")
                self.step = sem(f"{p}_step")
                self.act = sem(f"{p}_act")
                self.pe = sem(f"{p}_pe")
                self.out = sem(f"{p}_out")
                self.fin = sem(f"{p}_fin")
        ZA, ZB = Sample("sa"), Sample("sb")

        MA, MB = Mixer(NG), Mixer(1)
        PV0 = {id(MA): 0, id(MB): 2 * len(MB.batches)}

        def unit_at(u0, m=0, i=0):
            assert m % RING == 0
            if m:
                return u0 % RING, u0 + m * i, u0 // RING + (m // RING) * i
            return u0 % RING, u0, u0 // RING

        def load(sp, src, u0, m=0, i=0):
            slot, u, _ = unit_at(u0, m, i)
            sp.wait_ge(lo_ready, u - RING + 1)
            sp.dma_start(w_raw[:, slot, :].rearrange("p (k n) -> p k n", n=src.shape[-1]), src) \
                .then_inc(w_landed[slot], 16)

        def split_hi(act, u0, m=0, i=0):
            slot, u, use = unit_at(u0, m, i)
            act.wait_ge(w_landed[slot], 16 * use)
            act.wait_ge(w_used, u - RING + 1)
            act.copy(w_hi[:, slot, :], w_raw[:, slot, :]).then_inc(hi_ready, 1)

        def split_ahead(act, u0, m=0, i=0):
            if m or u0 + 2 < U_END:
                split_hi(act, u0 + 2, m, i)

        def split_lo(pool, u0, m=0, i=0):
            slot, u, _ = unit_at(u0, m, i)
            pool.wait_ge(hi_ready, u + 1)
            pool.tensor_tensor(w_lo[:, slot, :], w_raw[:, slot, :], w_hi[:, slot, :].bitcast(F32),
                               ALU.subtract).then_inc(lo_ready, 1)

        def units_pool(pool, u0, u1):
            loops = (u1 - u0) // RING
            with pool.Fori(0, loops) as i:
                for e in range(RING):
                    split_lo(pool, u0 + e, RING, i)
            for u in range(u0 + RING * loops, u1):
                split_lo(pool, u)

        def product(pe, out, whi, wlo, ahi, alo, first, last):
            pe.matmul(out, whi, ahi, start=first, stop=False)
            pe.matmul(out, whi, alo, start=False, stop=False)
            return pe.matmul(out, wlo, ahi, start=False, stop=last)

        def normed_product(pe, slot, n):
            w1 = w_hi[:, slot, :].rearrange("p (k n) -> p k n", n=P)
            w2 = w_lo[:, slot, :].rearrange("p (k n) -> p k n", n=P)
            for j in range(KC):
                pe.wait_ge(n_lo, 8 * n + j + 1)
                for t in range(NT):
                    mm = product(pe, acc_set(0)[:, t, :], w1[:, j, :], w2[:, j, :],
                                 xh[:, j, TH * t:TH * t + TH], xl[:, j, TH * t:TH * t + TH], j == 0, j == KC - 1)
                    if j == KC - 1:
                        yield mm

        def thirds(x):
            return x.rearrange("p (t n) -> p t n", n=TH)

        def acc_set(n):
            return acc[:, 3 * (n % 2):3 * (n % 2) + 3, 0:TH]

        def wcols(w, c, width=P):
            return w.rearrange("(k p) (c n) -> p k c n", p=P, n=width)[:, :, c, :]

        w_in = a["a_w_in"].rearrange("l k n -> (l k) n")
        w_aout = a["a_w_out"].rearrange("l k n -> (l k) n")
        w_q = a["b_w_q"].rearrange("l k n -> (l k) n")
        w_bout = a["b_w_out"].rearrange("l k n -> (l k) n")

        xs = carve(1024, 1024, 512, 512, 1024, 1024)
        x_stage, cw_stage, st_stage = xs[0:2], xs[2:4], xs[4:6]
        y_stage = xs[0:2]
        xp = a["x_prompt"].rearrange("b s d -> (b s) d")
        xsm = a["x_sample"].rearrange("b s d -> (b s) d")

        def rows_in_sp(sp):
            sp.dma_start(cst[:], a["consts"][:, 0:C_BLK]).then_inc(ident_in, 16)
            for n in range(NTILE + 1):
                if n >= 2:
                    sp.wait_ge(x_turned, n - 1)
                if n < NTILE:
                    sp.dma_start(x_stage[n % 2], xp[P * n:P * n + P, :]).then_inc(x_in[n % 2], 16)
                else:
                    sp.dma_start(x_stage[n % 2][0:NS], xsm).then_inc(x_in[n % 2], 16)
                if n == 1:
                    for u in range(U_QKV, U_QKV + 3):
                        load(sp, wcols(w_in, u - U_QKV), u)

        def tables_sp(sp):
            gains = [a["attn_norm_g"][0], a["ffn_norm_g"][0], a["b_kv_norm_g"], a["attn_norm_g"][1],
                     a["ffn_norm_g"][1]]
            for n, g in enumerate(gains):
                sp.dma_start(norm_rows[KC * n:KC * n + KC, :], g.rearrange("(k p) -> k p", p=P)).then_inc(tab_in, 16)
            sp.wait_ge(gain_rows_set, 1)
            for half in (0, HD):
                for c0, n, g in [(4 * e, 4, a["a_q_norm_g"][0, e]) for e in range(NG)] + \
                        [(12 + 4 * e, 4, a["a_k_norm_g"][0, e]) for e in range(NG)] + \
                        [(36, 1, a["b_k_norm_g"]), (38, 8, a["b_q_norm_g"][0])]:
                    sp.dma_start(head_rows[c0:c0 + n, half:half + HD],
                                 g.unsqueeze(0).to_broadcast([n, HD])).then_inc(tab_in, 16)
            sp.dma_start(sink_rows, a["b_sinks"][0].rearrange("(c h) -> c h", h=2)).then_inc(tab_in, 16)
            sp.dma_start(sink_col[:], a["b_sinks"][0].unsqueeze(1).to_broadcast([16, NS]).unsqueeze(2)) \
                .then_inc(const_in, 16)
            sp.dma_start(rope[:], a["consts"][:, C_COS:C_END].rearrange("p (a t) -> p a t", a=2)) \
                .then_inc(const_in, 16)
            sp.dma_start(mask_stage, a["consts"][:, C_MQ:C_COS]).then_inc(const_in, 16)
            sp.dma_start(op_stage, a["consts"][:, C_BLK:C_MQ]).then_inc(const_in, 16)
            for l in range(2):
                for t in range(3):
                    sp.dma_start(cw_stage[l][0:2 * FC, P * t:P * t + P],
                                 a["ffn_conv_w"][l, t].rearrange("(c f) -> c f", f=P)).then_inc(tab_in, 16)
                sp.dma_start(cw_stage[l][0:2 * FC, 3 * P:4 * P],
                             a["ffn_conv_b"][l].rearrange("(c f) -> c f", f=P)).then_inc(tab_in, 16)
                for t in range(2):
                    sp.dma_start(st_stage[l][2 * FC * t:2 * FC * (t + 1), :].rearrange("c (s f) -> c s f", f=P),
                                 a["state_ffn_conv"][l, :, t, :].rearrange("s (c f) -> c s f", f=P)) \
                        .then_inc(tab_in, 16)

        CONSTS_IN = 16 * 4
        TABLES_IN = 16 * (5 + 16 + 1 + 2 * 6)
        mask_stage, op_stage = arena[:, 6144:7168], arena[:, 7430:7430 + 2 * P]
        head_rows, norm_rows = arena[0:46, 7168:7296], arena[0:5 * KC, 7296:7424]
        sink_rows = arena[0:B_CHUNKS, 7424:7426]

        def rows_in_pe(pe):
            pe.wait_ge(ident_in, 16)
            for n in range(NTILE + 1):
                pe.wait_ge(x_in[n % 2], 16 * (n // 2 + 1))
                if n >= 3:
                    pe.wait_ge(h_set, 2 * (n - 3) + 2)
                rows = P if n < NTILE else NS
                for c in range(KC):
                    mm = pe.transpose(acc[:, (2 * n + c // 4) % 6, P * (c % 4):P * (c % 4) + rows],
                                      x_stage[n % 2][0:rows, P * c:P * c + P], ident[0:rows, 0:rows])
                mm.then_inc(x_turned, 1)
            pe.wait_ge(tab_in, TABLES_IN)
            pe.transpose(aux[:, 1, 0:46], head_rows, ident[0:46, 0:46])
            pe.transpose(aux[:, 1, 64:64 + 5 * KC], norm_rows, ident[0:5 * KC, 0:5 * KC])
            pe.transpose(aux[0:2, 1, 128:128 + B_CHUNKS], sink_rows, ident[0:B_CHUNKS, 0:B_CHUNKS]) \
                .then_inc(gains_turned, 1)
            pe.wait_ge(gains_set, 3)
            for l in range(2):
                if l:
                    pe.wait_ge(tab_set, 2)
                for t in range(4):
                    mm = pe.transpose(aux[:, 0, 2 * FC * t:2 * FC * (t + 1)], cw_stage[l][0:2 * FC, P * t:P * t + P],
                                      ident[0:2 * FC, 0:2 * FC])
                mm.then_inc(tab_turned, 1)
                for half in range(2):
                    pe.wait_ge(tab_set, 3 * l + half) if l or half else None
                    for s in range(4):
                        q = 4 * half + s
                        mm = pe.transpose(aux[:, 1, 4 * FC * s:4 * FC * (s + 1)],
                                          st_stage[l][0:4 * FC, P * q:P * q + P], ident[0:4 * FC, 0:4 * FC])
                    mm.then_inc(tab_turned, 1)
                    pe.wait_ge(tab_set, 3 * l + half + 2)

        def rows_in_dve(v):
            v.memset(head_rows, 1.0).then_inc(gain_rows_set, 1)
            for n in range(NTILE + 1):
                v.wait_ge(x_turned, n + 1)
                rows = P if n < NTILE else NS
                for b in range(2):
                    v.tensor_copy(hT[:, 4 * b:4 * b + 4, P * n:P * n + rows],
                                  acc[:, (2 * n + b) % 6, :].rearrange("p (c n) -> p c n", n=P)[:, :, 0:rows]) \
                        .then_inc(h_set, 1)
            v.wait_ge(gains_turned, 1)
            v.tensor_copy(head_g[:], aux[:, 1, 0:46]).then_inc(gains_set, 1)
            v.tensor_copy(norm_g[:].rearrange("p n k -> p (n k)"), aux[:, 1, 64:64 + 5 * KC]).then_inc(gains_set, 1)
            v.tensor_copy(sink[:], aux[0:2, 1, 128:128 + B_CHUNKS]).then_inc(gains_set, 1)
            for l in range(2):
                v.wait_ge(tab_turned, 3 * l + 1)
                v.tensor_copy(cw[:, l, :, :], aux[:, 0, 0:8 * FC].rearrange("p (t c) -> p t c", t=4)).then_inc(tab_set, 1)
                for half in range(2):
                    v.wait_ge(tab_turned, 3 * l + half + 2)
                    v.tensor_copy(st_T[:, l, 4 * half:4 * half + 4, :],
                                  aux[:, 1, 0:16 * FC].rearrange("p (s c) -> p s c", s=4)) \
                        .then_inc(tab_set, 1)

        def consts_dve(v):
            v.memset(eps[:], EPS).then_inc(const_set, 1)
            v.memset(sel_den[:], 0.0).then_inc(const_set, 1)
            v.wait_ge(ident_in, 16)
            v.wait_ge(const_in, CONSTS_IN)
            v.tensor_copy(masks[:].rearrange("p a m n -> p (a m n)"), mask_stage).then_inc(const_set, 1)
            v.tensor_copy(head_ops[:].rearrange("p a n -> p (a n)"), op_stage).then_inc(const_set, 1)
            v.tensor_copy(ident_b[:], ident).then_inc(const_set, 1)
            for h in range(2):
                v.tensor_scalar(sel[:, h, :], ones[0:2, :], cst[0:2, C_ID + h:C_ID + h + 1], None, ALU.mult) \
                    .then_inc(const_set, 1)
            v.wait_ge(gains_set, 3)
            v.tensor_scalar(sink8[:], sink[:], 1.0 / SCALE, None, ALU.mult).then_inc(const_set, 1)
            v.wait_ge(const_set, 8)
            for h in range(2):
                half = HD * (1 - h)
                v.tensor_copy(sel_den[:, h, half:half + HD], sel[:, h, half:half + HD].bitcast(F32)) \
                    .then_inc(const_set, 1)
            v.wait_ge(const_set, 10)
            v.tensor_scalar(sink_col[:], sink_col[:], 1.0 / SCALE, None, ALU.mult).then_inc(const_set, 1)

        CONSTS_SET = 11

        xf_n = carve(8 * T, T, T)[1:]
        sq_n0, sq_n1, sq_sum = carve(7000, T, T, T)[1:]
        sq_n = [sq_n0, sq_n1]
        STAT = {0: 0, 1: 1, 2: 2, 4: 3}

        def square_act(act, n, k, ready):
            ready(act)
            if k > 1:
                act.wait_ge(n_add, 7 * STAT[n] + k - 2)
            act.activation(sq_sum if k == 0 else sq_n[k % 2], hT[:, k, :], ACT.Square).then_inc(n_sq, 1)

        def square_dve(v, n, k):
            v.wait_ge(n_sq, 8 * STAT[n] + k + 1)
            if k:
                v.wait_ge(n_add, 7 * STAT[n] + k - 1)
                v.tensor_tensor(sq_sum, sq_sum, sq_n[k % 2], ALU.add).then_inc(n_add, 1)

        def norm_act(act, n):
            if n in STAT:
                act.wait_ge(n_mm, STAT[n] + 1)
                act.activation(thirds(rinv[:]), acc_set(0), ACT.Ln, bias=eps[:], scale=1.0 / D).then_inc(n_stat, 1)
                act.wait_ge(n_stat, 2 * STAT[n] + 1)
                act.activation(rinv[:], rinv[:], ACT.Exp, scale=-0.5).then_inc(n_stat, 1)
            for k in range(KC):
                act.wait_ge(n_x, 8 * n + k + 1)
                act.copy(xh[:, k, :], xf_n[k % 2]).then_inc(n_hi, 1)

        def norm_pe(pe, n):
            pe.wait_ge(n_add, 7 * STAT[n] + 7)
            for t in range(NT):
                mm = pe.matmul(acc_set(0)[:, t, :], ones, sq_sum[:, TH * t:TH * t + TH], start=True, stop=True)
            mm.then_inc(n_mm, 1)

        def norm_dve(v, n):
            if n in STAT:
                v.wait_ge(n_stat, 2 * STAT[n] + 2)
            def lo(k):
                v.wait_ge(n_hi, 8 * n + k + 1)
                v.tensor_tensor(xl[:, k, :], xf_n[k % 2], xh[:, k, :].bitcast(F32), ALU.subtract).then_inc(n_lo, 1)
            for k in range(KC):
                if k >= 2:
                    lo(k - 2)
                    v.wait_ge(n_lo, 8 * n + k - 1)
                v.scalar_tensor_tensor(xf_n[k % 2], hT[:, k, :], norm_g[:, n, k:k + 1], rinv[:],
                                       ALU.mult, ALU.mult).then_inc(n_x, 1)
            lo(KC - 2)
            lo(KC - 1)

        CH = 2
        CH_B = CH + A_CHUNKS
        Q_B = 24
        qg, sq_p, rr, ob0, ob1, t1b, t2b, lnb = carve(T, T, T, T, T, 2 * TH, 2 * TH, 2 * TH)
        outb = [ob0, ob1]
        sq_hi, qg_hi, sq_lo, qg_lo = f_hi[:, 0, :], f_hi[:, 1, :], f_lo[:, 0, :], f_lo[:, 1, :]

        def third(x, t):
            return x[:, TH * t:TH * t + TH]

        def counts_pe(pe):
            pe.sem_inc(w_used, RING)
            pe.sem_inc(third_full, 2 * CH)

        def counts_act(act):
            act.sem_inc(hi_ready, RING)
            act.sem_inc(acc_evac, 3 * CH)

        def proj_normed(pe, c, u0, n):
            pe.wait_ge(lo_ready, u0 + 1)
            pe.wait_ge(acc_evac, 3 * c - 3)
            for t, mm in enumerate(normed_product(pe, u0 % RING, n)):
                mm.then_inc(w_used if t == NT - 1 else third_full, 1)

        def proj_main(pe, c, k, u0, m, i, t):
            slot, u, _ = unit_at(u0, m, i)
            if t == 0:
                pe.wait_ge(lo_ready, u + 1)
                pe.wait_ge(acc_evac, 3 * c - 3)
            w1 = w_hi[:, slot, :].rearrange("p (k n) -> p k n", n=P)
            w2 = w_lo[:, slot, :].rearrange("p (k n) -> p k n", n=P)
            for j in range(KC):
                mm = product(pe, acc_set(k)[:, t, :], w1[:, j, :], w2[:, j, :], third(xh[:, j, :], t),
                             third(xl[:, j, :], t), j == 0, j == KC - 1)
            mm.then_inc(w_used if t == NT - 1 else third_full, 1)

        def proj_aux(pe, c, q, t):
            for bank, m, hi, lo, n, used, ready in (
                    (1, rot, qg_hi, qg_lo, 1, rot_used, rot_ready),
                    (0, blk, sq_hi, sq_lo, 2, ln_done, ssq_ready)):
                pe.wait_ge(aux_split, 2 * (3 * q + t) + n)
                pe.wait_ge(used, 3 * q + t)
                pe.matmul(aux[:, bank, 0:TH], m, third(hi, t), start=True, stop=False)
                pe.matmul(aux[:, bank, 0:TH], m, third(lo, t), start=False, stop=True) \
                    .then_inc(ready, 1)

        def proj_evac(act, c, k, u0, m, i, t, gain):
            _, u, _ = unit_at(u0, m, i)
            if t < NT - 1:
                act.wait_ge(third_full, 2 * c + t + 1)
            else:
                act.wait_ge(w_used, u + 1)
            act.wait_ge(chunk_out, 3 * c + t - 2)
            if gain is not None:
                act.activation(third(sq_p, t), acc_set(k)[:, t, :], ACT.Square)
                act.activation(third(qg, t), acc_set(k)[:, t, :], ACT.Copy, scale=gain).then_inc(acc_evac, 1)
                act.wait_ge(acc_evac, 3 * c + t + 1)
                act.copy(third(sq_hi, t), third(sq_p, t)).then_inc(sq_split, 1)
            else:
                act.copy(third(qg, t), acc_set(k)[:, t, :]).then_inc(acc_evac, 1)

        def proj_stat(act, q, t):
            s = third(lnb, t % 2)
            act.wait_ge(ssq_ready, 3 * q + t + 1)
            act.wait_ge(r_ready, 3 * q + t)
            act.activation(s, aux[:, 0, 0:TH], ACT.Ln, bias=eps[:], scale=1.0 / HD).then_inc(ln_done, 1)
            act.wait_ge(ln_done, 3 * q + t + 1)
            act.activation(third(rr, t), s, ACT.Exp, scale=-0.5).then_inc(r_ready, 1)

        def proj_split(v, c, q, t):
            n = 3 * q + t
            v.wait_ge(acc_evac, 3 * c + t + 1)
            v.tensor_copy(third(qg_hi, t), third(qg, t)).then_inc(qg_split, 1)
            v.wait_ge(qg_split, n + 1)
            v.tensor_tensor(third(qg_lo, t), third(qg, t), third(qg_hi, t).bitcast(F32), ALU.subtract) \
                .then_inc(aux_split, 1)
            v.wait_ge(sq_split, n + 1)
            v.tensor_tensor(third(sq_lo, t), third(sq_p, t), third(sq_hi, t).bitcast(F32), ALU.subtract) \
                .then_inc(aux_split, 1)

        def proj_dve(v, c, k, q, t):
            v.wait_ge(acc_evac, 3 * c + t + 1)
            if t == 0:
                v.wait_ge(stored[k], 8 * (c - k) - 16)
            if q is None:
                v.tensor_copy(third(outb[k], t), third(qg, t)).then_inc(chunk_out, 1)
                return
            n = 3 * q + t
            s1, s2 = third(t1b, t % 2), third(t2b, t % 2)
            v.wait_ge(chunk_out, 3 * c + t)
            v.tensor_tensor(s1, third(qg, t), third(rope[:, 0, :], t), ALU.mult).then_inc(qk_step, 1)
            v.wait_ge(rot_ready, 3 * q + t + 1)
            v.tensor_tensor(s2, aux[:, 1, 0:TH], third(rope[:, 1, :], t), ALU.mult).then_inc(rot_used, 1)
            v.wait_ge(qk_step, 2 * n + 1)
            v.wait_ge(rot_used, 3 * q + t + 1)
            v.tensor_tensor(s1, s1, s2, ALU.add).then_inc(qk_step, 1)
            v.wait_ge(qk_step, 2 * n + 2)
            v.wait_ge(r_ready, 3 * q + t + 1)
            v.tensor_tensor(third(outb[k], t), s1, third(rr, t), ALU.mult).then_inc(chunk_out, 1)

        def proj_a(eng, first, main, aux_of, aux_first):
            def step(one, other):
                for f in (other, one) if aux_first else (one, other):
                    f()
            first()
            with eng.Fori(0, 3) as i:
                for e in range(BODY):
                    for t in range(NT):
                        step(lambda: main(e + 1, BODY, i, t), lambda: aux_of(e, BODY, i, t))
            for n in range(3 * BODY + 1, A_CHUNKS):
                for t in range(NT):
                    step(lambda: main(n, 0, 0, t), lambda: aux_of(n - 1, 0, 0, t) if n <= 24 else None)

        def proj_a_pe(pe):
            proj_a(pe, lambda: proj_normed(pe, CH, U_QKV, 0),
                   lambda n, m, i, t: proj_main(pe, CH + n + m * i, n % 2, U_QKV + n, m, i, t),
                   lambda n, m, i, t: proj_aux(pe, CH + n + m * i, n + m * i, t), False)

        def proj_a_act(act):
            def main(n, m, i, t):
                if t == 0:
                    split_ahead(act, U_QKV + n, m, i)
                gain = None if m == 0 and n >= 24 else head_g[:, bass.ds(n + m * i, 1)] if m else head_g[:, n:n + 1]
                proj_evac(act, CH + n + m * i, n % 2, U_QKV + n, m, i, t, gain)
            proj_a(act, lambda: [main(0, 0, 0, t) for t in range(NT)], main, lambda n, m, i, t: proj_stat(act, n + m * i, t), True)

        def proj_a_dve(v):
            for t in range(2):
                proj_split(v, CH, 0, t)
            with v.Fori(0, 24 // BODY - 1) as i:
                for e in range(BODY):
                    for t in range(NT):
                        proj_dve(v, CH + e + BODY * i, e % 2, e + BODY * i, t)
                        f, tf = (e, 2) if t == 0 else (e + 1, t - 1)
                        proj_split(v, CH + f + BODY * i, f + BODY * i, tf)
            for n in range(24 - BODY, 24):
                for t in range(NT):
                    proj_dve(v, CH + n, n % 2, n, t)
                    f, tf = (n, 2) if t == 0 else (n + 1, t - 1)
                    if f < 24:
                        proj_split(v, CH + f, f, tf)
            with v.Fori(0, 12 // BODY) as i:
                for e in range(BODY):
                    for t in range(NT):
                        proj_dve(v, CH + 24 + e + BODY * i, e % 2, None, t)

        def store_chunk(sp, c, k, to):
            sp.wait_ge(chunk_out, 3 * c + 3)
            sp.dma_start(to, outb[k]).then_inc(stored[k], 16)

        def proj_a_sp(sp):
            with sp.Fori(0, A_CHUNKS // BODY - 1) as i:
                for e in range(BODY):
                    load(sp, wcols(w_in, e + 3 + BODY * i), U_QKV + 3 + e, BODY, i)
                    store_chunk(sp, CH + e + BODY * i, e % 2, scratch[e + BODY * i])
            for n in range(A_CHUNKS - BODY, A_CHUNKS):
                if n + 3 < A_CHUNKS:
                    load(sp, wcols(w_in, n + 3), U_QKV + n + 3)
                else:
                    load(sp, wcols(w_aout, n + 3 - A_CHUNKS, 2 * P), U_QKV + n + 3)
                store_chunk(sp, CH + n, n % 2, scratch[n])

        def proj_b_pe(pe):
            norm_pe(pe, 2)
            proj_normed(pe, CH_B, U_KV, 2)
            for t in range(NT):
                proj_main(pe, CH_B + 1, 1, U_KV + 1, 0, 0, t)
                proj_aux(pe, CH_B, Q_B, t)
            proj_normed(pe, CH_B + 2, U_BQ, 3)
            for n in range(1, B_CHUNKS):
                for t in range(NT):
                    proj_main(pe, CH_B + 2 + n, n % 2, U_BQ + n, 0, 0, t)
                    proj_aux(pe, CH_B + 1 + n, Q_B + n, t)
            for t in range(NT):
                proj_aux(pe, CH_B + 1 + B_CHUNKS, Q_B + B_CHUNKS, t)

        def proj_b_act(act):
            split_ahead(act, U_KV)
            for t in range(NT):
                proj_evac(act, CH_B, 0, U_KV, 0, 0, t, head_g[:, 36:37])
            split_ahead(act, U_KV + 1)
            for t in range(NT):
                proj_stat(act, Q_B, t)
                proj_evac(act, CH_B + 1, 1, U_KV + 1, 0, 0, t, None)
            act.wait_ge(w_used, U_BQ)
            norm_act(act, 3)
            for n in range(B_CHUNKS):
                split_ahead(act, U_BQ + n)
                for t in range(NT):
                    if n:
                        proj_stat(act, Q_B + n, t)
                    proj_evac(act, CH_B + 2 + n, n % 2, U_BQ + n, 0, 0, t, head_g[:, 38 + n:39 + n])
            for t in range(NT):
                proj_stat(act, Q_B + B_CHUNKS, t)

        def proj_b_dve(v):
            for t in range(NT):
                proj_split(v, CH_B, Q_B, t)
            for t in range(NT):
                proj_dve(v, CH_B, 0, Q_B, t)
            for t in range(NT):
                proj_dve(v, CH_B + 1, 1, None, t)
            norm_dve(v, 3)
            for t in range(2):
                proj_split(v, CH_B + 2, Q_B + 1, t)
            for n in range(B_CHUNKS):
                for t in range(NT):
                    proj_dve(v, CH_B + 2 + n, n % 2, Q_B + 1 + n, t)
                    f, tf = (n, 2) if t == 0 else (n + 1, t - 1)
                    if f < B_CHUNKS:
                        proj_split(v, CH_B + 2 + f, Q_B + 1 + f, tf)

        def proj_b_sp(sp):
            for n in range(2 + B_CHUNKS):
                if n + 3 < 2 + B_CHUNKS:
                    load(sp, wcols(w_q, n + 1), U_KV + n + 3)
                else:
                    load(sp, wcols(w_bout, n + 3 - 2 - B_CHUNKS), U_KV + n + 3)
                store_chunk(sp, CH_B + n, n % 2, scratch[A_CHUNKS + n])

        ADDED = {"a": 0, 0: KC, "b": KC + KC * FFN_TURNS, 1: 2 * KC + KC * FFN_TURNS}

        def out_main(pe, n, k, u0, half, kcs, last_of_unit):
            slot, u, _ = unit_at(u0)
            pe.wait_ge(lo_ready, u + 1)
            w1 = w_hi[:, slot, :].rearrange("p (k n) -> p k n", k=kcs)
            w2 = w_lo[:, slot, :].rearrange("p (k n) -> p k n", k=kcs)
            for t in range(NT):
                for j in range(kcs):
                    mm = product(pe, acc_set(k)[:, t, :], w1[:, j, P * half:P * half + P],
                                 w2[:, j, P * half:P * half + P], third(xh[:, j, :], t), third(xl[:, j, :], t),
                                 j == 0, j == kcs - 1)
            mm.then_inc(w_used if last_of_unit else res_full, 1)

        def add_to_h(v, n, k):
            v.tensor_tensor(thirds(hT[:, n, :]), thirds(hT[:, n, :]), acc_set(k), ALU.add).then_inc(h_added, 1)

        def aout_pe(pe):
            pe.wait_ge(ZA.fin, 1)
            for n in range(KC):
                if n >= 2:
                    pe.wait_ge(h_added, n - 1)
                out_main(pe, n, n % 2, U_AOUT + n // 2, n % 2, 4, n % 2 == 1)

        def aout_act(act):
            for n in range(4):
                split_ahead(act, U_AOUT + n)
                for k in (2 * n - 2, 2 * n - 1):
                    if k >= 0:
                        square_act(act, 1, k, lambda e: e.wait_ge(h_added, k + 1))
            for k in (KC - 2, KC - 1):
                square_act(act, 1, k, lambda e: e.wait_ge(h_added, k + 1))

        def aout_dve(v):
            for n in range(KC):
                if n % 2 == 0:
                    v.wait_ge(res_full, n // 2 + 1)
                else:
                    v.wait_ge(w_used, U_AOUT + n // 2 + 1)
                add_to_h(v, n, n % 2)
                if n:
                    square_dve(v, 1, n - 1)
            square_dve(v, 1, KC - 1)

        def bout_pe(pe):
            pe.wait_ge(ZB.fin, 1)
            for n in range(KC):
                if n >= 2:
                    pe.wait_ge(h_added, ADDED["b"] + n - 1)
                out_main(pe, n, n % 2, U_BOUT + n, 0, KC, True)

        def bout_act(act):
            for n in range(KC):
                split_ahead(act, U_BOUT + n)
                if n:
                    square_act(act, 4, n - 1, lambda e: e.wait_ge(h_added, ADDED["b"] + n))
            square_act(act, 4, KC - 1, lambda e: e.wait_ge(h_added, ADDED["b"] + KC))

        def bout_dve(v):
            for n in range(KC):
                v.wait_ge(w_used, U_BOUT + n + 1)
                add_to_h(v, n, n % 2)
                if n:
                    square_dve(v, 4, n - 1)
            square_dve(v, 4, KC - 1)

        U1 = T + 2
        ug, uv, cg, cv, ebuf, fbuf, tail_sb = carve(U1, U1, T, T, T, T, 640)
        GATE, VAL = 0, 1
        u_ext, c_out = [ug, uv], [cg, cv]
        UPS = 4 * FFN_TURNS
        CONV_STEPS = 4
        TURN_STEPS = 4 * CONV_STEPS
        LAST = FFN_TURNS - 1

        class Turn:
            def __init__(self, l, i, last):
                self.l, self.i, self.last = l, i, last
                self.m = 0 if last else 6
                self.off = 6 * i if last else 0
                self.ii = 0 if last else i
                self.unit0 = [U_FFN0, U_FFN1][l]
                self.up = UPS * l + 4 * i
                self.added = ADDED[l] + KC * i
                self.res = 4 + 7 * FFN_TURNS * l + 7 * i
                self.f = 2 * FFN_TURNS * l + 2 * i
                self.steps = TURN_STEPS * FFN_TURNS * l + CONV_STEPS + TURN_STEPS * i
                self.d0 = 4 if last else 5

            def unit(self, o):
                return self.unit0 + self.off + o, self.m, self.ii

            def no(self, o):
                return unit_at(*self.unit(o))[1]

        def turns(eng, l, body, *extra):
            with eng.Fori(0, LAST) as i:
                body(eng, Turn(l, i, False))
            body(eng, Turn(l, LAST, True))

        def up_pe(pe, unit, k):
            slot, u, _ = unit_at(*unit)
            pe.wait_ge(lo_ready, u + 1)
            w1 = w_hi[:, slot, :].rearrange("p (k n) -> p k n", n=P)
            w2 = w_lo[:, slot, :].rearrange("p (k n) -> p k n", n=P)
            for t in range(NT):
                for j in range(KC):
                    mm = product(pe, acc_set(k)[:, t, :], w1[:, j, :], w2[:, j, :], third(xh[:, j, :], t),
                                 third(xl[:, j, :], t), j == 0, j == KC - 1)
            mm.then_inc(w_used, 1)

        def ffn_turn_pe(pe, z):
            pe.wait_ge(h_added, z.added - 1)
            up_pe(pe, z.unit(1), 1)
            pe.wait_ge(h_added, z.added)
            pe.wait_ge(up_evac, z.up + 1)
            up_pe(pe, z.unit(2), 0)
            pe.wait_ge(up_evac, z.up + 2)
            up_pe(pe, z.unit(3), 1)
            if not z.last:
                pe.wait_ge(up_evac, z.up + 3)
                up_pe(pe, z.unit(4), 0)
            k0 = 0 if z.last else 1
            slots = [unit_at(*z.unit(z.d0 + e))[0] for e in range(2)]
            pe.wait_ge(lo_ready, z.no(z.d0 + 1) + 1)
            pe.wait_ge(flo_ready, z.f + 2)
            for n in range(KC):
                if n == 0:
                    pe.wait_ge(up_evac, z.up + (3 if z.last else 4))
                elif n == 1:
                    pe.wait_ge(up_evac, z.up + (4 if z.last else 5))
                else:
                    pe.wait_ge(h_added, z.added + n - 1)
                for t in range(NT):
                    for e, s in enumerate(slots):
                        mm = product(pe, acc_set(k0 + n)[:, t, :], w_hi[:, s, P * n:P * n + P],
                                     w_lo[:, s, P * n:P * n + P], third(f_hi[:, e, :], t),
                                     third(f_lo[:, e, :], t), e == 0, e == 1)
                        if n == KC - 1 and t == NT - 1:
                            mm.then_inc(w_used, 1)
                if n < KC - 1:
                    mm.then_inc(res_full, 1)

        def ffn_pe(pe, l):
            norm_pe(pe, 1 + 3 * l)
            u0 = [U_FFN0, U_FFN1][l]
            pe.wait_ge(lo_ready, u0 + 1)
            *_, mm = normed_product(pe, u0 % RING, 1 + 3 * l)
            mm.then_inc(w_used, 1)
            turns(pe, l, ffn_turn_pe)
            pe.wait_ge(conv_out, UPS * (l + 1))
            pe.wait_ge(tail_set, 2 * l)
            for s in range(5):
                mm = pe.transpose(aux[0:4 * FC, s // 4, P * (s % 4):P * (s % 4) + P],
                                  u_tail[:, 2 * s:2 * s + 2, :].rearrange("p a c -> p (a c)"), ident)
            mm.then_inc(tail_turned, 1)

        def up_evac_act(act, z, o, which, k):
            split_ahead(act, *z.unit(o))
            act.wait_ge(w_used, z.no(o) + 1)
            act.wait_ge(conv_out, z.up + o - 1)
            act.copy(thirds(u_ext[which][:, 2:U1]), acc_set(k)).then_inc(up_evac, 1)

        def gate_act(act, z, e):
            act.wait_ge(conv_out, z.up + 2 * e + 1)
            act.wait_ge(f_raw, z.f + e)
            act.activation(ebuf, cg, ACT.Silu).then_inc(e_ready, 1)
            act.wait_ge(f_raw, z.f + e + 1)
            act.wait_ge(w_used, z.no(1))
            act.copy(f_hi[:, e, :], fbuf).then_inc(fhi_ready, 1)

        def ffn_turn_act(act, z):
            up_evac_act(act, z, 1, VAL, 1)
            gate_act(act, z, 0)
            up_evac_act(act, z, 2, GATE, 0)
            up_evac_act(act, z, 3, VAL, 1)
            gate_act(act, z, 1)
            if not z.last:
                up_evac_act(act, z, 4, GATE, 0)
            split_ahead(act, *z.unit(z.d0))
            if z.last and z.l == 0:
                for k in range(KC):
                    square_act(act, 2, k, lambda e: e.wait_ge(h_added, ADDED["b"] - KC + k + 1))
            split_ahead(act, *z.unit(z.d0 + 1))

        def ffn_act(act, l):
            norm_act(act, 1 + 3 * l)
            act.preload_act_table_set("silu_and_others")
            u0 = [U_FFN0, U_FFN1][l]
            split_ahead(act, u0)
            act.wait_ge(w_used, u0 + 1)
            act.copy(thirds(u_ext[GATE][:, 2:U1]), acc_set(0)).then_inc(up_evac, 1)
            turns(act, l, ffn_turn_act)
            if l == 0:
                act.preload_act_table_set("natural_log_exp_and_others")

        def conv_dve(v, l, n, which, ch, s, products):
            u, c = u_ext[which], c_out[which]
            w = [cw[:, l, t, bass.ds(ch, 1)] for t in range(4)]
            state = [st_T[:, l, :, bass.ds(ch + 2 * FC * t, 1)] for t in range(2)]
            cs = c[:, SEQ:T].unsqueeze(2)
            v.wait_ge(up_evac, n + 1)
            v.wait_ge(f_raw, products)
            v.tensor_scalar(c[:, 0:T], u[:, 2:U1], w[2], w[3], ALU.mult, ALU.add).then_inc(conv_step, 1)
            v.tensor_copy(u_tail[:, :, bass.ds(ch, 1)], u[:, SEQ:U1].unsqueeze(2))
            v.wait_ge(conv_step, s + 1)
            v.scalar_tensor_tensor(c[:, 0:SEQ], u[:, 1:SEQ + 1], w[1], c[:, 0:SEQ], ALU.mult, ALU.add) \
                .then_inc(conv_step, 1)
            v.scalar_tensor_tensor(cs, state[1], w[1], cs, ALU.mult, ALU.add).then_inc(conv_step, 1)
            v.wait_ge(conv_step, s + 2)
            v.scalar_tensor_tensor(c[:, 0:SEQ], u[:, 0:SEQ], w[0], c[:, 0:SEQ], ALU.mult, ALU.add) \
                .then_inc(conv_step, 1)
            v.wait_ge(conv_step, s + 3)
            v.scalar_tensor_tensor(cs, state[0], w[0], cs, ALU.mult, ALU.add).then_inc(conv_out, 1)

        def gated_dve(v, z, e):
            v.wait_ge(conv_out, z.up + 2 * e + 2)
            v.wait_ge(e_ready, z.f + e + 1)
            v.wait_ge(flo_ready, z.f + e)
            v.tensor_tensor(fbuf, cv, ebuf, ALU.mult).then_inc(f_raw, 1)
            v.wait_ge(fhi_ready, z.f + e + 1)
            v.tensor_tensor(f_lo[:, e, :], fbuf, f_hi[:, e, :].bitcast(F32), ALU.subtract).then_inc(flo_ready, 1)

        def ffn_turn_dve(v, z):
            s, l, g = z.steps, z.l, 2 * z.i
            conv_dve(v, l, z.up + 1, VAL, FC + g, s, z.f)
            gated_dve(v, z, 0)
            s += CONV_STEPS
            conv_dve(v, l, z.up + 2, GATE, g + 1, s, z.f + 1)
            conv_dve(v, l, z.up + 3, VAL, FC + g + 1, s + CONV_STEPS, z.f + 1)
            gated_dve(v, z, 1)
            s += 2 * CONV_STEPS
            if not z.last:
                conv_dve(v, l, z.up + 4, GATE, g + 2, s, z.f + 2)
            k0 = 0 if z.last else 1
            for n in range(KC):
                if n < KC - 1:
                    v.wait_ge(res_full, z.res + n + 1)
                else:
                    v.wait_ge(w_used, z.no(z.d0 + 1) + 1)
                add_to_h(v, n, k0 + n)
                if z.last and l == 0 and n:
                    square_dve(v, 2, n - 1)
            if z.last and l == 0:
                square_dve(v, 2, KC - 1)

        def ffn_dve(v, l):
            norm_dve(v, 1 + 3 * l)
            v.wait_ge(n_lo, 8 * (1 + 3 * l) + KC)
            for n in range(2):
                v.memset(u_ext[n][:, 0:2], 0.0).then_inc(chain, 1)
            v.wait_ge(chain, 2 * (l + 1))
            conv_dve(v, l, UPS * l, GATE, 0, TURN_STEPS * FFN_TURNS * l, 2 * FFN_TURNS * l)
            turns(v, l, ffn_turn_dve)
            v.wait_ge(tail_turned, l + 1)
            v.wait_ge(tail_out, 16 * TAILS * l)
            v.tensor_copy(tail_sb[0:4 * FC, 0:512], aux[0:4 * FC, 0, :]).then_inc(tail_set, 1)
            v.tensor_copy(tail_sb[0:4 * FC, 512:640], aux[0:4 * FC, 1, 0:P]).then_inc(tail_set, 1)

        TAILS = 1 + NS
        up_w = [a["ffn_w_up"][l] for l in range(2)]

        def down_unit(l, c):
            return a["ffn_w_down"][l].rearrange("(c p) (k n) -> c p k n", p=P, k=1)[c]

        CACHE_PIECES = (A_PAIRS, B_CHUNKS, 2 * FFN_TURNS + 1)
        ROW = 8 * HD
        caches = [a["cache_a_kv_w128"], a["cache_a_kv_w512"], a["cache_a_kv_w2048"]]
        out_caches = [outs["a_w128_sample"], outs["a_w512_sample"], outs["a_w2048_sample"]]

        def copy_piece(sp, g, n):
            kept, pieces = (GROUPS[g][0] - 1) * ROW, CACHE_PIECES[g]
            src = caches[g][0].rearrange("s x w h d -> (s x) (w h d)")[:, ROW:]
            dst = out_caches[g][0].rearrange("s x w h d -> (s x) (w h d)")[:, 0:kept]
            sp.dma_start(dst.rearrange("r (n e) -> r n e", n=pieces)[:, n, :],
                         src.rearrange("r (n e) -> r n e", n=pieces)[:, n, :]).then_inc(copied, 16)

        def ffn_turn_sp(sp, z):
            l, g = z.l, 2 * z.i
            load(sp, wcols(up_w[l], g + FC), *z.unit(1))
            load(sp, wcols(up_w[l], g + 1), *z.unit(2))
            load(sp, wcols(up_w[l], g + 1 + FC), *z.unit(3))
            copy_piece(sp, 2, FFN_TURNS * l + z.i)
            if not z.last:
                load(sp, wcols(up_w[l], g + 2), *z.unit(4))
            for e in range(2):
                load(sp, down_unit(l, g + e), *z.unit(z.d0 + e))

        def ffn_sp(sp, l):
            load(sp, wcols(up_w[l], 0), [U_FFN0, U_FFN1][l])
            turns(sp, l, ffn_turn_sp)

        def tails_sp(sp, l):
            sp.wait_ge(tail_set, 2 * l + 2)
            sp.dma_start(outs["ffn_conv_prompt"][l, 0].rearrange("t (c f) -> (t c) f", f=P),
                         tail_sb[0:4 * FC, 0:P]).then_inc(tail_out, 16)
            for s in range(NS):
                r = 2 * FC * (s % 2)
                sp.dma_start(outs["ffn_conv_sample"][l, s, 1].rearrange("(c f) -> c f", f=P),
                             tail_sb[r:r + 2 * FC, P * (1 + s // 2):P * (2 + s // 2)]).then_inc(tail_out, 16)

        EXPORTS = [(0, 7, 1), (1, 4, 4), (2, 0, 4), (2, 4, 4)]

        class Buffers:
            def __init__(self, M):
                if M.ng > 1:
                    vt, pt, self.mrow, bm, self.stg, self.o_raw = carve(
                        24 * 192, 3 * 512, SEQ, 2 * M.cols, 4 * 512, SEQ)
                    self.q = [[x[:, 4 + g, 0:SEQ].bitcast(F32) for x in (xh, xl)] for g in range(NG)]
                    self.k = [x.bitcast(F32) for x in (f_hi[:, 0, 0:SEQ], f_hi[:, 1, 0:SEQ], f_lo[:, 0, 0:SEQ])]
                    self.v = [x.bitcast(F32) for x in (xh[:, 7, 0:SEQ], xl[:, 7, 0:SEQ], f_lo[:, 1, 0:SEQ])]
                    self.padded = [self.q[g][h] for g in range(NG) for h in range(2)]
                else:
                    q0, q1, k0, k1, vt, pt, self.mrow, bm, self.o_raw, self.e_row = carve(
                        SEQ, SEQ, SEQ, SEQ, 8 * 192, 3 * 512, SEQ, 2 * M.cols, SEQ, SEQ)
                    self.q, self.k, self.v = [q0, q1], [k0, k1], [f_hi[:, 0, 0:SEQ].bitcast(F32)]
                    self.padded = self.k
                self.ng = M.ng
                self.vt = vt.rearrange("p (t c) -> p t c", c=192)
                self.pt = pt
                self.bm = bm.rearrange("p (h c) -> p h c", h=2)
                self.o = self.mrow

            def queries(self, g, hh, slot):
                return self.q[g][hh] if self.ng > 1 else self.q[slot]

            def keys(self, g, hh):
                return self.k[g] if self.ng > 1 else self.k[hh]

        BUF = {id(M): Buffers(M) for M in (MA, MB)}

        def moves(M):
            vt = [("t", g, t, 4) for g in range(M.ng) for t in (0, 4)]
            if M.ng == 1:
                return vt
            return vt + [("v", *e) for e in EXPORTS] + [("k", *e) for e in EXPORTS]

        def moves_pe(pe, M, S, it, r):
            B, nb, NM = BUF[id(M)], len(M.batches), len(moves(M))
            pe.wait_ge(S.v_in, 16 * (3 if M.ng > 1 else 2) * (r + 1))
            for n, (what, g, t0, cnt) in enumerate(moves(M)):
                if n < 6:
                    pe.wait_ge(S.sc_exp, 2 * nb * it)
                else:
                    pe.wait_ge(S.copied, NM * r + n - 5)
                if what == "k":
                    pe.wait_ge(S.q_in[g], 48 * (r + 1))
                src = B.k[g] if what == "k" else B.v[g]
                for e in range(cnt):
                    x = tile_tokens(src, g, t0 + e) if what == "t" else src[:, P * (t0 + e):P * (t0 + e) + P]
                    mm = pe.transpose(acc[:, n % 6, P * e:P * e + P], x, ident)
                mm.then_inc(S.moved, 1)

        def moves_dve(v_, M, S, it, r):
            B, nb, NM = BUF[id(M)], len(M.batches), len(moves(M))
            for n, (what, g, t0, cnt) in enumerate(moves(M)):
                v_.wait_ge(S.moved, NM * r + n + 1)
                if what == "t":
                    v_.wait_ge(S.pv, PV0[id(M)] + 2 * nb * it)
                    v_.tensor_copy(B.vt[:, 8 * g + t0:8 * g + t0 + 4, :]
                                   .rearrange("p t (a b) -> p t a b", b=HD)[:, :, 0:3:2, :],
                                   acc[:, n % 6, :].rearrange("p (t a b) -> p t a b", t=4, a=2)).then_inc(S.copied, 1)
                else:
                    v_.wait_ge(S.exported, 64 * (2 * r + (what == "k")))
                    s = [e[0:2] for e in EXPORTS].index((g, t0))
                    v_.tensor_copy(B.stg[:, 512 * s:512 * s + P * cnt], acc[:, n % 6, 0:P * cnt]).then_inc(S.copied, 1)

        def attn_pe(pe, M, S, it, r, slot=0):
            B, nb, NM = BUF[id(M)], len(M.batches), len(moves(M))
            if M.ng == 1:
                pe.wait_ge(S.k_in, 32 * (r + 1))
                pe.wait_ge(S.q_in[slot], 8 * (it - slot) + 16)
            for hh in range(2):
                for b, (g, kind, blocks) in enumerate(M.batches):
                    n = nb * hh + b
                    if n < 6:
                        pe.wait_ge(S.copied, NM * (r + 1))
                        pe.wait_ge(S.sc_exp, 2 * nb * it)
                    else:
                        pe.wait_ge(S.maxed, 2 * nb * it + n - 5)
                    w = len(blocks) * P
                    pe.matmul(acc[:, n % 6, 0:w], ident_b[:],
                              masks[:, 0, kind, :].unsqueeze(1).to_broadcast([P, len(blocks), P]),
                              start=True, stop=False)
                    for e, (tq, tk, _) in enumerate(blocks):
                        mm = pe.matmul(acc[:, n % 6, P * e:P * e + P], tile_tokens(B.queries(g, hh, slot), g, tq),
                                       tile_tokens(B.keys(g, hh), g, tk), start=False, stop=e == len(blocks) - 1)
                    mm.then_inc(S.scored, 1)
            pe.wait_ge(S.merged, it + 1)
            for g in range(M.ng):
                for t in range(NTILE):
                    mm = pe.transpose(acc[0:2, 2 * g + t // 4, P * (t % 4):P * (t % 4) + P],
                                      B.bm[:, :, 8 * g + t], ident)
                mm.then_inc(S.turned, 1)

            def scores(n):
                hh, b = divmod(n, nb)
                g, kind, blocks = M.batches[b]
                if n < 6:
                    pe.wait_ge(S.shift, it + 1)
                else:
                    pe.wait_ge(S.sc_exp, 2 * nb * it + n - 5)
                w = len(blocks) * P
                pe.matmul(acc[:, n % 6, 0:w], ident_b[:],
                          masks[:, 1, kind, :].unsqueeze(1).to_broadcast([P, len(blocks), P]),
                          start=True, stop=False)
                pe.matmul(acc[:, n % 6, 0:w], sel[:, hh, :], batch_tokens(neg_max[:, :], g, kind, blocks),
                          start=False, stop=False)
                for e, (tq, tk, _) in enumerate(blocks):
                    mm = pe.matmul(acc[:, n % 6, P * e:P * e + P], tile_tokens(B.keys(g, hh), g, tk),
                                   tile_tokens(B.queries(g, hh, slot), g, tq), start=False,
                                   stop=e == len(blocks) - 1)
                mm.then_inc(S.sc_full, 1)

            def values(n):
                hh, b = divmod(n, nb)
                g, kind, blocks = M.batches[b]
                pe.wait_ge(S.sc_exp, 2 * nb * it + n + 1)
                if b == 0:
                    pe.wait_ge(S.o_out, 2 * it + hh)
                o = aux[:, :, :].rearrange("p a n -> p (a n)")
                vc = slice(HD * hh, HD * hh + P)
                probs = B.pt[:, 512 * (n % 3):512 * (n % 3) + 512]
                if M.ng == 1 and b == nb - 1:
                    for half in range(2):
                        pe.matmul(aux[:, half, :], sel_den[:, hh, :], B.e_row[0:2, 512 * half:512 * half + 512],
                                  start=False, stop=False, skip_group_check=True)
                for e, (tq, tk, _) in enumerate(blocks):
                    pe_ = probs[:, P * e:P * e + P]
                    kw = dict(start=b < 2 and e == 0, stop=b == nb - 1, skip_group_check=True)
                    if g < 2:
                        mm = pe.matmul(tile_tokens(o, g, tq), B.vt[:, 8 * g + tk, vc], pe_, **kw)
                    else:
                        for half in range(0, P, HD):
                            mm = pe.matmul(tile_tokens(o, g, tq)[:, half:half + HD], B.vt[:, 8 * g + tk, vc],
                                           pe_[:, half:half + HD], **kw)
                mm.then_inc(S.pv, 1)

            scores(0)
            for n in range(1, 2 * nb):
                scores(n)
                values(n - 1)
            values(2 * nb - 1)

        def head_rows_of(hh):
            return slice(HD * hh, HD * hh + HD), slice(HD * (1 - hh), HD * (1 - hh) + HD)

        def attn_act(act, M, S, it):
            B, nb, pv0 = BUF[id(M)], len(M.batches), PV0[id(M)]
            if M.ng == 1:
                act.wait_ge(S.shift, it + 1)
                act.wait_ge(S.pv, pv0 + 2 * nb * it)
                act.activation(B.e_row[0:2, :], neg_max[:, :].bitcast(F32), ACT.Exp, bias=sink_now[:],
                               scale=SCALE)

            def reciprocals(hh):
                rows, den = head_rows_of(hh)
                act.wait_ge(S.o_out, 2 * it + hh + 1)
                act.activation(rinv[rows, 0:SEQ], B.o_raw[den, :], ACT.Ln).then_inc(S.o_ln, 1)
                act.wait_ge(S.o_ln, 2 * it + hh + 1)
                act.activation(rinv[rows, 0:SEQ], rinv[rows, 0:SEQ], ACT.Exp, scale=-1.0).then_inc(S.o_rec, 1)

            for n in range(2 * nb):
                w = len(M.batches[n % nb][2]) * P
                act.wait_ge(S.sc_full, 2 * nb * it + n + 1)
                act.wait_ge(S.pv, pv0 + 2 * nb * it + max(0, n - 2))
                act.activation(B.pt[:, 512 * (n % 3):512 * (n % 3) + w], acc[:, n % 6, 0:w], ACT.Exp, scale=SCALE) \
                    .then_inc(S.sc_exp, 1)
                if n == nb + 1:
                    reciprocals(0)
            reciprocals(1)
            act.wait_ge(S.o_norm, 2 * it + 2)
            act.copy(xh[:, it, 0:SEQ], B.o).then_inc(S.o_hi, 1)

        def attn_pool(pool, M, S, it):
            B = BUF[id(M)]
            for hh in range(2):
                rows, _ = head_rows_of(hh)
                pool.wait_ge(S.o_rec, 2 * it + hh + 1)
                if hh == 0:
                    pool.wait_ge(S.o_lo, it)
                pool.tensor_tensor(B.o[rows, :], B.o_raw[rows, :], rinv[rows, 0:SEQ], ALU.mult).then_inc(S.o_norm, 1)
            pool.wait_ge(S.o_hi, it + 1)
            pool.sem_inc(S.o_go, 1)
            pool.tensor_tensor(xl[:, it, 0:SEQ], B.o, xh[:, it, 0:SEQ].bitcast(F32), ALU.subtract).then_inc(S.o_lo, 1)

        def clear_dve(v_, M, S):
            B = BUF[id(M)]
            for n, x in enumerate(B.padded):
                other = HD * (1 - n % 2)
                v_.memset(x[other:other + HD, :], 0.0)
            v_.memset(B.vt[:, :, HD:2 * HD], 1.0).then_inc(S.cleared, 1)

        def attn_dve(v_, M, S, it):
            B, nb, pv0 = BUF[id(M)], len(M.batches), PV0[id(M)]
            bm = B.bm
            for hh in range(2):
                for b, (g, kind, blocks) in enumerate(M.batches):
                    n = nb * hh + b
                    c0 = blocks[0][2]
                    v_.wait_ge(S.scored, 2 * nb * it + n + 1)
                    if n == 0:
                        v_.wait_ge(S.turned, M.ng * it)
                    v_.tensor_reduce(bm[:, hh, c0:c0 + len(blocks)],
                                     acc[:, n % 6, 0:P * len(blocks)].rearrange("p (e n) -> p e n", n=P),
                                     AX_X, ALU.max).then_inc(S.maxed, 1)
            v_.wait_ge(S.maxed, 2 * nb * (it + 1))
            c1 = 8 * M.ng
            if M.ng > 1:
                v_.tensor_tensor(bm[:, :, 9:16:2], bm[:, :, 9:16:2], bm[:, :, c1 + 7:c1 + 11], ALU.max)
            v_.tensor_tensor(bm[:, :, 1:8], bm[:, :, 1:8], bm[:, :, c1:c1 + 7], ALU.max).then_inc(S.merged, 1)
            m = B.mrow[0:2, :]
            NR = M.ng + (M.ng == 1)
            for g in range(M.ng):
                v_.wait_ge(S.turned, M.ng * it + g + 1)
                src = acc[0:2, 2 * g:2 * g + 2, :].rearrange("p a n -> p (a n)")
                if g == 0:
                    v_.wait_ge(S.o_lo, it)
                    v_.tensor_copy(m, src).then_inc(S.rowed, 1)
                else:
                    v_.wait_ge(S.rowed, NR * it + g)
                    st = 4 * g
                    mv_ = m.rearrange("p (n s) -> p s n", s=st)
                    v_.tensor_tensor(mv_, mv_, src.rearrange("p (s n) -> p s n", s=st), ALU.max).then_inc(S.rowed, 1)
            if M.ng == 1:
                v_.wait_ge(S.rowed, NR * it + 1)
                v_.wait_ge(S.pv, pv0 + 2 * nb * it)
                v_.tensor_copy(sink_now[:], sink[:, bass.ds(it, 1)])
                v_.tensor_scalar(m, m, sink8[:, bass.ds(it, 1)], None, ALU.max).then_inc(S.rowed, 1)
            v_.wait_ge(S.rowed, NR * (it + 1))
            v_.wait_ge(S.pv, pv0 + 2 * nb * it)
            v_.tensor_scalar(neg_max[:, :], m, -1.0, None, ALU.mult).then_inc(S.shift, 1)
            for hh in range(2):
                v_.wait_ge(S.pv, pv0 + 2 * nb * it + nb * (hh + 1))
                v_.wait_ge(S.o_norm, 2 * it + hh)
                v_.tensor_copy(B.o_raw, aux[:, :, :].rearrange("p a n -> p (a n)")).then_inc(S.o_out, 1)

        def attn_a_sp(sp, i):
            B, S, M = BUF[id(MA)], SA, MA
            nb, NM = len(M.batches), len(moves(M))
            chunk = lambda w, g: scratch[12 * w + 4 * g:12 * w + 4 * g + 4].rearrange("c p t -> p c t")[:, i, 0:SEQ]
            for g in range(NG):
                sp.dma_start(B.v[g], chunk(2, g)).then_inc(S.v_in, 16)
            sp.wait_ge(S.pv, 2 * nb * i)
            for g in range(NG):
                sp.dma_start(B.k[g], chunk(1, g)).then_inc(S.q_in[g], 16)
                for h in range(2):
                    sp.dma_start(B.q[g][h][HD * h:HD * h + HD, :], chunk(0, g)[HD * h:HD * h + HD, :]) \
                        .then_inc(S.q_in[g], 16)
            outs_g = [outs["a_w128_prompt"], outs["a_w512_prompt"], outs["a_w2048_prompt"]]
            for w in (1, 0):
                for s, (g, t0, cnt) in enumerate(EXPORTS):
                    sp.wait_ge(S.copied, NM * i + 10 - 4 * w + s + 1)
                    sp.sem_inc(S.seen, 1)
                    kept = min(GROUPS[g][0], SEQ)
                    first = t0 - (SEQ - kept) // P
                    dst = outs_g[g][0, 0, w].rearrange("(t p) (j h) d -> p t j (h d)", p=P, j=A_PAIRS)
                    sp.dma_start(dst[:, first:first + cnt, i, :],
                                 B.stg[:, 512 * s:512 * s + P * cnt].rearrange("p (t c) -> p t c", c=P)) \
                        .then_inc(S.exported, 16)
            copy_piece(sp, 0, i)

        PAIRS_KV = B_CHUNKS // 2

        def attn_b_sp(sp, kv):
            B, S, nb = BUF[id(MB)], SB, len(MB.batches)
            sp.wait_ge(S.pv, PV0[id(MB)] + 2 * nb * PAIRS_KV * kv)
            rows = scratch[A_CHUNKS:A_CHUNKS + 2, HD * kv:HD * kv + HD, 0:SEQ]
            for half in (0, HD):
                sp.dma_start(B.v[0][half:half + HD, :], rows[1]).then_inc(S.v_in, 16)
            for h in range(2):
                sp.dma_start(B.k[h][HD * h:HD * h + HD, :], rows[0]).then_inc(S.k_in, 16)
            qs = scratch[A_CHUNKS + 2 + PAIRS_KV * kv:A_CHUNKS + 2 + PAIRS_KV * (kv + 1)].rearrange("(i e) p t -> p e i t", e=2)
            with sp.Fori(0, PAIRS_KV // 2) as i:
                for e in range(2):
                    sp.wait_ge(S.pv, 2 * nb * (PAIRS_KV * kv + 2 * i + e))
                    sp.dma_start(B.q[e], qs[:, e, i, 0:SEQ]).then_inc(S.q_in[e], 16)
                    copy_piece(sp, 1, PAIRS_KV * kv + 2 * i + e)

        CROW = A_PAIRS * P
        s_ring, s_kt, s_kvn, s_stc, s_all, s_pT, s_cols, s_qb, s_prod, s_dg, s_D, s_red, s_of = carve(
            4 * 1024, 2 * 512, 24 * P, 192, 387, 192, 36 * NS, 192, 96, 192, 192, 8, 32)
        s_ring = s_ring.rearrange("p (r a n) -> p r a n", r=4, a=2)
        s_cols = s_cols.rearrange("p (c s) -> p c s", s=NS)
        s_qb = s_qb.rearrange("p (c s h) -> p c s h", s=NS, h=2)
        STEPS_A = NG * NS // 2

        def sample_a_sp(sp):
            nb = len(MA.batches)
            sp.wait_ge(SA.pv, 2 * nb * A_PAIRS)
            sp.wait_ge(SA.exported, 16 * 8 * A_PAIRS)
            sp.wait_ge(SA.o_lo, A_PAIRS)
            sp.dma_start(s_cols, scratch[0:A_CHUNKS, :, SEQ:T].rearrange("c p t -> p c t")).then_inc(ZA.cols, 16)
            for n in range(2 * STEPS_A):
                w, (g, s2) = n // STEPS_A, divmod(n % STEPS_A, NS // 2)
                if 4 <= n < STEPS_A + 4:
                    sp.wait_ge(ZA.moved, 2 * (n - 4) + 2 + 6)
                elif n >= STEPS_A + 4:
                    sp.wait_ge(ZA.pe, n - STEPS_A - 3)
                src = caches[g][0, 2 * s2:2 * s2 + 2, w].rearrange("s (n d) h e -> n d s (h e)", d=GROUPS[g][1])
                sp.dma_start(s_ring[:, n % 4, :, :], src[:, 0]).then_inc(ZA.cache[n % 4], 16)
                if n == 4:
                    sp.wait_ge(ZA.kt, 6)
                    for w2 in range(2):
                        for g2 in range(NG):
                            W = GROUPS[g2][0]
                            sp.dma_start(out_caches[g2][0, :, w2, W - 1].rearrange("s h d -> s (h d)"),
                                         s_kvn[0:NS, CROW * (3 * w2 + g2):CROW * (3 * w2 + g2) + CROW]) \
                                .then_inc(ZA.out, 16)

        def sample_a_pe(pe):
            nb = len(MA.batches)
            pe.wait_ge(SA.sc_exp, 2 * nb * A_PAIRS)
            pe.wait_ge(SA.o_out, 2 * A_PAIRS)
            pe.wait_ge(ZA.cols, 16)
            for b in range(6):
                for e in range(4):
                    mm = pe.transpose(acc[0:NS, b, P * e:P * e + P], s_cols[:, 12 + 4 * b + e, :], ident)
                mm.then_inc(ZA.moved, 1)
            pe.wait_ge(ZA.prep, 4)
            for g in range(NG):
                for h in range(2):
                    mm = pe.matmul(aux[32 * h:32 * h + 32, 1, g:g + 1],
                                   s_prod[HD * h:HD * h + HD, 32 * g:32 * g + 32], ones[HD * h:HD * h + HD, 0:1],
                                   start=True, stop=True)
            pe.wait_ge(ZA.kt, 6)

            def turn(m):
                n, e = divmod(m, 2)
                if e == 0:
                    pe.wait_ge(ZA.cache[n % 4], 16 * (n // 4 + 1))
                if m >= 4:
                    pe.wait_ge(ZA.kt, m - 3 + 6)
                for c in range(4):
                    mm = pe.transpose(acc[:, m % 4, P * c:P * c + P], s_ring[:, n % 4, e, P * c:P * c + P], ident)
                mm.then_inc(ZA.moved, 1)

            def score(m):
                n, e = divmod(m, 2)
                g, s2 = divmod(n, NS // 2)
                s = 2 * s2 + e
                pe.wait_ge(ZA.kt, m + 1 + 6)
                for c in range(4):
                    at0 = 64 * g + 8 * c + s
                    mm = pe.matmul(aux[:, 0, at0:at0 + 33:32], s_kt[:, 512 * (m % 2) + P * c:512 * (m % 2) + P * c + P],
                                   s_qb[:, 4 * g + c, s, :], start=True, stop=True)
                mm.then_inc(ZA.scored, 1)

            turn(0)
            for m in range(1, 2 * STEPS_A):
                turn(m)
                score(m - 1)
            score(2 * STEPS_A - 1)
            pe.wait_ge(ZA.step, 1)
            for g in range(NG):
                mm = pe.transpose(acc[0:64, 0, P * g:P * g + P], s_stc[:, 64 * g:64 * g + 64], ident)
            mm.then_inc(ZA.moved, 1)
            pe.wait_ge(ZA.step, 9)
            for g in range(NG):
                pe.transpose(acc[:, 1, 64 * g:64 * g + 64], s_all[0:64, P * g:P * g + P], ident[0:64, 0:64])
            pe.matmul(acc[0:NS, 2, 0:192], cst[0:64, C_E64:C_E64 + NS], s_dg[0:64, :], start=True, stop=True) \
                .then_inc(ZA.moved, 1)
            pe.wait_ge(ZA.step, 11)
            for n in range(STEPS_A):
                g, s2 = divmod(n, NS // 2)
                r = STEPS_A + n
                pe.wait_ge(ZA.cache[r % 4], 16 * (r // 4 + 1))
                for e in range(2):
                    s = 2 * s2 + e
                    for c in range(4):
                        mm = pe.matmul(acc[:, 3, 16 * c + 2 * s:16 * c + 2 * s + 2],
                                       s_ring[:, r % 4, e, P * c:P * c + P],
                                       s_pT[:, 64 * g + 8 * c + s:64 * g + 8 * c + s + 33:32],
                                       start=(n == 0 and e == 0 and c == 0), stop=False, skip_group_check=True)
                mm.then_inc(ZA.pe, 1)
            for g in range(NG):
                for c in range(4):
                    mm = pe.matmul(acc[:, 3, 16 * c:16 * c + 16].rearrange("p (s h) -> p s h", h=2),
                                   s_kvn[0:NS, CROW * (3 + g) + P * c:CROW * (3 + g) + P * c + P],
                                   s_D[0:NS, 64 * g:64 * g + 64].rearrange("p (h c s) -> p c s h", h=2, c=4)[:, c],
                                   start=False, stop=True, skip_group_check=True)
            mm.then_inc(ZA.pe, 1)

        def sample_a_dve(v):
            v.wait_ge(ZA.cols, 16)
            v.memset(s_qb, 0.0).then_inc(ZA.prep, 1)
            v.tensor_tensor(s_prod.rearrange("p (c s) -> p c s", s=NS), s_cols[:, 0:12, :], s_cols[:, 12:24, :],
                            ALU.mult).then_inc(ZA.prep, 1)
            v.wait_ge(ZA.prep, 1)
            for h in range(2):
                v.tensor_copy(s_qb[HD * h:HD * h + HD, :, :, h], s_cols[HD * h:HD * h + HD, 0:12, :]) \
                    .then_inc(ZA.prep, 1)
            for b in range(6):
                v.wait_ge(ZA.moved, b + 1)
                v.tensor_copy(s_kvn[0:NS, 512 * b:512 * b + 512], acc[0:NS, b, :]).then_inc(ZA.kt, 1)
            for m in range(2 * STEPS_A):
                v.wait_ge(ZA.moved, m + 1 + 6)
                if m >= 2:
                    v.wait_ge(ZA.scored, m - 1)
                v.tensor_copy(s_kt[:, 512 * (m % 2):512 * (m % 2) + 512], acc[:, m % 4, :]).then_inc(ZA.kt, 1)
            v.wait_ge(ZA.scored, 2 * STEPS_A)
            v.tensor_copy(s_stc, aux[:, 0, 0:192]).then_inc(ZA.step, 1)
            v.wait_ge(ZA.moved, 2 * STEPS_A + 7)
            v.tensor_copy(s_all[0:64, 0:384], acc[0:64, 0, 0:384]).then_inc(ZA.step, 1)
            v.tensor_copy(s_all[0:64, 384:387], aux[0:64, 1, 0:NG]).then_inc(ZA.step, 1)
            v.wait_ge(ZA.step, 3)
            v.tensor_reduce(s_red[0:64, 0:1], s_all[0:64, :], AX_X, ALU.max).then_inc(ZA.step, 1)
            v.wait_ge(ZA.step, 4)
            v.tensor_scalar(s_red[0:64, 1:2], s_red[0:64, 0:1], -SCALE, None, ALU.mult).then_inc(ZA.step, 1)
            v.wait_ge(ZA.act, 1)
            v.reciprocal(s_red[0:64, 3:4], s_red[0:64, 2:3]).then_inc(ZA.step, 1)
            v.wait_ge(ZA.step, 6)
            v.tensor_scalar(s_all[0:64, :], s_all[0:64, :], s_red[0:64, 3:4], None, ALU.mult).then_inc(ZA.step, 1)
            v.wait_ge(ZA.step, 7)
            for g in range(NG):
                ins = v.tensor_scalar(s_dg[0:64, 64 * g:64 * g + 64], ident[0:64, 0:64],
                                      s_all[0:64, 384 + g:385 + g], None, ALU.mult)
                if g:
                    ins.then_inc(ZA.step, 1)
            v.wait_ge(ZA.moved, 2 * STEPS_A + 8)
            v.tensor_copy(s_pT, acc[:, 1, 0:192]).then_inc(ZA.step, 1)
            v.tensor_copy(s_D[0:NS, :], acc[0:NS, 2, 0:192]).then_inc(ZA.step, 1)
            v.wait_ge(ZA.pe, STEPS_A + 1)
            for h in range(2):
                v.tensor_copy(s_of[HD * h:HD * h + HD, :],
                              acc[HD * h:HD * h + HD, 3, 0:64].rearrange("p (n h) -> p n h", h=2)[:, :, h]) \
                    .then_inc(ZA.step, 1)
            v.wait_ge(ZA.step, 13)
            v.wait_ge(ZA.act, 2)
            v.tensor_tensor(xl[:, 0:4, SEQ:T], s_of.rearrange("p (c s) -> p c s", s=NS),
                            xh[:, 0:4, SEQ:T].bitcast(F32), ALU.subtract).then_inc(ZA.fin, 1)

        def sample_a_act(act):
            act.wait_ge(ZA.step, 5)
            act.activation(s_all[0:64, :], s_all[0:64, :], ACT.Exp, bias=s_red[0:64, 1:2], scale=SCALE,
                           accum_out=s_red[0:64, 2:3]).then_inc(ZA.act, 1)
            act.wait_ge(ZA.step, 13)
            act.copy(xh[:, 0:4, SEQ:T], s_of.rearrange("p (c s) -> p c s", s=NS)).then_inc(ZA.act, 1)

        NH = 2 * B_CHUNKS
        b_k, b_v, b_kt, b_cols, b_qb, b_prod, b_stc, b_all, b_pT, b_dg, b_D, b_kvn, b_red, b_of, b_new, b_rows = carve(
            NS * P, NS * P, NS * P, 10 * NS, P, P, P, 130, P, P, P, 256, 8, 64, 256, 256)
        b_cols = b_cols.rearrange("p (c s) -> p c s", s=NS)
        b_qb = b_qb.rearrange("p (h s) -> p h s", s=NS)
        b_of = b_of.rearrange("p (c s) -> p c s", s=NS)

        def sample_b_sp(sp):
            nb = len(MB.batches)
            sp.wait_ge(SB.pv, PV0[id(MB)] + 2 * nb * B_CHUNKS)
            sp.wait_ge(SB.o_lo, B_CHUNKS)
            sp.dma_start(b_cols, scratch[A_CHUNKS:46, :, SEQ:T].rearrange("c p t -> p c t")).then_inc(ZB.cols, 16)
            sp.dma_start(b_new.rearrange("p (c t) -> p c t", c=2),
                         scratch[A_CHUNKS:A_CHUNKS + 2, :, SEQ - P:SEQ].rearrange("c p t -> p c t")) \
                .then_inc(ZB.cols, 16)
            for w, x in enumerate((b_k, b_v)):
                sp.dma_start(x.rearrange("p (s c) -> p s c", s=NS),
                             a["cache_b_kv"][:, w].rearrange("s w h d -> w s (h d)")).then_inc(ZB.cache[w], 16)
            sp.wait_ge(ZB.kt, 2)
            for w in range(2):
                sp.dma_start(outs["b_kv_sample"][:, w, P - 1].rearrange("s h d -> s (h d)"),
                             b_kvn[0:NS, P * w:P * w + P]).then_inc(ZB.out, 16)
                sp.dma_start(outs["b_kv_prompt"][0, w].rearrange("t h d -> t (h d)"),
                             b_rows[:, P * w:P * w + P]).then_inc(ZB.out, 16)

        def sample_b_pe(pe):
            nb = len(MB.batches)
            pe.wait_ge(SB.sc_exp, 2 * nb * B_CHUNKS)
            pe.wait_ge(SB.o_out, 2 * B_CHUNKS)
            pe.wait_ge(ZB.cols, 32)
            for w in range(2):
                mm = pe.transpose(acc[0:NS, 5, P * w:P * w + P], b_cols[:, w, :], ident)
            mm.then_inc(ZB.moved, 1)
            for w in range(2):
                mm = pe.transpose(acc[:, 4, P * w:P * w + P], b_new[:, P * w:P * w + P], ident)
            mm.then_inc(ZB.moved, 1)
            pe.wait_ge(ZB.cache[0], 16)
            for s in range(NS):
                mm = pe.transpose(acc[:, s // 4, P * (s % 4):P * (s % 4) + P], b_k[:, P * s:P * s + P], ident)
            mm.then_inc(ZB.moved, 1)
            pe.wait_ge(ZB.prep, 6)
            pe.matmul(aux[:, 1, 0:1], b_prod, ones[:, 0:1], start=True, stop=True)
            pe.wait_ge(ZB.kt, 4)
            for s in range(NS):
                mm = pe.matmul(aux[:, 0, s:s + 8 * (NH - 1) + 1:8], b_kt[:, P * s:P * s + P], b_qb[:, :, s],
                               start=True, stop=True)
            mm.then_inc(ZB.scored, 1)
            pe.wait_ge(ZB.step, 1)
            pe.transpose(acc[:, 2, 0:P], b_stc, ident).then_inc(ZB.moved, 1)
            pe.wait_ge(ZB.step, 10)
            pe.transpose(acc[:, 3, 0:P], b_all[:, 0:P], ident)
            pe.matmul(acc[0:NS, 1, 0:P], cst[:, C_E128:C_E128 + NS], b_dg, start=True, stop=True).then_inc(ZB.moved, 1)
            pe.wait_ge(ZB.step, 12)
            pe.wait_ge(ZB.cache[1], 16)
            for s in range(NS):
                pe.matmul(acc[:, 0, s:s + 8 * (NH - 1) + 1:8], b_v[:, P * s:P * s + P],
                          b_pT[:, s:s + 8 * (NH - 1) + 1:8], start=(s == 0), stop=False, skip_group_check=True)
            pe.matmul(acc[:, 0, 0:P], b_kvn[0:NS, P:2 * P], b_D[0:NS, :], start=False, stop=True,
                      skip_group_check=True).then_inc(ZB.pe, 1)

        def sample_b_dve(v):
            v.wait_ge(ZB.cols, 32)
            v.memset(b_qb, 0.0).then_inc(ZB.prep, 1)
            v.wait_ge(ZB.prep, 1)
            for kv in range(2):
                for h in range(2):
                    v.tensor_copy(b_qb[HD * kv:HD * kv + HD, 8 * kv + h:8 * kv + 8:2, :],
                                  b_cols[HD * h:HD * h + HD, 2 + 4 * kv:6 + 4 * kv, :]).then_inc(ZB.prep, 1)
            v.wait_ge(ZB.prep, 5)
            v.tensor_tensor(b_prod.rearrange("p (h s) -> p h s", s=NS), b_qb,
                            b_cols[:, 0, :].unsqueeze(1).to_broadcast([P, NH, NS]), ALU.mult).then_inc(ZB.prep, 1)
            v.wait_ge(ZB.moved, 1)
            v.tensor_copy(b_kvn[0:NS, :], acc[0:NS, 5, 0:256]).then_inc(ZB.kt, 1)
            v.wait_ge(ZB.moved, 2)
            v.tensor_copy(b_rows, acc[:, 4, 0:256]).then_inc(ZB.kt, 1)
            v.wait_ge(ZB.moved, 3)
            for half in range(2):
                v.tensor_copy(b_kt[:, 512 * half:512 * half + 512], acc[:, half, :]).then_inc(ZB.kt, 1)
            v.wait_ge(ZB.scored, 1)
            v.tensor_copy(b_stc, aux[:, 0, 0:P]).then_inc(ZB.step, 1)
            v.wait_ge(ZB.moved, 4)
            v.tensor_copy(b_all[:, 0:P], acc[:, 2, 0:P]).then_inc(ZB.step, 1)
            v.tensor_copy(b_all[:, P:P + 1], aux[:, 1, 0:1]).then_inc(ZB.step, 1)
            v.tensor_copy(b_all[:, P + 1:P + 2], sink_col[:]).then_inc(ZB.step, 1)
            v.wait_ge(ZB.step, 2)
            v.memset(b_all[:, 0:1], MASKED).then_inc(ZB.step, 1)
            v.wait_ge(ZB.step, 5)
            v.tensor_reduce(b_red[:, 0:1], b_all, AX_X, ALU.max).then_inc(ZB.step, 1)
            v.wait_ge(ZB.step, 6)
            v.tensor_scalar(b_red[:, 1:2], b_red[:, 0:1], -SCALE, None, ALU.mult).then_inc(ZB.step, 1)
            v.wait_ge(ZB.act, 1)
            v.reciprocal(b_red[:, 3:4], b_red[:, 2:3]).then_inc(ZB.step, 1)
            v.wait_ge(ZB.step, 8)
            v.tensor_scalar(b_all, b_all, b_red[:, 3:4], None, ALU.mult).then_inc(ZB.step, 1)
            v.wait_ge(ZB.step, 9)
            v.tensor_scalar(b_dg, ident, b_all[:, P:P + 1], None, ALU.mult).then_inc(ZB.step, 1)
            v.wait_ge(ZB.moved, 5)
            v.tensor_copy(b_pT, acc[:, 3, 0:P]).then_inc(ZB.step, 1)
            v.tensor_copy(b_D[0:NS, :], acc[0:NS, 1, 0:P]).then_inc(ZB.step, 1)
            v.wait_ge(ZB.pe, 1)
            for kv in range(2):
                for h in range(2):
                    v.tensor_copy(b_of[HD * h:HD * h + HD, 4 * kv:4 * kv + 4, :],
                                  acc[HD * kv:HD * kv + HD, 0, 0:P].rearrange("p (h s) -> p h s", s=NS)
                                  [:, 8 * kv + h:8 * kv + 8:2, :]).then_inc(ZB.step, 1)
            v.wait_ge(ZB.step, 16)
            v.wait_ge(ZB.act, 2)
            v.tensor_tensor(xl[:, :, SEQ:T], b_of, xh[:, :, SEQ:T].bitcast(F32), ALU.subtract).then_inc(ZB.fin, 1)

        def sample_b_act(act):
            act.wait_ge(ZB.step, 7)
            act.activation(b_all, b_all, ACT.Exp, bias=b_red[:, 1:2], scale=SCALE,
                           accum_out=b_red[:, 2:3]).then_inc(ZB.act, 1)
            act.wait_ge(ZB.step, 16)
            act.copy(xh[:, :, SEQ:T], b_of).then_inc(ZB.act, 1)

        yp = outs["y_prompt"].rearrange("b s d -> (b s) d")
        ys = outs["y_sample"].rearrange("b s d -> (b s) d")

        def rows_out_pe(pe):
            pe.wait_ge(h_added, ADDED[1] + KC * FFN_TURNS)
            for n in range(NTILE + 1):
                rows = P if n < NTILE else NS
                if n >= 3:
                    pe.wait_ge(y_set, 2 * (n - 3) + 2)
                for c in range(KC):
                    mm = pe.transpose(acc[0:rows, (2 * n + c // 4) % 6, P * (c % 4):P * (c % 4) + P],
                                      hT[:, c, P * n:P * n + rows], ident)
                mm.then_inc(y_turned, 1)

        def rows_out_dve(v):
            for n in range(NTILE + 1):
                rows = P if n < NTILE else NS
                v.wait_ge(y_turned, n + 1)
                if n >= 2:
                    v.wait_ge(y_out[n % 2], 16 * (n // 2))
                for b in range(2):
                    v.tensor_copy(y_stage[n % 2][0:rows, 512 * b:512 * b + 512], acc[0:rows, (2 * n + b) % 6, :]) \
                        .then_inc(y_set, 1)

        def rows_out_sp(sp):
            for n in range(NTILE + 1):
                sp.wait_ge(y_set, 2 * n + 2)
                if n < NTILE:
                    sp.dma_start(yp[P * n:P * n + P, :], y_stage[n % 2]).then_inc(y_out[n % 2], 16)
                else:
                    sp.dma_start(ys, y_stage[n % 2][0:NS]).then_inc(y_out[n % 2], 16)

        def copies_sp(sp):
            copy_piece(sp, 2, CACHE_PIECES[2] - 1)
            sp.dma_start(outs["b_kv_sample"][:, :, 0:P - 1].rearrange("s x w h d -> (s x) (w h d)"),
                         a["cache_b_kv"][:, :, 1:P].rearrange("s x w h d -> (s x) (w h d)")).then_inc(copied, 16)
            for l in range(2):
                sp.dma_start(outs["ffn_conv_sample"][l, :, 0], a["state_ffn_conv"][l, :, 1]).then_inc(copied, 16)
        COPIES = sum(CACHE_PIECES) + 1 + 2

        block = ctx.enter_context(nc.Block())

        @block.sync
        def _(sp):
            rows_in_sp(sp)
            tables_sp(sp)
            proj_a_sp(sp)
            for k in range(2):
                sp.wait_ge(stored[k], 16 * A_CHUNKS // 2)
            with sp.Fori(0, A_PAIRS) as i:
                attn_a_sp(sp, i)
            sample_a_sp(sp)
            load(sp, wcols(w_aout, 3, 2 * P), U_AOUT + 3)
            ffn_sp(sp, 0)
            for n in range(3):
                load(sp, wcols([a["b_w_kv"], a["b_w_kv"], w_q][n], [0, 1, 0][n]), U_KV + n)
            tails_sp(sp, 0)
            proj_b_sp(sp)
            for k in range(2):
                sp.wait_ge(stored[k], 16 * 46 // 2)
            for kv in range(2):
                attn_b_sp(sp, kv)
            sample_b_sp(sp)
            for n in range(3, KC):
                load(sp, wcols(w_bout, n), U_BOUT + n)
            copies_sp(sp)
            ffn_sp(sp, 1)
            tails_sp(sp, 1)
            rows_out_sp(sp)
            sp.wait_ge(y_out[0], 16 * 5)
            sp.wait_ge(y_out[1], 16 * 4)
            sp.wait_ge(tail_out, 16 * TAILS * 2)
            sp.wait_ge(ZA.out, 16 * 6)
            sp.wait_ge(ZB.out, 16 * 4)
            sp.wait_ge(SA.exported, 16 * 8 * A_PAIRS)
            sp.wait_ge(copied, 16 * COPIES)

        @block.gpsimd
        def _(pool):
            pool.sem_inc(lo_ready, RING)
            units_pool(pool, U_QKV, U_AOUT + 2)
            with pool.Fori(0, A_PAIRS) as i:
                attn_pool(pool, MA, SA, i)
            units_pool(pool, U_AOUT + 2, U_BOUT + 2)
            with pool.Fori(0, B_CHUNKS) as i:
                attn_pool(pool, MB, SB, i)
            units_pool(pool, U_BOUT + 2, U_END)

        @block.scalar
        def _(act):
            act.preload_act_table_set("natural_log_exp_and_others")
            counts_act(act)
            split_hi(act, U_QKV)
            split_hi(act, U_QKV + 1)
            act.wait_ge(const_set, CONSTS_SET)
            act.wait_ge(tab_set, 6)
            for k in range(KC):
                square_act(act, 0, k, lambda e: e.wait_ge(h_set, 2 * (NTILE + 1)))
            norm_act(act, 0)
            proj_a_act(act)
            with act.Fori(0, A_PAIRS) as i:
                attn_act(act, MA, SA, i)
            sample_a_act(act)
            aout_act(act)
            ffn_act(act, 0)
            norm_act(act, 2)
            act.wait_ge(tail_out, 16 * TAILS)
            proj_b_act(act)
            with act.Fori(0, B_CHUNKS) as i:
                attn_act(act, MB, SB, i)
            sample_b_act(act)
            bout_act(act)
            ffn_act(act, 1)

        @block.vector
        def _(v):
            v.sem_inc(chunk_out, 3 * CH)
            rows_in_dve(v)
            consts_dve(v)
            for k in range(KC):
                square_dve(v, 0, k)
            norm_dve(v, 0)
            proj_a_dve(v)
            for k in range(2):
                v.wait_ge(stored[k], 16 * A_CHUNKS // 2)
            clear_dve(v, MA, SA)
            with v.Fori(0, A_PAIRS) as i:
                moves_dve(v, MA, SA, i, i)
                attn_dve(v, MA, SA, i)
            sample_a_dve(v)
            aout_dve(v)
            ffn_dve(v, 0)
            norm_dve(v, 2)
            proj_b_dve(v)
            for k in range(2):
                v.wait_ge(stored[k], 16 * 46 // 2)
            clear_dve(v, MB, SB)
            for kv in range(2):
                moves_dve(v, MB, SB, PAIRS_KV * kv, kv)
                with v.Fori(0, PAIRS_KV) as i:
                    attn_dve(v, MB, SB, PAIRS_KV * kv + i)
            sample_b_dve(v)
            bout_dve(v)
            ffn_dve(v, 1)
            rows_out_dve(v)

        @block.tensor
        def _(pe):
            counts_pe(pe)
            rows_in_pe(pe)
            pe.wait_ge(const_set, CONSTS_SET)
            norm_pe(pe, 0)
            proj_a_pe(pe)
            pe.wait_ge(chunk_out, 3 * CH_B)
            pe.wait_ge(SA.cleared, 1)
            with pe.Fori(0, A_PAIRS) as i:
                moves_pe(pe, MA, SA, i, i)
                attn_pe(pe, MA, SA, i, i)
            sample_a_pe(pe)
            aout_pe(pe)
            ffn_pe(pe, 0)
            proj_b_pe(pe)
            pe.wait_ge(chunk_out, 3 * (CH_B + 2 + B_CHUNKS))
            pe.wait_ge(SB.cleared, 1)
            pe.sem_inc(SB.pv, PV0[id(MB)])
            for kv in range(2):
                moves_pe(pe, MB, SB, PAIRS_KV * kv, kv)
                with pe.Fori(0, PAIRS_KV // 2) as i:
                    for e in range(2):
                        attn_pe(pe, MB, SB, PAIRS_KV * kv + 2 * i + e, kv, slot=e)
            sample_b_pe(pe)
            bout_pe(pe)
            ffn_pe(pe, 1)
            rows_out_pe(pe)


INPUTS = ["x_prompt", "x_sample", "cache_a_kv_w128", "cache_a_kv_w512", "cache_a_kv_w2048", "cache_b_kv",
          "state_ffn_conv", "attn_norm_g", "ffn_norm_g", "a_w_in", "a_q_norm_g", "a_k_norm_g", "a_w_out",
          "b_kv_norm_g", "b_w_kv", "b_k_norm_g", "b_w_q", "b_q_norm_g", "b_sinks", "b_w_out",
          "ffn_w_up", "ffn_conv_w", "ffn_conv_b", "ffn_w_down"]
OUTPUTS = [
    ("y_prompt", (1, SEQ, D)), ("y_sample", (NS, 1, D)),
    ("a_w128_prompt", (1, 1, 2, 128, 8, HD)), ("a_w128_sample", (1, NS, 2, 128, 8, HD)),
    ("a_w512_prompt", (1, 1, 2, 512, 8, HD)), ("a_w512_sample", (1, NS, 2, 512, 8, HD)),
    ("a_w2048_prompt", (1, 1, 2, SEQ, 8, HD)), ("a_w2048_sample", (1, NS, 2, 2048, 8, HD)),
    ("b_kv_prompt", (1, 2, 128, 2, HD)), ("b_kv_sample", (NS, 2, 128, 2, HD)),
    ("ffn_conv_prompt", (2, 1, 2, 2 * DFF)), ("ffn_conv_sample", (2, NS, 2, 2 * DFF)),
]


def kernel(**inputs):
    import concourse.bacc as bacc
    from concourse.bass_utils import run_bass_kernel_spmd

    nc = bacc.Bacc("TRN2", target_bir_lowering=False, num_devices=1, dynamic_dma_scratch_size=1024)
    arrays, a, outs = {}, {}, {}
    for name in INPUTS:
        arrays["in_" + name] = np.ascontiguousarray(inputs[name])
    arrays["in_consts"] = shape_constants()
    for name, x in arrays.items():
        a[name[3:]] = nc.dram_tensor(name, x.shape, F32, kind="ExternalInput").ap()
    for name, shape in OUTPUTS:
        outs[name] = nc.dram_tensor("out_" + name, shape, F32, kind="ExternalOutput").ap()
    build(nc, a, outs)
    r = run_bass_kernel_spmd(nc, [arrays], core_ids=[0])
    return tuple(r.results[0]["out_" + name] for name, _ in OUTPUTS)
```

```python
from contextlib import ExitStack

import numpy as np

import concourse.bass as bass
from concourse import mybir

F32 = mybir.dt.float32
F32R = mybir.dt.float32r
BF16 = mybir.dt.bfloat16
ALU = mybir.AluOpType
ACT = mybir.ActivationFunctionType
AX_X = mybir.AxisListType.X

P = 128
D = 1024
KC = D // P
SEQ = 1024
NS = 8
T = SEQ + NS
NT = 3
TH = T // NT
HD = 64
DFF = 2816
FC = DFF // P
PAST = 4096
GROUPS = ((128, 1), (512, 4), (2048, 16))
NG = len(GROUPS)
A_PAIRS = 4
B_CHUNKS = 8
EPS = 1e-6
SCALE = HD ** -0.5
MASKED = -1e30
RING = 3
BODY = 6
A_CHUNKS = 36
NTILE = SEQ // P

U_QKV = RING
U_AOUT = U_QKV + A_CHUNKS
U_FFN0 = U_AOUT + 8
FFN_TURNS = FC // 2
FFN_UNITS = 6 * FFN_TURNS
U_KV = U_FFN0 + FFN_UNITS
U_BQ = U_KV + 2
U_BOUT = U_BQ + B_CHUNKS
U_FFN1 = U_BOUT + 8
U_END = U_FFN1 + FFN_UNITS

C_ID, C_ONES, C_E64, C_E128, C_BLK, C_ROT = 0, 128, 256, 264, 272, 400
C_MQ, C_MK = 528, 1040
C_COS, C_SIN = 1552, 1552 + T
C_END = C_SIN + T
CUR, PREV_A, BOTH, PREV_B = range(4)


def shape_constants():
    c = np.zeros((P, C_END), np.float32)
    i = np.arange(P)
    c[:, C_ID:C_ID + P] = np.eye(P)
    c[:, C_ONES:C_ONES + P] = 1.0
    c[:, C_BLK:C_BLK + P] = i[:, None] // HD == i[None, :] // HD
    for m in range(P):
        half = m % HD < HD // 2
        c[m + HD // 2 if half else m - HD // 2, C_ROT + m] = -1.0 if half else 1.0
    c[:, C_E64:C_E64 + NS] = i[:, None] % NS == np.arange(NS)
    c[:, C_E128:C_E128 + NS] = i[:, None] % NS == np.arange(NS)
    q, k = i[:, None], i[None, :]
    valid = [k <= q, k >= q, (k <= q) & (k % 2 == q % 2), k > q]
    for n, v in enumerate(valid):
        m = np.where(v, 0.0, MASKED)
        c[:, C_MQ + n * P:C_MQ + (n + 1) * P] = m
        c[:, C_MK + n * P:C_MK + (n + 1) * P] = m.T
    pos = np.concatenate([np.arange(SEQ), np.full(NS, PAST)]).astype(np.float32)
    inv = (10000.0 ** (-np.arange(HD // 2) / (HD // 2))).astype(np.float32)
    ang = (pos[None, :] * inv[i % (HD // 2), None]).astype(np.float32)
    c[:, C_COS:C_COS + T] = np.cos(ang.astype(np.float64))
    c[:, C_SIN:C_SIN + T] = np.sin(ang.astype(np.float64))
    return c


class Mixer:

    def __init__(self, groups):
        self.ng = groups
        b = []
        prev = PREV_A if groups > 1 else PREV_B
        cols = 8 * groups
        for g in range(groups):
            kind = BOTH if g == 2 else CUR
            for t in (0, 4):
                b.append((g, kind, [(t + e, t + e, 8 * g + t + e) for e in range(4)]))
        b.append((0, prev, [(t, t - 1, cols + t - 1) for t in range(1, 5)]))
        b.append((0, prev, [(t, t - 1, cols + t - 1) for t in range(5, 8)]))
        if groups > 1:
            b.append((1, prev, [(2 * r + 1, 2 * r, cols + 7 + r) for r in range(4)]))
        self.batches = b
        self.cols = cols + 7 + (4 if groups > 1 else 0)


def tile_tokens(x, g, tile):
    if g == 0:
        return x[:, P * tile:P * tile + P]
    if g == 1:
        r, b = divmod(tile, 2)
        return x.rearrange("p (n s) -> p s n", s=4)[:, r, P * b:P * b + P]
    return x.rearrange("p (n s) -> p s n", s=8)[:, tile, :]


def batch_tokens(x, g, kind, blocks):
    t0 = blocks[0][0]
    if g == 0:
        return x[:, P * t0:P * (t0 + len(blocks))]
    if g == 1:
        s = x.rearrange("p (n s) -> p s n", s=4)
        return s[:, 0:4, P:2 * P] if kind == PREV_A else s[:, t0 // 2:t0 // 2 + 2, :]
    return x.rearrange("p (n s) -> p s n", s=8)[:, t0:t0 + 4, :]


def build(nc, a, outs):
    with ExitStack() as ctx:
        def sb(name, shape, dt=F32):
            return ctx.enter_context(nc.sbuf_tensor(name, shape, dt))

        def sem(name):
            return ctx.enter_context(nc.semaphore(name))

        hT = sb("hT", [P, KC, T])
        xh = sb("xh", [P, KC, T], F32R)
        xl = sb("xl", [P, KC, T], F32R)
        w_raw = sb("w_raw", [P, RING, 1024])
        w_hi = sb("w_hi", [P, RING, 1024], F32R)
        w_lo = sb("w_lo", [P, RING, 1024], F32R)
        f_hi = sb("f_hi", [P, 2, T], F32R)
        f_lo = sb("f_lo", [P, 2, T], F32R)
        cst = sb("cst", [P, C_BLK])
        head_ops = sb("head_ops", [P, 2, P], F32R)
        rope = sb("rope", [P, 2, T])
        masks = sb("masks", [P, 2, 4, P], BF16)
        ident_b = sb("ident_b", [P, P], BF16)
        sel = sb("sel", [2, 2, P], F32R)
        sel_den = sb("sel_den", [2, 2, P])
        neg_max = sb("neg_max", [2, SEQ], F32R)
        rinv = sb("rinv", [P, T])
        norm_g = sb("norm_g", [P, 5, KC])
        head_g = sb("head_g", [P, 46])
        eps = sb("eps", [P, 1])
        cw = sb("cw", [P, 2, 4, 2 * FC])
        st_T = sb("st_T", [P, 2, NS, 4 * FC])
        u_tail = sb("u_tail", [P, 10, 2 * FC])
        sink8 = sb("sink8", [2, B_CHUNKS])
        sink = sb("sink", [2, B_CHUNKS])
        sink_now = sb("sink_now", [2, 1])
        sink_col = sb("sink_col", [P, 1])
        ARENA = 10800
        arena = sb("arena", [P, ARENA])
        acc = ctx.enter_context(nc.psum_tensor("acc", [P, 6, 512], F32))
        aux = ctx.enter_context(nc.psum_tensor("aux", [P, 2, 512], F32))

        ident = cst[:, C_ID:C_ID + P]
        ones = cst[:, C_ONES:C_ONES + P]
        blk, rot = head_ops[:, 0, :], head_ops[:, 1, :]

        def carve(*sizes):
            at, views = 0, []
            for s in sizes:
                views.append(arena[:, at:at + s])
                at += s
            assert at <= ARENA, at
            return views

        scratch = nc.dram_tensor("scratch", [46, P, T], F32).ap()

        ident_in = sem("ident_in")
        const_in = sem("const_in")
        const_set = sem("const_set")
        x_in = [sem(f"x_in{i}") for i in range(4)]
        x_turned = sem("x_turned")
        h_set = sem("h_set")
        tab_in = sem("tab_in")
        conv_in = sem("conv_in")
        gain_rows_set = sem("gain_rows_set")
        gains_turned = sem("gains_turned")
        gains_set = sem("gains_set")
        tab_turned = sem("tab_turned")
        tab_set = sem("tab_set")
        w_landed = [sem(f"w_landed{i}") for i in range(RING)]
        hi_ready = sem("hi_ready")
        lo_ready = sem("lo_ready")
        w_used = sem("w_used")
        n_sq = sem("n_sq")
        n_mm = sem("n_mm")
        n_stat = sem("n_stat")
        n_add = sem("n_add")
        n_x = sem("n_x")
        n_hi = sem("n_hi")
        n_lo = sem("n_lo")
        n_lo_odd = sem("n_lo_odd")
        third_full = sem("third_full")
        acc_evac = sem("acc_evac")
        sq_split = sem("sq_split")
        qg_split = sem("qg_split")
        aux_split = sem("aux_split")
        ssq_ready = sem("ssq_ready")
        rot_ready = sem("rot_ready")
        ln_done = sem("ln_done")
        r_ready = sem("r_ready")
        rot_used = sem("rot_used")
        qk_step = sem("qk_step")
        chunk_out = sem("chunk_out")
        stored = [sem(f"stored{i}") for i in range(2)]
        res_full = sem("res_full")
        h_added = sem("h_added")
        first_full = sem("first_full")
        first_added = sem("first_added")
        up_evac = sem("up_evac")
        conv_step = sem("conv_step")
        conv_out = sem("conv_out")
        e_ready = sem("e_ready")
        f_raw = sem("f_raw")
        fhi_ready = sem("fhi_ready")
        flo_ready = sem("flo_ready")
        tail_turned = sem("tail_turned")
        tail_set = sem("tail_set")
        tail_out = sem("tail_out")
        y_turned = sem("y_turned")
        y_set = sem("y_set")
        y_out = [sem(f"y_out{i}") for i in range(2)]
        copied = sem("copied")
        chain = sem("chain")

        class Attn:
            def __init__(self, p, first):
                self.v_in = sem(f"{p}_v_in")
                self.k_in = sem(f"{p}_k_in")
                self.q_in = [sem(f"{p}_q_in{i}") for i in range(NG if first else 2)]
                self.cleared = sem(f"{p}_cleared")
                self.moved = sem(f"{p}_moved")
                self.copied = sem(f"{p}_copied")
                self.scored = sem(f"{p}_scored")
                self.maxed = sem(f"{p}_maxed")
                self.merged = sem(f"{p}_merged")
                self.turned = sem(f"{p}_turned")
                self.rowed = sem(f"{p}_rowed")
                self.shift = sem(f"{p}_shift")
                self.sc_full = sem(f"{p}_sc_full")
                self.sc_exp = sem(f"{p}_sc_exp")
                self.pv = sem(f"{p}_pv")
                self.o_out = sem(f"{p}_o_out")
                self.o_ln = sem(f"{p}_o_ln")
                self.o_rec = sem(f"{p}_o_rec")
                self.o_norm = sem(f"{p}_o_norm")
                self.o_hi = sem(f"{p}_o_hi")
                self.o_go = sem(f"{p}_o_go")
                if first:
                    self.exported = sem(f"{p}_exported")
                    self.seen = sem(f"{p}_seen")
                self.o_lo = sem(f"{p}_o_lo")
        SA, SB = Attn("a", True), Attn("b", False)

        class Sample:
            def __init__(self, p, slots):
                self.cols = sem(f"{p}_cols")
                self.cache = [sem(f"{p}_cache{i}") for i in range(slots)]
                self.prep = sem(f"{p}_prep")
                self.moved = sem(f"{p}_moved")
                self.kt = sem(f"{p}_kt")
                self.step = sem(f"{p}_step")
                self.act = sem(f"{p}_act")
                self.pe = sem(f"{p}_pe")
                self.out = sem(f"{p}_out")
                self.fin = sem(f"{p}_fin")
                if slots == 2:
                    self.scored = sem(f"{p}_scored")
                    return
                self.split = sem(f"{p}_split")
                self.spread = sem(f"{p}_spread")
                self.multiplied = sem(f"{p}_multiplied")
                self.summed = sem(f"{p}_summed")
                self.kept = sem(f"{p}_kept")
        ZA, ZB = Sample("sa", 4), Sample("sb", 2)

        MA, MB = Mixer(NG), Mixer(1)
        PV0 = {id(MA): 0, id(MB): 2 * len(MB.batches)}

        def unit_at(u0, m=0, i=0):
            assert m % RING == 0
            if m:
                return u0 % RING, u0 + m * i, u0 // RING + (m // RING) * i
            return u0 % RING, u0, u0 // RING

        def load(sp, src, u0, m=0, i=0):
            slot, u, _ = unit_at(u0, m, i)
            sp.wait_ge(lo_ready, u - RING + 1)
            sp.dma_start(w_raw[:, slot, :].rearrange("p (k n) -> p k n", n=src.shape[-1]), src) \
                .then_inc(w_landed[slot], 16)

        def split_hi(act, u0, m=0, i=0):
            slot, u, use = unit_at(u0, m, i)
            act.wait_ge(w_landed[slot], 16 * use)
            act.wait_ge(w_used, u - RING + 1)
            act.copy(w_hi[:, slot, :], w_raw[:, slot, :]).then_inc(hi_ready, 1)

        def split_ahead(act, u0, m=0, i=0):
            if m or u0 + 2 < U_END:
                split_hi(act, u0 + 2, m, i)

        def split_lo(pool, u0, m=0, i=0):
            slot, u, _ = unit_at(u0, m, i)
            pool.wait_ge(hi_ready, u + 1)
            pool.tensor_tensor(w_lo[:, slot, :], w_raw[:, slot, :], w_hi[:, slot, :].bitcast(F32),
                               ALU.subtract).then_inc(lo_ready, 1)

        def units_pool(pool, u0, u1):
            loops = (u1 - u0) // RING
            if loops:
                with pool.Fori(0, loops) as i:
                    for e in range(RING):
                        split_lo(pool, u0 + e, RING, i)
            for u in range(u0 + RING * loops, u1):
                split_lo(pool, u)

        def product(pe, out, whi, wlo, ahi, alo, first, last):
            pe.matmul(out, whi, ahi, start=first, stop=False)
            pe.matmul(out, whi, alo, start=False, stop=False)
            return pe.matmul(out, wlo, ahi, start=False, stop=last)

        def normed_product(pe, slot, n):
            w1 = w_hi[:, slot, :].rearrange("p (k n) -> p k n", n=P)
            w2 = w_lo[:, slot, :].rearrange("p (k n) -> p k n", n=P)
            for j in range(KC):
                wait_normed(pe, n, j)
                for t in range(NT):
                    mm = product(pe, acc_set(0)[:, t, :], w1[:, j, :], w2[:, j, :],
                                 xh[:, j, TH * t:TH * t + TH], xl[:, j, TH * t:TH * t + TH], j == 0, j == KC - 1)
                    if j == KC - 1:
                        yield mm

        def thirds(x):
            return x.rearrange("p (t n) -> p t n", n=TH)

        def acc_set(n):
            return acc[:, 3 * (n % 2):3 * (n % 2) + 3, 0:TH]

        def wcols(w, c, width=P):
            return w.rearrange("(k p) (c n) -> p k c n", p=P, n=width)[:, :, c, :]

        w_in = a["a_w_in"].rearrange("l k n -> (l k) n")
        w_aout = a["a_w_out"].rearrange("l k n -> (l k) n")
        w_q = a["b_w_q"].rearrange("l k n -> (l k) n")
        w_bout = a["b_w_out"].rearrange("l k n -> (l k) n")

        XS = 4
        x_stage = carve(*[1024] * XS)
        y_stage = x_stage[0:2]
        conv_stage = carve(7 * T, 512, 512, 1024, 1024)[1:]
        cw_stage, st_stage = conv_stage[0:2], conv_stage[2:4]
        xp = a["x_prompt"].rearrange("b s d -> (b s) d")
        xsm = a["x_sample"].rearrange("b s d -> (b s) d")

        def rows_in_sp(sp):
            sp.dma_start(cst[:], a["consts"][:, 0:C_BLK]).then_inc(ident_in, 16)
            for n in range(NTILE + 1):
                if n >= XS:
                    sp.wait_ge(x_turned, n - XS + 1)
                if n < NTILE:
                    sp.dma_start(x_stage[n % XS], xp[P * n:P * n + P, :]).then_inc(x_in[n % XS], 16)
                else:
                    sp.dma_start(x_stage[n % XS][0:NS], xsm).then_inc(x_in[n % XS], 16)
                if n == XS - 1:
                    gains_sp(sp)
            for u in range(U_QKV, U_QKV + 3):
                load(sp, wcols(w_in, u - U_QKV), u)

        def gains_sp(sp):
            gains = [a["attn_norm_g"][0], a["ffn_norm_g"][0], a["b_kv_norm_g"], a["attn_norm_g"][1],
                     a["ffn_norm_g"][1]]
            for n, g in enumerate(gains):
                sp.dma_start(norm_rows[KC * n:KC * n + KC, :], g.rearrange("(k p) -> k p", p=P)).then_inc(tab_in, 16)
            sp.wait_ge(gain_rows_set, 1)
            for c0, n, g in [(4 * e, 4, a["a_q_norm_g"][0, e]) for e in range(NG)] + \
                    [(12 + 4 * e, 4, a["a_k_norm_g"][0, e]) for e in range(NG)] + \
                    [(36, 1, a["b_k_norm_g"]), (38, 8, a["b_q_norm_g"][0])]:
                sp.dma_start(head_rows[c0:c0 + n, :].rearrange("c (h d) -> c h d", h=2),
                             g.unsqueeze(0).unsqueeze(0).to_broadcast([n, 2, HD])).then_inc(tab_in, 16)
            sp.dma_start(sink_rows, a["b_sinks"][0].rearrange("(c h) -> c h", h=2)).then_inc(tab_in, 16)
            sp.dma_start(sink_col[:], a["b_sinks"][0].unsqueeze(1).to_broadcast([16, NS]).unsqueeze(2)) \
                .then_inc(const_in, 16)
            sp.dma_start(rope[:], a["consts"][:, C_COS:C_END].rearrange("p (a t) -> p a t", a=2)) \
                .then_inc(const_in, 16)
            sp.dma_start(mask_stage, a["consts"][:, C_MQ:C_COS]).then_inc(const_in, 16)
            sp.dma_start(op_stage, a["consts"][:, C_BLK:C_MQ]).then_inc(const_in, 16)

        def conv_tables_sp(sp):
            wait_normed(sp, 0, KC - 2)
            wait_normed(sp, 0, KC - 1)
            for l in range(2):
                sp.dma_start(cw_stage[l][0:2 * FC, 0:3 * P].rearrange("c (t f) -> c t f", t=3),
                             a["ffn_conv_w"][l].rearrange("t (c f) -> c t f", f=P)).then_inc(conv_in, 16)
                sp.dma_start(cw_stage[l][0:2 * FC, 3 * P:4 * P],
                             a["ffn_conv_b"][l].rearrange("(c f) -> c f", f=P)).then_inc(conv_in, 16)
                for t in range(2):
                    sp.dma_start(st_stage[l][2 * FC * t:2 * FC * (t + 1), :].rearrange("c (s f) -> c s f", f=P),
                                 a["state_ffn_conv"][l, :, t, :].rearrange("s (c f) -> c s f", f=P)) \
                        .then_inc(conv_in, 16)

        CONSTS_IN = 16 * 4
        GAINS_IN = 16 * (5 + 8 + 1)
        mask_stage, op_stage = arena[:, 6144:7168], arena[:, 7430:7430 + 2 * P]
        head_rows, norm_rows = arena[0:46, 7168:7296], arena[0:5 * KC, 7296:7424]
        sink_rows = arena[0:B_CHUNKS, 7424:7426]

        def rows_in_pe(pe):
            pe.wait_ge(ident_in, 16)
            for n in range(NTILE + 1):
                pe.wait_ge(x_in[n % XS], 16 * (n // XS + 1))
                if n >= 3:
                    pe.wait_ge(h_set, 2 * (n - 3) + 2)
                rows = P if n < NTILE else NS
                for c in range(KC):
                    mm = pe.transpose(acc[:, (2 * n + c // 4) % 6, P * (c % 4):P * (c % 4) + rows],
                                      x_stage[n % XS][0:rows, P * c:P * c + P], ident[0:rows, 0:rows])
                mm.then_inc(x_turned, 1)
            pe.wait_ge(tab_in, GAINS_IN)
            pe.transpose(aux[:, 1, 0:46], head_rows, ident[0:46, 0:46])
            pe.transpose(aux[:, 1, 64:64 + 5 * KC], norm_rows, ident[0:5 * KC, 0:5 * KC])
            pe.transpose(aux[0:2, 1, 128:128 + B_CHUNKS], sink_rows, ident[0:B_CHUNKS, 0:B_CHUNKS]) \
                .then_inc(gains_turned, 1)

        def conv_tables_pe(pe):
            pe.wait_ge(conv_in, 16 * 2 * 4)
            pe.wait_ge(chunk_out, 3 * CH_B)
            for l in range(2):
                if l:
                    pe.wait_ge(tab_set, 2)
                for t in range(4):
                    mm = pe.transpose(aux[:, 0, 2 * FC * t:2 * FC * (t + 1)], cw_stage[l][0:2 * FC, P * t:P * t + P],
                                      ident[0:2 * FC, 0:2 * FC])
                mm.then_inc(tab_turned, 1)
                for half in range(2):
                    pe.wait_ge(tab_set, 3 * l + half) if l or half else None
                    for s in range(4):
                        q = 4 * half + s
                        mm = pe.transpose(aux[:, 1, 4 * FC * s:4 * FC * (s + 1)],
                                          st_stage[l][0:4 * FC, P * q:P * q + P], ident[0:4 * FC, 0:4 * FC])
                    mm.then_inc(tab_turned, 1)
                    pe.wait_ge(tab_set, 3 * l + half + 2)

        def rows_in_dve(v):
            v.memset(head_rows, 1.0).then_inc(gain_rows_set, 1)
            for n in range(NTILE + 1):
                v.wait_ge(x_turned, n + 1)
                rows = P if n < NTILE else NS
                for b in range(2):
                    v.tensor_copy(hT[:, 4 * b:4 * b + 4, P * n:P * n + rows],
                                  acc[:, (2 * n + b) % 6, :].rearrange("p (c n) -> p c n", n=P)[:, :, 0:rows]) \
                        .then_inc(h_set, 1)
            v.wait_ge(gains_turned, 1)
            v.tensor_copy(head_g[:], aux[:, 1, 0:46]).then_inc(gains_set, 1)
            v.tensor_copy(norm_g[:].rearrange("p n k -> p (n k)"), aux[:, 1, 64:64 + 5 * KC]).then_inc(gains_set, 1)
            v.tensor_copy(sink[:], aux[0:2, 1, 128:128 + B_CHUNKS]).then_inc(gains_set, 1)

        def conv_tables_dve(v):
            for l in range(2):
                v.wait_ge(tab_turned, 3 * l + 1)
                v.tensor_copy(cw[:, l, :, :], aux[:, 0, 0:8 * FC].rearrange("p (t c) -> p t c", t=4)).then_inc(tab_set, 1)
                for half in range(2):
                    v.wait_ge(tab_turned, 3 * l + half + 2)
                    v.tensor_copy(st_T[:, l, 4 * half:4 * half + 4, :],
                                  aux[:, 1, 0:16 * FC].rearrange("p (s c) -> p s c", s=4)) \
                        .then_inc(tab_set, 1)

        def consts_dve(v):
            v.memset(eps[:], EPS).then_inc(const_set, 1)
            v.memset(sel_den[:], 0.0).then_inc(const_set, 1)
            v.wait_ge(ident_in, 16)
            v.wait_ge(const_in, CONSTS_IN)
            v.tensor_copy(masks[:].rearrange("p a m n -> p (a m n)"), mask_stage).then_inc(const_set, 1)
            v.tensor_copy(head_ops[:].rearrange("p a n -> p (a n)"), op_stage).then_inc(const_set, 1)
            v.tensor_copy(ident_b[:], ident).then_inc(const_set, 1)
            for h in range(2):
                v.tensor_scalar(sel[:, h, :], ones[0:2, :], cst[0:2, C_ID + h:C_ID + h + 1], None, ALU.mult) \
                    .then_inc(const_set, 1)
            v.wait_ge(gains_set, 3)
            v.tensor_scalar(sink8[:], sink[:], 1.0 / SCALE, None, ALU.mult).then_inc(const_set, 1)
            v.wait_ge(const_set, 8)
            for h in range(2):
                half = HD * (1 - h)
                v.tensor_copy(sel_den[:, h, half:half + HD], sel[:, h, half:half + HD].bitcast(F32)) \
                    .then_inc(const_set, 1)
            v.wait_ge(const_set, 10)
            v.tensor_scalar(sink_col[:], sink_col[:], 1.0 / SCALE, None, ALU.mult).then_inc(const_set, 1)

        CONSTS_SET = 11

        XF = 3
        xf_n = carve(7 * T, *[T] * XF)[1:]

        def wait_normed(eng, n, k):
            eng.wait_ge((n_lo, n_lo_odd)[k % 2], KC // 2 * n + k // 2 + 1)

        def norm_lo(eng, n, k):
            eng.wait_ge(n_hi, 8 * n + k + 1)
            eng.tensor_tensor(xl[:, k, :], xf_n[k % XF], xh[:, k, :].bitcast(F32), ALU.subtract) \
                .then_inc((n_lo, n_lo_odd)[k % 2], 1)

        def norm_pool(pool, n):
            for k in range(1, KC, 2):
                norm_lo(pool, n, k)

        sq_n0, sq_n1, sq_sum = carve(7000, T, T, T)[1:]
        sq_n = [sq_n0, sq_n1]
        STAT = {0: 0, 1: 1, 2: 2, 4: 3}

        def square_act(act, n, k, ready):
            ready(act)
            if k > 1:
                act.wait_ge(n_add, 7 * STAT[n] + k - 2)
            act.activation(sq_sum if k == 0 else sq_n[k % 2], hT[:, k, :], ACT.Square).then_inc(n_sq, 1)

        def square_dve(v, n, k):
            v.wait_ge(n_sq, 8 * STAT[n] + k + 1)
            if k:
                v.wait_ge(n_add, 7 * STAT[n] + k - 1)
                v.tensor_tensor(sq_sum, sq_sum, sq_n[k % 2], ALU.add).then_inc(n_add, 1)

        def norm_act(act, n):
            if n in STAT:
                act.wait_ge(n_mm, STAT[n] + 1)
                act.activation(thirds(rinv[:]), acc_set(0), ACT.Ln, bias=eps[:], scale=1.0 / D).then_inc(n_stat, 1)
                act.wait_ge(n_stat, 2 * STAT[n] + 1)
                act.activation(rinv[:], rinv[:], ACT.Exp, scale=-0.5).then_inc(n_stat, 1)
            for k in range(KC):
                act.wait_ge(n_x, 8 * n + k + 1)
                act.copy(xh[:, k, :], xf_n[k % XF]).then_inc(n_hi, 1)

        def norm_pe(pe, n):
            pe.wait_ge(n_add, 7 * STAT[n] + 7)
            for t in range(NT):
                mm = pe.matmul(acc_set(0)[:, t, :], ones, sq_sum[:, TH * t:TH * t + TH], start=True, stop=True)
            mm.then_inc(n_mm, 1)

        def norm_dve(v, n):
            if n in STAT:
                v.wait_ge(n_stat, 2 * STAT[n] + 2)
            for k in range(KC):
                if k >= XF:
                    wait_normed(v, n, k - XF)
                v.scalar_tensor_tensor(xf_n[k % XF], hT[:, k, :], norm_g[:, n, k:k + 1], rinv[:],
                                       ALU.mult, ALU.mult).then_inc(n_x, 1)
                if k % 2:
                    norm_lo(v, n, k - 1)

        CH = 2
        CH_B = CH + A_CHUNKS
        Q_B = 24
        qg, sq_p, rr, ob0, ob1, t1b, t2b, lnb = carve(T, T, T, T, T, 2 * TH, 2 * TH, 2 * TH)
        outb = [ob0, ob1]
        sq_hi, qg_hi, sq_lo, qg_lo = f_hi[:, 0, :], f_hi[:, 1, :], f_lo[:, 0, :], f_lo[:, 1, :]

        def third(x, t):
            return x[:, TH * t:TH * t + TH]

        def counts_pe(pe):
            pe.sem_inc(w_used, RING)
            pe.sem_inc(third_full, 2 * CH)

        def counts_act(act):
            act.sem_inc(hi_ready, RING)
            act.sem_inc(acc_evac, 3 * CH)

        def proj_normed(pe, c, u0, n):
            pe.wait_ge(lo_ready, u0 + 1)
            pe.wait_ge(acc_evac, 3 * c - 3)
            for t, mm in enumerate(normed_product(pe, u0 % RING, n)):
                mm.then_inc(w_used if t == NT - 1 else third_full, 1)

        def proj_main(pe, c, k, u0, m, i, t):
            slot, u, _ = unit_at(u0, m, i)
            if t == 0:
                pe.wait_ge(lo_ready, u + 1)
                pe.wait_ge(acc_evac, 3 * c - 3)
            w1 = w_hi[:, slot, :].rearrange("p (k n) -> p k n", n=P)
            w2 = w_lo[:, slot, :].rearrange("p (k n) -> p k n", n=P)
            for j in range(KC):
                mm = product(pe, acc_set(k)[:, t, :], w1[:, j, :], w2[:, j, :], third(xh[:, j, :], t),
                             third(xl[:, j, :], t), j == 0, j == KC - 1)
            mm.then_inc(w_used if t == NT - 1 else third_full, 1)

        def proj_aux(pe, c, q, t):
            for bank, m, hi, lo, n, used, ready in (
                    (1, rot, qg_hi, qg_lo, 1, rot_used, rot_ready),
                    (0, blk, sq_hi, sq_lo, 2, ln_done, ssq_ready)):
                pe.wait_ge(aux_split, 2 * (3 * q + t) + n)
                pe.wait_ge(used, 3 * q + t)
                pe.matmul(aux[:, bank, 0:TH], m, third(hi, t), start=True, stop=False)
                pe.matmul(aux[:, bank, 0:TH], m, third(lo, t), start=False, stop=True) \
                    .then_inc(ready, 1)

        def proj_evac(act, c, k, u0, m, i, t, gain):
            _, u, _ = unit_at(u0, m, i)
            if t < NT - 1:
                act.wait_ge(third_full, 2 * c + t + 1)
            else:
                act.wait_ge(w_used, u + 1)
            act.wait_ge(chunk_out, 3 * c + t - 2)
            if gain is not None:
                act.activation(third(sq_p, t), acc_set(k)[:, t, :], ACT.Square)
                act.activation(third(qg, t), acc_set(k)[:, t, :], ACT.Copy, scale=gain).then_inc(acc_evac, 1)
                act.wait_ge(acc_evac, 3 * c + t + 1)
                act.copy(third(sq_hi, t), third(sq_p, t)).then_inc(sq_split, 1)
            else:
                act.copy(third(qg, t), acc_set(k)[:, t, :]).then_inc(acc_evac, 1)

        def proj_stat(act, q, t):
            s = third(lnb, t % 2)
            act.wait_ge(ssq_ready, 3 * q + t + 1)
            act.wait_ge(r_ready, 3 * q + t)
            act.activation(s, aux[:, 0, 0:TH], ACT.Ln, bias=eps[:], scale=1.0 / HD).then_inc(ln_done, 1)
            act.wait_ge(ln_done, 3 * q + t + 1)
            act.activation(third(rr, t), s, ACT.Exp, scale=-0.5).then_inc(r_ready, 1)

        def proj_split(v, c, q, t):
            n = 3 * q + t
            v.wait_ge(acc_evac, 3 * c + t + 1)
            v.tensor_copy(third(qg_hi, t), third(qg, t)).then_inc(qg_split, 1)
            v.wait_ge(qg_split, n + 1)
            v.tensor_tensor(third(qg_lo, t), third(qg, t), third(qg_hi, t).bitcast(F32), ALU.subtract) \
                .then_inc(aux_split, 1)
            v.wait_ge(sq_split, n + 1)
            v.tensor_tensor(third(sq_lo, t), third(sq_p, t), third(sq_hi, t).bitcast(F32), ALU.subtract) \
                .then_inc(aux_split, 1)

        def proj_dve(v, c, k, q, t):
            v.wait_ge(acc_evac, 3 * c + t + 1)
            if t == 0:
                v.wait_ge(stored[k], 8 * (c - k) - 16)
            if q is None:
                v.tensor_copy(third(outb[k], t), third(qg, t)).then_inc(chunk_out, 1)
                return
            n = 3 * q + t
            s1, s2 = third(t1b, t % 2), third(t2b, t % 2)
            v.wait_ge(chunk_out, 3 * c + t)
            v.tensor_tensor(s1, third(qg, t), third(rope[:, 0, :], t), ALU.mult).then_inc(qk_step, 1)
            v.wait_ge(rot_ready, 3 * q + t + 1)
            v.tensor_tensor(s2, aux[:, 1, 0:TH], third(rope[:, 1, :], t), ALU.mult).then_inc(rot_used, 1)
            v.wait_ge(qk_step, 2 * n + 1)
            v.wait_ge(rot_used, 3 * q + t + 1)
            v.tensor_tensor(s1, s1, s2, ALU.add).then_inc(qk_step, 1)
            v.wait_ge(qk_step, 2 * n + 2)
            v.wait_ge(r_ready, 3 * q + t + 1)
            v.tensor_tensor(third(outb[k], t), s1, third(rr, t), ALU.mult).then_inc(chunk_out, 1)

        def proj_a(eng, first, main, aux_of, aux_first):
            def step(one, other):
                for f in (other, one) if aux_first else (one, other):
                    f()
            first()
            with eng.Fori(0, 3) as i:
                for e in range(BODY):
                    for t in range(NT):
                        step(lambda: main(e + 1, BODY, i, t), lambda: aux_of(e, BODY, i, t))
            for n in range(3 * BODY + 1, A_CHUNKS):
                for t in range(NT):
                    step(lambda: main(n, 0, 0, t), lambda: aux_of(n - 1, 0, 0, t) if n <= 24 else None)

        def proj_a_pe(pe):
            proj_a(pe, lambda: proj_normed(pe, CH, U_QKV, 0),
                   lambda n, m, i, t: proj_main(pe, CH + n + m * i, n % 2, U_QKV + n, m, i, t),
                   lambda n, m, i, t: proj_aux(pe, CH + n + m * i, n + m * i, t), False)

        def proj_a_act(act):
            def main(n, m, i, t):
                if t == 0:
                    split_ahead(act, U_QKV + n, m, i)
                gain = None if m == 0 and n >= 24 else head_g[:, bass.ds(n + m * i, 1)] if m else head_g[:, n:n + 1]
                proj_evac(act, CH + n + m * i, n % 2, U_QKV + n, m, i, t, gain)
            proj_a(act, lambda: [main(0, 0, 0, t) for t in range(NT)], main, lambda n, m, i, t: proj_stat(act, n + m * i, t), True)

        def proj_a_dve(v):
            for t in range(2):
                proj_split(v, CH, 0, t)
            with v.Fori(0, 24 // BODY - 1) as i:
                for e in range(BODY):
                    for t in range(NT):
                        proj_dve(v, CH + e + BODY * i, e % 2, e + BODY * i, t)
                        f, tf = (e, 2) if t == 0 else (e + 1, t - 1)
                        proj_split(v, CH + f + BODY * i, f + BODY * i, tf)
            for n in range(24 - BODY, 24):
                for t in range(NT):
                    proj_dve(v, CH + n, n % 2, n, t)
                    f, tf = (n, 2) if t == 0 else (n + 1, t - 1)
                    if f < 24:
                        proj_split(v, CH + f, f, tf)
            with v.Fori(0, 12 // BODY) as i:
                for e in range(BODY):
                    for t in range(NT):
                        proj_dve(v, CH + 24 + e + BODY * i, e % 2, None, t)

        def store_chunk(sp, c, k, to):
            sp.wait_ge(chunk_out, 3 * c + 3)
            sp.dma_start(to, outb[k]).then_inc(stored[k], 16)

        def proj_a_sp(sp):
            with sp.Fori(0, A_CHUNKS // BODY - 1) as i:
                for e in range(BODY):
                    load(sp, wcols(w_in, e + 3 + BODY * i), U_QKV + 3 + e, BODY, i)
                    store_chunk(sp, CH + e + BODY * i, e % 2, scratch[e + BODY * i])
            for n in range(A_CHUNKS - BODY, A_CHUNKS):
                if n + 3 < A_CHUNKS:
                    load(sp, wcols(w_in, n + 3), U_QKV + n + 3)
                else:
                    load(sp, wcols(w_aout, n + 3 - A_CHUNKS, 2 * P), U_QKV + n + 3)
                store_chunk(sp, CH + n, n % 2, scratch[n])

        def proj_b_pe(pe):
            norm_pe(pe, 2)
            proj_normed(pe, CH_B, U_KV, 2)
            for t in range(NT):
                proj_main(pe, CH_B + 1, 1, U_KV + 1, 0, 0, t)
                proj_aux(pe, CH_B, Q_B, t)
            proj_normed(pe, CH_B + 2, U_BQ, 3)
            for n in range(1, B_CHUNKS):
                for t in range(NT):
                    proj_main(pe, CH_B + 2 + n, n % 2, U_BQ + n, 0, 0, t)
                    proj_aux(pe, CH_B + 1 + n, Q_B + n, t)
            for t in range(NT):
                proj_aux(pe, CH_B + 1 + B_CHUNKS, Q_B + B_CHUNKS, t)

        def proj_b_act(act):
            split_ahead(act, U_KV)
            for t in range(NT):
                proj_evac(act, CH_B, 0, U_KV, 0, 0, t, head_g[:, 36:37])
            split_ahead(act, U_KV + 1)
            for t in range(NT):
                proj_stat(act, Q_B, t)
                proj_evac(act, CH_B + 1, 1, U_KV + 1, 0, 0, t, None)
            act.wait_ge(w_used, U_BQ)
            norm_act(act, 3)
            for n in range(B_CHUNKS):
                split_ahead(act, U_BQ + n)
                for t in range(NT):
                    if n:
                        proj_stat(act, Q_B + n, t)
                    proj_evac(act, CH_B + 2 + n, n % 2, U_BQ + n, 0, 0, t, head_g[:, 38 + n:39 + n])
            for t in range(NT):
                proj_stat(act, Q_B + B_CHUNKS, t)

        def proj_b_dve(v):
            for t in range(NT):
                proj_split(v, CH_B, Q_B, t)
            for t in range(NT):
                proj_dve(v, CH_B, 0, Q_B, t)
            for t in range(NT):
                proj_dve(v, CH_B + 1, 1, None, t)
            norm_dve(v, 3)
            for t in range(2):
                proj_split(v, CH_B + 2, Q_B + 1, t)
            for n in range(B_CHUNKS):
                for t in range(NT):
                    proj_dve(v, CH_B + 2 + n, n % 2, Q_B + 1 + n, t)
                    f, tf = (n, 2) if t == 0 else (n + 1, t - 1)
                    if f < B_CHUNKS:
                        proj_split(v, CH_B + 2 + f, Q_B + 1 + f, tf)

        def proj_b_sp(sp):
            for n in range(2 + B_CHUNKS):
                if n + 3 < 2 + B_CHUNKS:
                    load(sp, wcols(w_q, n + 1), U_KV + n + 3)
                else:
                    load(sp, wcols(w_bout, n + 3 - 2 - B_CHUNKS), U_KV + n + 3)
                store_chunk(sp, CH_B + n, n % 2, scratch[A_CHUNKS + n])

        ADDED = {"a": 0, 0: KC, "b": KC + KC * FFN_TURNS, 1: 2 * KC + KC * FFN_TURNS}

        def out_main(pe, n, banks, u0, half, kcs, parts, done):
            slot, u, _ = unit_at(u0)
            pe.wait_ge(lo_ready, u + 1)
            w1 = w_hi[:, slot, :].rearrange("p (k n) -> p k n", k=kcs)
            w2 = w_lo[:, slot, :].rearrange("p (k n) -> p k n", k=kcs)
            for t in parts:
                for j in range(kcs):
                    mm = product(pe, banks[:, t - parts[0], :], w1[:, j, P * half:P * half + P],
                                 w2[:, j, P * half:P * half + P], third(xh[:, j, :], t), third(xl[:, j, :], t),
                                 j == 0, j == kcs - 1)
            mm.then_inc(done, 1)

        def add_to_h(v, n, k):
            v.tensor_tensor(thirds(hT[:, n, :]), thirds(hT[:, n, :]), acc_set(k), ALU.add).then_inc(h_added, 1)

        PIECES = 2 * KC

        def aout_first_pe(pe, n):
            if n == 0:
                pe.wait_ge(SA.o_lo, A_PAIRS)
            elif n >= 2:
                pe.wait_ge(first_added, n - 1)
            out_main(pe, n // 2, acc[:, 4 + n % 2:5 + n % 2, 0:TH], U_AOUT + n // 4, n // 2 % 2, 4, (n % 2,),
                     w_used if n % 4 == 3 else first_full)

        def aout_first_dve(v, n):
            if n % 4 == 3:
                v.wait_ge(w_used, U_AOUT + n // 4 + 1)
            else:
                v.wait_ge(first_full, 3 * (n // 4) + n % 4 + 1)
            h = third(hT[:, n // 2, :], n % 2)
            v.tensor_tensor(h, h, acc[:, 4 + n % 2, 0:TH], ALU.add).then_inc(first_added, 1)

        def aout_pe(pe):
            pe.wait_ge(ZA.fin, 1)
            for n in range(KC):
                if n >= 2:
                    pe.wait_ge(h_added, n - 1)
                out_main(pe, n, acc_set(n)[:, 2:3, :], U_AOUT + 4 + n // 2, n % 2, 4, (2,),
                         w_used if n % 2 else res_full)

        def aout_act(act):
            for n in range(3, 8):
                split_ahead(act, U_AOUT + n)
                if n >= 4:
                    for k in (2 * n - 10, 2 * n - 9):
                        if k >= 0:
                            square_act(act, 1, k, lambda e: e.wait_ge(h_added, k + 1))
            for k in (KC - 2, KC - 1):
                square_act(act, 1, k, lambda e: e.wait_ge(h_added, k + 1))

        def aout_dve(v):
            for n in range(KC):
                if n % 2 == 0:
                    v.wait_ge(res_full, n // 2 + 1)
                else:
                    v.wait_ge(w_used, U_AOUT + 4 + n // 2 + 1)
                h = third(hT[:, n, :], 2)
                v.tensor_tensor(h, h, acc_set(n)[:, 2, :], ALU.add).then_inc(h_added, 1)
                if n:
                    square_dve(v, 1, n - 1)
            square_dve(v, 1, KC - 1)

        def bout_pe(pe):
            pe.wait_ge(SB.o_lo, B_CHUNKS)
            pe.wait_ge(ZB.fin, 1)
            for n in range(KC):
                if n >= 2:
                    pe.wait_ge(h_added, ADDED["b"] + n - 1)
                out_main(pe, n, acc_set(n), U_BOUT + n, 0, KC, (0, 1, 2), w_used)

        def bout_act(act):
            for n in range(KC):
                split_ahead(act, U_BOUT + n)
                if n:
                    square_act(act, 4, n - 1, lambda e: e.wait_ge(h_added, ADDED["b"] + n))
            square_act(act, 4, KC - 1, lambda e: e.wait_ge(h_added, ADDED["b"] + KC))

        def bout_dve(v):
            for n in range(KC):
                v.wait_ge(w_used, U_BOUT + n + 1)
                add_to_h(v, n, n % 2)
                if n:
                    square_dve(v, 4, n - 1)
            square_dve(v, 4, KC - 1)

        U1 = T + 2
        ug, uv, cg, cv, ebuf, fbuf, tail_sb = carve(U1, U1, T, T, T, T, 640)
        GATE, VAL = 0, 1
        u_ext, c_out = [ug, uv], [cg, cv]
        UPS = 4 * FFN_TURNS
        CONV_STEPS = 4
        TURN_STEPS = 4 * CONV_STEPS
        LAST = FFN_TURNS - 1

        class Turn:
            def __init__(self, l, i, last):
                self.l, self.i, self.last = l, i, last
                self.m = 0 if last else 6
                self.off = 6 * i if last else 0
                self.ii = 0 if last else i
                self.unit0 = [U_FFN0, U_FFN1][l]
                self.up = UPS * l + 4 * i
                self.added = ADDED[l] + KC * i
                self.res = 4 + 7 * FFN_TURNS * l + 7 * i
                self.f = 2 * FFN_TURNS * l + 2 * i
                self.steps = TURN_STEPS * FFN_TURNS * l + CONV_STEPS + TURN_STEPS * i
                self.d0 = 4 if last else 5

            def unit(self, o):
                return self.unit0 + self.off + o, self.m, self.ii

            def no(self, o):
                return unit_at(*self.unit(o))[1]

        def turns(eng, l, body):
            with eng.Fori(0, LAST) as i:
                body(eng, Turn(l, i, False))
            body(eng, Turn(l, LAST, True))

        def up_pe(pe, unit, k):
            slot, u, _ = unit_at(*unit)
            pe.wait_ge(lo_ready, u + 1)
            w1 = w_hi[:, slot, :].rearrange("p (k n) -> p k n", n=P)
            w2 = w_lo[:, slot, :].rearrange("p (k n) -> p k n", n=P)
            for t in range(NT):
                for j in range(KC):
                    mm = product(pe, acc_set(k)[:, t, :], w1[:, j, :], w2[:, j, :], third(xh[:, j, :], t),
                                 third(xl[:, j, :], t), j == 0, j == KC - 1)
            mm.then_inc(w_used, 1)

        def ffn_turn_pe(pe, z):
            pe.wait_ge(h_added, z.added - 1)
            up_pe(pe, z.unit(1), 1)
            pe.wait_ge(h_added, z.added)
            pe.wait_ge(up_evac, z.up + 1)
            up_pe(pe, z.unit(2), 0)
            pe.wait_ge(up_evac, z.up + 2)
            up_pe(pe, z.unit(3), 1)
            if not z.last:
                pe.wait_ge(up_evac, z.up + 3)
                up_pe(pe, z.unit(4), 0)
            k0 = 0 if z.last else 1
            slots = [unit_at(*z.unit(z.d0 + e))[0] for e in range(2)]
            pe.wait_ge(lo_ready, z.no(z.d0 + 1) + 1)

            def down(n, e, t):
                s = slots[e]
                return product(pe, acc_set(k0 + n)[:, t, :], w_hi[:, s, P * n:P * n + P],
                               w_lo[:, s, P * n:P * n + P], third(f_hi[:, e, :], t), third(f_lo[:, e, :], t),
                               e == 0, e == 1)

            early = 2 if z.last else 0
            pe.wait_ge(flo_ready, z.f + 1)
            for n in range(early):
                pe.wait_ge(up_evac, z.up + n + 3)
                for t in range(NT):
                    down(n, 0, t)
            pe.wait_ge(flo_ready, z.f + 2)
            for n in range(KC):
                if n >= 2:
                    pe.wait_ge(h_added, z.added + n - 1)
                elif not z.last:
                    pe.wait_ge(up_evac, z.up + n + 4)
                for t in range(NT):
                    if n >= early:
                        m0 = down(n, 0, t)
                    m1 = down(n, 1, t)
                if n < KC - 1:
                    m1.then_inc(res_full, 1)
                else:
                    m0.then_inc(w_used, 1)
                    m1.then_inc(w_used, 1)

        def ffn_pe(pe, l):
            norm_pe(pe, 1 + 3 * l)
            u0 = [U_FFN0, U_FFN1][l]
            pe.wait_ge(lo_ready, u0 + 1)
            *_, mm = normed_product(pe, u0 % RING, 1 + 3 * l)
            mm.then_inc(w_used, 1)
            turns(pe, l, ffn_turn_pe)
            pe.wait_ge(conv_out, UPS * (l + 1))
            pe.wait_ge(tail_set, 2 * l)
            for s in range(5):
                mm = pe.transpose(aux[0:4 * FC, s // 4, P * (s % 4):P * (s % 4) + P],
                                  u_tail[:, 2 * s:2 * s + 2, :].rearrange("p a c -> p (a c)"), ident)
            mm.then_inc(tail_turned, 1)

        def up_evac_act(act, z, o, which, k):
            act.wait_ge(w_used, z.no(o) + 1)
            act.wait_ge(conv_out, z.up + o - 1)
            act.copy(thirds(u_ext[which][:, 2:U1]), acc_set(k)).then_inc(up_evac, 1)

        def gate_act(act, z, e):
            act.wait_ge(conv_out, z.up + 2 * e + 1)
            act.wait_ge(f_raw, z.f + e)
            act.activation(ebuf, cg, ACT.Silu).then_inc(e_ready, 1)
            act.wait_ge(f_raw, z.f + e + 1)
            act.wait_ge(w_used, z.no(1))
            act.copy(f_hi[:, e, :], fbuf).then_inc(fhi_ready, 1)

        def ffn_turn_act(act, z):
            split_ahead(act, *z.unit(1))
            up_evac_act(act, z, 1, VAL, 1)
            split_ahead(act, *z.unit(2))
            gate_act(act, z, 0)
            up_evac_act(act, z, 2, GATE, 0)
            split_ahead(act, *z.unit(3))
            up_evac_act(act, z, 3, VAL, 1)
            if not z.last:
                split_ahead(act, *z.unit(4))
            gate_act(act, z, 1)
            if not z.last:
                up_evac_act(act, z, 4, GATE, 0)
            split_ahead(act, *z.unit(z.d0))
            if z.last and z.l == 0:
                for k in range(KC):
                    square_act(act, 2, k, lambda e: e.wait_ge(h_added, ADDED["b"] - KC + k + 1))
            split_ahead(act, *z.unit(z.d0 + 1))

        def ffn_act(act, l):
            norm_act(act, 1 + 3 * l)
            act.preload_act_table_set("silu_and_others")
            u0 = [U_FFN0, U_FFN1][l]
            split_ahead(act, u0)
            act.wait_ge(w_used, u0 + 1)
            act.copy(thirds(u_ext[GATE][:, 2:U1]), acc_set(0)).then_inc(up_evac, 1)
            turns(act, l, ffn_turn_act)
            if l == 0:
                act.preload_act_table_set("natural_log_exp_and_others")

        def conv_dve(v, l, n, which, ch, s, products):
            u, c = u_ext[which], c_out[which]
            w = [cw[:, l, t, bass.ds(ch, 1)] for t in range(4)]
            state = [st_T[:, l, :, bass.ds(ch + 2 * FC * t, 1)] for t in range(2)]
            cs = c[:, SEQ:T].unsqueeze(2)
            v.wait_ge(up_evac, n + 1)
            v.wait_ge(f_raw, products)
            v.tensor_scalar(c[:, 0:T], u[:, 2:U1], w[2], w[3], ALU.mult, ALU.add).then_inc(conv_step, 1)
            v.tensor_copy(u_tail[:, :, bass.ds(ch, 1)], u[:, SEQ:U1].unsqueeze(2))
            v.wait_ge(conv_step, s + 1)
            v.scalar_tensor_tensor(c[:, 0:SEQ], u[:, 1:SEQ + 1], w[1], c[:, 0:SEQ], ALU.mult, ALU.add) \
                .then_inc(conv_step, 1)
            v.scalar_tensor_tensor(cs, state[1], w[1], cs, ALU.mult, ALU.add).then_inc(conv_step, 1)
            v.wait_ge(conv_step, s + 2)
            v.scalar_tensor_tensor(c[:, 0:SEQ], u[:, 0:SEQ], w[0], c[:, 0:SEQ], ALU.mult, ALU.add) \
                .then_inc(conv_step, 1)
            v.wait_ge(conv_step, s + 3)
            v.scalar_tensor_tensor(cs, state[0], w[0], cs, ALU.mult, ALU.add).then_inc(conv_out, 1)

        def gated_dve(v, z, e):
            v.wait_ge(conv_out, z.up + 2 * e + 2)
            v.wait_ge(e_ready, z.f + e + 1)
            v.wait_ge(flo_ready, z.f + e)
            v.tensor_tensor(fbuf, cv, ebuf, ALU.mult).then_inc(f_raw, 1)
            v.wait_ge(fhi_ready, z.f + e + 1)
            v.tensor_tensor(f_lo[:, e, :], fbuf, f_hi[:, e, :].bitcast(F32), ALU.subtract).then_inc(flo_ready, 1)

        def ffn_turn_dve(v, z):
            s, l, g = z.steps, z.l, 2 * z.i
            conv_dve(v, l, z.up + 1, VAL, FC + g, s, z.f)
            gated_dve(v, z, 0)
            s += CONV_STEPS
            conv_dve(v, l, z.up + 2, GATE, g + 1, s, z.f + 1)
            conv_dve(v, l, z.up + 3, VAL, FC + g + 1, s + CONV_STEPS, z.f + 1)
            gated_dve(v, z, 1)
            s += 2 * CONV_STEPS
            k0 = 0 if z.last else 1
            for n in range(KC):
                if n < KC - 1:
                    v.wait_ge(res_full, z.res + n + 1)
                else:
                    v.wait_ge(w_used, z.no(z.d0 + 1) + 1)
                add_to_h(v, n, k0 + n)
                if z.last and l == 0 and n:
                    square_dve(v, 2, n - 1)
            if not z.last:
                conv_dve(v, l, z.up + 4, GATE, g + 2, s, z.f + 2)
            elif l == 0:
                square_dve(v, 2, KC - 1)

        def ffn_dve(v, l):
            norm_dve(v, 1 + 3 * l)
            for k in (KC - 2, KC - 1):
                wait_normed(v, 1 + 3 * l, k)
            for n in range(2):
                v.memset(u_ext[n][:, 0:2], 0.0).then_inc(chain, 1)
            v.wait_ge(chain, 2 * (l + 1))
            conv_dve(v, l, UPS * l, GATE, 0, TURN_STEPS * FFN_TURNS * l, 2 * FFN_TURNS * l)
            turns(v, l, ffn_turn_dve)
            v.wait_ge(tail_turned, l + 1)
            v.wait_ge(tail_out, 16 * TAILS * l)
            v.tensor_copy(tail_sb[0:4 * FC, 0:512], aux[0:4 * FC, 0, :]).then_inc(tail_set, 1)
            v.tensor_copy(tail_sb[0:4 * FC, 512:640], aux[0:4 * FC, 1, 0:P]).then_inc(tail_set, 1)

        TAILS = 1 + NS
        up_w = [a["ffn_w_up"][l] for l in range(2)]

        def down_unit(l, c):
            return a["ffn_w_down"][l].rearrange("(c p) (k n) -> c p k n", p=P, k=1)[c]

        CACHE_PIECES = (A_PAIRS, B_CHUNKS, 2 * FFN_TURNS + 1)
        ROW = 8 * HD
        caches = [a["cache_a_kv_w128"], a["cache_a_kv_w512"], a["cache_a_kv_w2048"]]
        out_caches = [outs["a_w128_sample"], outs["a_w512_sample"], outs["a_w2048_sample"]]

        def copy_piece(sp, g, n):
            kept, pieces = (GROUPS[g][0] - 1) * ROW, CACHE_PIECES[g]
            src = caches[g][0].rearrange("s x w h d -> (s x) (w h d)")[:, ROW:]
            dst = out_caches[g][0].rearrange("s x w h d -> (s x) (w h d)")[:, 0:kept]
            sp.dma_start(dst.rearrange("r (n e) -> r n e", n=pieces)[:, n, :],
                         src.rearrange("r (n e) -> r n e", n=pieces)[:, n, :]).then_inc(copied, 16)

        def ffn_turn_sp(sp, z):
            l, g = z.l, 2 * z.i
            load(sp, wcols(up_w[l], g + FC), *z.unit(1))
            load(sp, wcols(up_w[l], g + 1), *z.unit(2))
            load(sp, wcols(up_w[l], g + 1 + FC), *z.unit(3))
            copy_piece(sp, 2, FFN_TURNS * l + z.i)
            if not z.last:
                load(sp, wcols(up_w[l], g + 2), *z.unit(4))
            for e in range(2):
                load(sp, down_unit(l, g + e), *z.unit(z.d0 + e))

        def ffn_sp(sp, l):
            load(sp, wcols(up_w[l], 0), [U_FFN0, U_FFN1][l])
            turns(sp, l, ffn_turn_sp)

        def tails_sp(sp, l):
            sp.wait_ge(tail_set, 2 * l + 2)
            sp.dma_start(outs["ffn_conv_prompt"][l, 0].rearrange("t (c f) -> (t c) f", f=P),
                         tail_sb[0:4 * FC, 0:P]).then_inc(tail_out, 16)
            for s in range(NS):
                r = 2 * FC * (s % 2)
                sp.dma_start(outs["ffn_conv_sample"][l, s, 1].rearrange("(c f) -> c f", f=P),
                             tail_sb[r:r + 2 * FC, P * (1 + s // 2):P * (2 + s // 2)]).then_inc(tail_out, 16)

        EXPORTS = [(0, 7, 1), (1, 4, 4), (2, 0, 4), (2, 4, 4)]

        class Buffers:
            def __init__(self, M):
                if M.ng > 1:
                    vt, pt, self.mrow, bm, self.stg, self.o_raw = carve(
                        24 * 192, 3 * 512, SEQ, 2 * M.cols, 2 * P + 3 * 512, SEQ)
                    self.q = [[x[:, 4 + g, 0:SEQ].bitcast(F32) for x in (xh, xl)] for g in range(NG)]
                    self.k = [x.bitcast(F32) for x in (f_hi[:, 0, 0:SEQ], f_hi[:, 1, 0:SEQ], f_lo[:, 0, 0:SEQ])]
                    self.v = [x.bitcast(F32) for x in (xh[:, 7, 0:SEQ], xl[:, 7, 0:SEQ], f_lo[:, 1, 0:SEQ])]
                    self.padded = [self.q[g][h] for g in range(NG) for h in range(2)]
                else:
                    q0, q1, k0, k1, vt, pt, self.mrow, bm, self.o_raw, self.e_row = carve(
                        SEQ, SEQ, SEQ, SEQ, 8 * 192, 3 * 512, SEQ, 2 * M.cols, SEQ, SEQ)
                    self.q, self.k, self.v = [q0, q1], [k0, k1], [f_hi[:, 0, 0:SEQ].bitcast(F32)]
                    self.padded = self.k
                self.ng = M.ng
                self.vt = vt.rearrange("p (t c) -> p t c", c=192)
                self.pt = pt
                self.bm = bm.rearrange("p (h c) -> p h c", h=2)
                self.o = self.mrow

            def stage(self, what, s):
                if s == 0:
                    return self.stg[:, P * (what == "v"):P * (what == "v") + P]
                x = self.stg[:, 2 * P:] if what == "k" else self.pt
                return x[:, 512 * (s - 1):512 * s]

            def queries(self, g, hh, slot):
                return self.q[g][hh] if self.ng > 1 else self.q[slot]

            def keys(self, g, hh):
                return self.k[g] if self.ng > 1 else self.k[hh]

        BUF = {id(M): Buffers(M) for M in (MA, MB)}

        def moves(M):
            vt = [("t", g, t, 4) for g in range(M.ng) for t in (0, 4)]
            if M.ng == 1:
                return vt
            return vt + [("v", *e) for e in EXPORTS] + [("k", *e) for e in EXPORTS]

        def moves_pe(pe, M, S, it, r):
            B, nb, NM = BUF[id(M)], len(M.batches), len(moves(M))
            pe.wait_ge(S.v_in, 16 * (3 if M.ng > 1 else 2) * (r + 1))
            for n, (what, g, t0, cnt) in enumerate(moves(M)):
                if n < 6:
                    pe.wait_ge(S.sc_exp, 2 * nb * it)
                else:
                    pe.wait_ge(S.copied, NM * r + n - 5)
                if what == "k":
                    pe.wait_ge(S.k_in, 48 * (r + 1))
                src = B.k[g] if what == "k" else B.v[g]
                for e in range(cnt):
                    x = tile_tokens(src, g, t0 + e) if what == "t" else src[:, P * (t0 + e):P * (t0 + e) + P]
                    mm = pe.transpose(acc[:, n % 6, P * e:P * e + P], x, ident)
                mm.then_inc(S.moved, 1)

        def moves_dve(v_, M, S, it, r):
            B, nb, NM = BUF[id(M)], len(M.batches), len(moves(M))
            for n, (what, g, t0, cnt) in enumerate(moves(M)):
                v_.wait_ge(S.moved, NM * r + n + 1)
                if what == "t":
                    v_.wait_ge(S.pv, PV0[id(M)] + 2 * nb * it)
                    v_.tensor_copy(B.vt[:, 8 * g + t0:8 * g + t0 + 4, :]
                                   .rearrange("p t (a b) -> p t a b", b=HD)[:, :, 0:3:2, :],
                                   acc[:, n % 6, :].rearrange("p (t a b) -> p t a b", t=4, a=2)).then_inc(S.copied, 1)
                else:
                    v_.wait_ge(S.exported, 128 * r)
                    s = [e[0:2] for e in EXPORTS].index((g, t0))
                    v_.tensor_copy(B.stage(what, s), acc[:, n % 6, 0:P * cnt]).then_inc(S.copied, 1)

        def max_rows(M, g):
            banks = [aux[0:2, 0:2, :], acc[0:2, 2:4, :], acc[0:2, 4:6, :]][g if M.ng > 1 else 2]
            return banks.rearrange("p a n -> p (a n)")

        def attn_pe(pe, M, S, it, r, slot=0):
            B, nb, NM = BUF[id(M)], len(M.batches), len(moves(M))
            if M.ng == 1:
                pe.wait_ge(S.k_in, 32 * (r + 1))
                pe.wait_ge(S.q_in[slot], 8 * (it - slot) + 16)
            for hh in range(2):
                for b, (g, kind, blocks) in enumerate(M.batches):
                    n = nb * hh + b
                    if M.ng > 1 and hh == 0:
                        pe.wait_ge(S.q_in[g], 32 * (r + 1))
                    if n < 6:
                        pe.wait_ge(S.copied, NM * (r + 1))
                        pe.wait_ge(S.sc_exp, 2 * nb * it)
                    else:
                        pe.wait_ge(S.maxed, 2 * nb * it + n - 5)
                    w = len(blocks) * P
                    pe.matmul(acc[:, n % 6, 0:w], ident_b[:],
                              masks[:, 0, kind, :].unsqueeze(1).to_broadcast([P, len(blocks), P]),
                              start=True, stop=False)
                    for e, (tq, tk, _) in enumerate(blocks):
                        mm = pe.matmul(acc[:, n % 6, P * e:P * e + P], tile_tokens(B.queries(g, hh, slot), g, tq),
                                       tile_tokens(B.keys(g, hh), g, tk), start=False, stop=e == len(blocks) - 1)
                    mm.then_inc(S.scored, 1)
            pe.wait_ge(S.merged, it + 1)
            for g in range(M.ng):
                for t in range(NTILE):
                    mm = pe.transpose(max_rows(M, g)[:, P * t:P * t + P], B.bm[:, :, 8 * g + t], ident)
                mm.then_inc(S.turned, 1)
            early = 2 if M.ng > 1 else 4

            def scores_open(n):
                hh, b = divmod(n, nb)
                g, kind, blocks = M.batches[b]
                if early <= n < 6:
                    pe.wait_ge(S.shift, it + 1)
                elif n >= 6:
                    pe.wait_ge(S.sc_exp, 2 * nb * it + n - 5)
                w = len(blocks) * P
                pe.matmul(acc[:, n % 6, 0:w], ident_b[:],
                          masks[:, 1, kind, :].unsqueeze(1).to_broadcast([P, len(blocks), P]),
                          start=True, stop=False)
                for e, (tq, tk, _) in enumerate(blocks):
                    pe.matmul(acc[:, n % 6, P * e:P * e + P], tile_tokens(B.keys(g, hh), g, tk),
                              tile_tokens(B.queries(g, hh, slot), g, tq), start=False, stop=False)

            def scores_shift(n):
                hh, b = divmod(n, nb)
                g, kind, blocks = M.batches[b]
                pe.matmul(acc[:, n % 6, 0:len(blocks) * P], sel[:, hh, :],
                          batch_tokens(neg_max[:, :], g, kind, blocks), start=False, stop=True) \
                    .then_inc(S.sc_full, 1)

            def values(n):
                hh, b = divmod(n, nb)
                g, kind, blocks = M.batches[b]
                pe.wait_ge(S.sc_exp, 2 * nb * it + n + 1)
                if b == 0:
                    pe.wait_ge(S.o_out, 2 * it + hh)
                o = aux[:, :, :].rearrange("p a n -> p (a n)")
                vc = slice(HD * hh, HD * hh + P)
                probs = B.pt[:, 512 * (n % 3):512 * (n % 3) + 512]
                if M.ng == 1 and b == nb - 1:
                    for half in range(2):
                        pe.matmul(aux[:, half, :], sel_den[:, hh, :], B.e_row[0:2, 512 * half:512 * half + 512],
                                  start=False, stop=False, skip_group_check=True)
                for e, (tq, tk, _) in enumerate(blocks):
                    pe_ = probs[:, P * e:P * e + P]
                    kw = dict(start=b < 2 and e == 0, stop=b == nb - 1, skip_group_check=True)
                    if g < 2:
                        mm = pe.matmul(tile_tokens(o, g, tq), B.vt[:, 8 * g + tk, vc], pe_, **kw)
                    else:
                        for half in range(0, P, HD):
                            mm = pe.matmul(tile_tokens(o, g, tq)[:, half:half + HD], B.vt[:, 8 * g + tk, vc],
                                           pe_[:, half:half + HD], **kw)
                mm.then_inc(S.pv, 1)

            for n in range(early):
                scores_open(n)
            pe.wait_ge(S.shift, it + 1)
            for n in range(early):
                scores_shift(n)
            for n in range(2 * nb):
                if n + 1 >= early and n + 1 < 2 * nb:
                    scores_open(n + 1)
                    scores_shift(n + 1)
                values(n)

        def head_rows_of(hh):
            return slice(HD * hh, HD * hh + HD), slice(HD * (1 - hh), HD * (1 - hh) + HD)

        def attn_act(act, M, S, it):
            B, nb, pv0 = BUF[id(M)], len(M.batches), PV0[id(M)]
            if M.ng == 1:
                act.wait_ge(S.shift, it + 1)
                act.wait_ge(S.pv, pv0 + 2 * nb * it)
                act.activation(B.e_row[0:2, :], neg_max[:, :].bitcast(F32), ACT.Exp, bias=sink_now[:],
                               scale=SCALE)

            def reciprocals(hh):
                rows, den = head_rows_of(hh)
                act.wait_ge(S.o_out, 2 * it + hh + 1)
                act.activation(rinv[rows, 0:SEQ], B.o_raw[den, :], ACT.Ln).then_inc(S.o_ln, 1)
                act.wait_ge(S.o_ln, 2 * it + hh + 1)
                act.activation(rinv[rows, 0:SEQ], rinv[rows, 0:SEQ], ACT.Exp, scale=-1.0).then_inc(S.o_rec, 1)

            if M.ng > 1:
                act.wait_ge(S.exported, 128 * (it + 1))
            for n in range(2 * nb):
                w = len(M.batches[n % nb][2]) * P
                act.wait_ge(S.sc_full, 2 * nb * it + n + 1)
                act.wait_ge(S.pv, pv0 + 2 * nb * it + max(0, n - 2))
                act.activation(B.pt[:, 512 * (n % 3):512 * (n % 3) + w], acc[:, n % 6, 0:w], ACT.Exp, scale=SCALE) \
                    .then_inc(S.sc_exp, 1)
                if n == nb + 1:
                    reciprocals(0)
            reciprocals(1)
            act.wait_ge(S.o_norm, 2 * it + 2)
            act.copy(xh[:, it, 0:SEQ], B.o).then_inc(S.o_hi, 1)

        def attn_pool(pool, M, S, it):
            B = BUF[id(M)]
            for hh in range(2):
                rows, _ = head_rows_of(hh)
                pool.wait_ge(S.o_rec, 2 * it + hh + 1)
                if hh == 0:
                    pool.wait_ge(S.o_lo, it)
                pool.tensor_tensor(B.o[rows, :], B.o_raw[rows, :], rinv[rows, 0:SEQ], ALU.mult).then_inc(S.o_norm, 1)
            pool.wait_ge(S.o_hi, it + 1)
            pool.sem_inc(S.o_go, 1)
            pool.tensor_tensor(xl[:, it, 0:SEQ], B.o, xh[:, it, 0:SEQ].bitcast(F32), ALU.subtract).then_inc(S.o_lo, 1)

        def clear_dve(v_, M, S):
            B = BUF[id(M)]
            for n, x in enumerate(B.padded):
                other = HD * (1 - n % 2)
                v_.memset(x[other:other + HD, :], 0.0)
            v_.memset(B.vt[:, :, HD:2 * HD], 1.0).then_inc(S.cleared, 1)

        def attn_dve(v_, M, S, it):
            B, nb, pv0 = BUF[id(M)], len(M.batches), PV0[id(M)]
            bm = B.bm
            for hh in range(2):
                for b, (g, kind, blocks) in enumerate(M.batches):
                    n = nb * hh + b
                    c0 = blocks[0][2]
                    v_.wait_ge(S.scored, 2 * nb * it + n + 1)
                    if n == 0:
                        v_.wait_ge(S.turned, M.ng * it)
                    v_.tensor_reduce(bm[:, hh, c0:c0 + len(blocks)],
                                     acc[:, n % 6, 0:P * len(blocks)].rearrange("p (e n) -> p e n", n=P),
                                     AX_X, ALU.max).then_inc(S.maxed, 1)
            v_.wait_ge(S.maxed, 2 * nb * (it + 1))
            c1 = 8 * M.ng
            if M.ng > 1:
                v_.tensor_tensor(bm[:, :, 9:16:2], bm[:, :, 9:16:2], bm[:, :, c1 + 7:c1 + 11], ALU.max)
            v_.tensor_tensor(bm[:, :, 1:8], bm[:, :, 1:8], bm[:, :, c1:c1 + 7], ALU.max).then_inc(S.merged, 1)
            for g in range(M.ng):
                v_.wait_ge(S.turned, M.ng * it + g + 1)
                src = max_rows(M, g)
                if g == M.ng - 1:
                    v_.wait_ge(S.pv, pv0 + 2 * nb * it)
                if M.ng == 1:
                    v_.tensor_copy(sink_now[:], sink[:, bass.ds(it, 1)])
                    v_.tensor_scalar(neg_max[:, :], src, sink8[:, bass.ds(it, 1)], -1.0, ALU.max, ALU.mult) \
                        .then_inc(S.shift, 1)
                elif g == 0:
                    v_.wait_ge(S.o_lo, it)
                    v_.tensor_scalar(B.mrow[0:2, :], src, -1.0, None, ALU.mult).then_inc(S.rowed, 1)
                else:
                    v_.wait_ge(S.rowed, 2 * it + g)
                    m, to = [x.rearrange("p (n s) -> p s n", s=4 * g) for x in
                             (B.mrow[0:2, :], neg_max[:, :] if g == 2 else B.mrow[0:2, :])]
                    v_.scalar_tensor_tensor(to, src.rearrange("p (s n) -> p s n", s=4 * g), -1.0, m,
                                            ALU.mult, ALU.min).then_inc(S.shift if g == 2 else S.rowed, 1)
            for hh in range(2):
                v_.wait_ge(S.pv, pv0 + 2 * nb * it + nb * (hh + 1))
                v_.wait_ge(S.o_norm, 2 * it + hh)
                v_.tensor_copy(B.o_raw, aux[:, :, :].rearrange("p a n -> p (a n)")).then_inc(S.o_out, 1)

        def attn_a_sp(sp, i):
            B, S, M = BUF[id(MA)], SA, MA
            nb, NM = len(M.batches), len(moves(M))
            chunk = lambda w, g: scratch[12 * w + 4 * g:12 * w + 4 * g + 4].rearrange("c p t -> p c t")[:, i, 0:SEQ]
            for g in range(NG):
                sp.dma_start(B.v[g], chunk(2, g)).then_inc(S.v_in, 16)
            sp.wait_ge(S.pv, 2 * nb * i)
            for g in range(NG):
                sp.dma_start(B.k[g], chunk(1, g)).then_inc(S.k_in, 16)
            for g in range(NG):
                for h in range(2):
                    sp.dma_start(B.q[g][h][HD * h:HD * h + HD, :], chunk(0, g)[HD * h:HD * h + HD, :]) \
                        .then_inc(S.q_in[g], 16)
            outs_g = [outs["a_w128_prompt"], outs["a_w512_prompt"], outs["a_w2048_prompt"]]
            for w in (1, 0):
                for s, (g, t0, cnt) in enumerate(EXPORTS):
                    sp.wait_ge(S.copied, NM * i + 10 - 4 * w + s + 1)
                    sp.sem_inc(S.seen, 1)
                    kept = min(GROUPS[g][0], SEQ)
                    first = t0 - (SEQ - kept) // P
                    dst = outs_g[g][0, 0, w].rearrange("(t p) (j h) d -> p t j (h d)", p=P, j=A_PAIRS)
                    sp.dma_start(dst[:, first:first + cnt, i, :],
                                 B.stage("kv"[w], s).rearrange("p (t c) -> p t c", c=P)) \
                        .then_inc(S.exported, 16)
            copy_piece(sp, 0, i)

        PAIRS_KV = B_CHUNKS // 2

        def attn_b_sp(sp, kv):
            B, S, nb = BUF[id(MB)], SB, len(MB.batches)
            sp.wait_ge(S.pv, PV0[id(MB)] + 2 * nb * PAIRS_KV * kv)
            rows = scratch[A_CHUNKS:A_CHUNKS + 2, HD * kv:HD * kv + HD, 0:SEQ]
            for half in (0, HD):
                sp.dma_start(B.v[0][half:half + HD, :], rows[1]).then_inc(S.v_in, 16)
            for h in range(2):
                sp.dma_start(B.k[h][HD * h:HD * h + HD, :], rows[0]).then_inc(S.k_in, 16)
            qs = scratch[A_CHUNKS + 2 + PAIRS_KV * kv:A_CHUNKS + 2 + PAIRS_KV * (kv + 1)].rearrange("(i e) p t -> p e i t", e=2)
            with sp.Fori(0, PAIRS_KV // 2) as i:
                for e in range(2):
                    sp.wait_ge(S.pv, 2 * nb * (PAIRS_KV * kv + 2 * i + e))
                    sp.dma_start(B.q[e], qs[:, e, i, 0:SEQ]).then_inc(S.q_in[e], 16)
                    copy_piece(sp, 1, PAIRS_KV * kv + 2 * i + e)

        CROW = A_PAIRS * P
        STEPS_A = NG * NS // 2
        s_r0, s_r1, s_r2, s_r3, s_r4, s_r5, s_all, s_pT, s_dg, s_D, s_kvn, s_stc, s_prod, s_red, s_of, s_cols = carve(
            *[1024] * 6, 387, 192, 192, 192, 24 * P, 192, 96, 8, 32, 36 * NS)
        s_ring, s_mul = [s_r0, s_r1, s_r2, s_r3], [s_r4, s_r5]
        RS = len(s_ring)
        s_ring = [x.rearrange("p (a n) -> p a n", a=2) for x in s_ring]
        s_qh, s_ql = [x[0:NS, 4:6, :].rearrange("p k t -> p (k t)")[:, 0:NG * CROW] for x in (xh, xl)]
        s_sel = xh[0:NS, 6, 0:NS * P].rearrange("p (s n) -> p s n", n=P)
        s_cols = s_cols.rearrange("p (c s) -> p c s", s=NS)

        FIRST = 3

        def sample_a_sp(sp):
            nb = len(MA.batches)

            def cache_rows(n):
                w, (g, s2) = n // STEPS_A, divmod(n % STEPS_A, NS // 2)
                m = n - RS
                if 0 <= m < STEPS_A:
                    sp.wait_ge(ZA.multiplied, m + 1)
                elif m >= 0:
                    sp.wait_ge(ZA.pe, m - STEPS_A + 1)
                src = caches[g][0, 2 * s2:2 * s2 + 2, w].rearrange("s (n d) h e -> n d s (h e)", d=GROUPS[g][1])
                sp.dma_start(s_ring[n % RS], src[:, 0]).then_inc(ZA.cache[n % RS], 16)

            sp.dma_start(s_cols, scratch[0:A_CHUNKS, :, SEQ:T].rearrange("c p t -> p c t")).then_inc(ZA.cols, 16)
            for n in (3, 4):
                load(sp, wcols(w_aout, n % 4, 2 * P), U_AOUT + n)
            sp.wait_ge(SA.pv, 2 * nb * A_PAIRS)
            for n in range(2 * STEPS_A):
                cache_rows(n)
            sp.wait_ge(ZA.kept, 2 * NG)
            for w2 in range(2):
                for g2 in range(NG):
                    sp.dma_start(out_caches[g2][0, :, w2, GROUPS[g2][0] - 1].rearrange("s h d -> s (h d)"),
                                 s_kvn[0:NS, CROW * (3 * w2 + g2):CROW * (3 * w2 + g2) + CROW]).then_inc(ZA.out, 16)

        def sample_a_pe(pe):
            nb = len(MA.batches)
            pe.wait_ge(SA.sc_exp, 2 * nb * A_PAIRS)
            pe.wait_ge(SA.o_out, 2 * A_PAIRS)
            pe.wait_ge(ZA.cols, 16)
            for g in range(NG):
                for e in range(4):
                    mm = pe.transpose(acc[0:NS, g, P * e:P * e + P], s_cols[:, 4 * g + e, :], ident)
                mm.then_inc(ZA.moved, 1)
            pe.wait_ge(ZA.prep, 2)
            for g in range(NG):
                for h in range(2):
                    pe.matmul(aux[32 * h:32 * h + 32, 1, g:g + 1],
                              s_prod[HD * h:HD * h + HD, 32 * g:32 * g + 32], ones[HD * h:HD * h + HD, 0:1],
                              start=True, stop=True)
            pe.wait_ge(ZA.split, NG)
            for n in range(STEPS_A):
                g, s2 = divmod(n, NS // 2)
                if n >= 2:
                    pe.wait_ge(ZA.multiplied, n - 1)
                for e in range(2):
                    for x in (s_qh, s_ql):
                        mm = pe.matmul(acc[:, (2 * n + e) % 4, :], s_sel[:, 2 * s2 + e, :],
                                       x[:, CROW * g:CROW * g + CROW], start=x is s_qh, stop=x is s_ql)
                mm.then_inc(ZA.spread, 1)
                if 0 <= n - FIRST < PIECES // 2:
                    aout_first_pe(pe, n - FIRST)
                b = n - (STEPS_A - 2 * NG)
                if b >= 0:
                    if b:
                        pe.wait_ge(ZA.kept, b)
                    for e in range(4):
                        mm = pe.transpose(aux[0:NS, 0, P * e:P * e + P], s_cols[:, 12 + 4 * b + e, :], ident)
                    mm.then_inc(ZA.moved, 1)
            pe.wait_ge(ZA.summed, STEPS_A)
            for g in range(NG):
                mm = pe.transpose(acc[0:64, 0, P * g:P * g + P], s_stc[:, 64 * g:64 * g + 64], ident)
            mm.then_inc(ZA.moved, 1)
            pe.wait_ge(ZA.step, 8)
            for g in range(NG):
                pe.transpose(acc[:, 1, 64 * g:64 * g + 64], s_all[0:64, P * g:P * g + P], ident[0:64, 0:64])
            pe.matmul(acc[0:NS, 2, 0:192], cst[0:64, C_E64:C_E64 + NS], s_dg[0:64, :], start=True, stop=True) \
                .then_inc(ZA.moved, 1)
            pe.wait_ge(ZA.step, 10)
            for n in range(STEPS_A):
                g, s2 = divmod(n, NS // 2)
                r = STEPS_A + n
                pe.wait_ge(ZA.cache[r % RS], 16 * (r // RS + 1))
                for e in range(2):
                    s = 2 * s2 + e
                    for c in range(4):
                        mm = pe.matmul(acc[:, 3, 16 * c + 2 * s:16 * c + 2 * s + 2],
                                       s_ring[r % RS][:, e, P * c:P * c + P],
                                       s_pT[:, 64 * g + 8 * c + s:64 * g + 8 * c + s + 33:32],
                                       start=(n == 0 and e == 0 and c == 0), stop=False, skip_group_check=True)
                mm.then_inc(ZA.pe, 1)
                if n < PIECES // 2:
                    aout_first_pe(pe, PIECES // 2 + n)
            pe.wait_ge(ZA.kept, 2 * NG)
            for g in range(NG):
                for c in range(4):
                    mm = pe.matmul(acc[:, 3, 16 * c:16 * c + 16].rearrange("p (s h) -> p s h", h=2),
                                   s_kvn[0:NS, CROW * (3 + g) + P * c:CROW * (3 + g) + P * c + P],
                                   s_D[0:NS, 64 * g:64 * g + 64].rearrange("p (h c s) -> p c s h", h=2, c=4)[:, c],
                                   start=False, stop=True, skip_group_check=True)
            mm.then_inc(ZA.pe, 1)

        def head_sums(v, n):
            g, s2 = divmod(n, NS // 2)
            to = s_stc.rearrange("p (g h c s) -> p g s c h", g=NG, h=2, s=NS)
            v.wait_ge(ZA.multiplied, n + 1)
            for e in range(2):
                ins = v.tensor_reduce(to[:, g, 2 * s2 + e], s_mul[n % 2][:, 512 * e:512 * e + 512]
                                      .rearrange("p (c h d) -> p c h d", h=2, d=HD), AX_X, ALU.add)
            ins.then_inc(ZA.summed, 1)

        def sample_a_dve(v):
            v.wait_ge(SA.pv, 2 * len(MA.batches) * A_PAIRS)
            v.tensor_copy(s_sel, ident[0:NS, 0:NS].unsqueeze(2).to_broadcast([NS, NS, P])).then_inc(ZA.prep, 1)
            v.wait_ge(ZA.cols, 16)
            v.tensor_tensor(s_prod.rearrange("p (c s) -> p c s", s=NS), s_cols[:, 0:12, :], s_cols[:, 12:24, :],
                            ALU.mult).then_inc(ZA.prep, 1)
            for b in range(NG):
                q = slice(CROW * b, CROW * b + CROW)
                v.wait_ge(ZA.moved, b + 1)
                v.tensor_copy(s_qh[:, q], acc[0:NS, b, :]).then_inc(ZA.kt, 1)
                v.wait_ge(ZA.kt, b + 1)
                v.tensor_tensor(s_ql[:, q], acc[0:NS, b, :], s_qh[:, q].bitcast(F32), ALU.subtract) \
                    .then_inc(ZA.split, 1)

            for n in range(STEPS_A):
                v.wait_ge(ZA.cache[n % RS], 16 * (n // RS + 1))
                v.wait_ge(ZA.spread, n + 1)
                if n >= 2:
                    v.wait_ge(ZA.summed, n - 1)
                v.tensor_tensor(s_mul[n % 2].rearrange("p (a n) -> p a n", a=2), s_ring[n % RS],
                                acc[:, 2 * n % 4:2 * n % 4 + 2, :], ALU.mult).then_inc(ZA.multiplied, 1)
                if n:
                    head_sums(v, n - 1)
                if 0 <= n - 1 - FIRST < PIECES // 2:
                    aout_first_dve(v, n - 1 - FIRST)
            head_sums(v, STEPS_A - 1)
            v.wait_ge(ZA.moved, 10)
            v.tensor_copy(s_all[0:64, 0:384], acc[0:64, 0, 0:384]).then_inc(ZA.step, 1)
            v.tensor_copy(s_all[0:64, 384:387], aux[0:64, 1, 0:NG]).then_inc(ZA.step, 1)
            v.wait_ge(ZA.step, 2)
            v.tensor_reduce(s_red[0:64, 0:1], s_all[0:64, :], AX_X, ALU.max).then_inc(ZA.step, 1)
            v.wait_ge(ZA.step, 3)
            v.tensor_scalar(s_red[0:64, 1:2], s_red[0:64, 0:1], -SCALE, None, ALU.mult).then_inc(ZA.step, 1)
            v.wait_ge(ZA.act, 1)
            v.reciprocal(s_red[0:64, 3:4], s_red[0:64, 2:3]).then_inc(ZA.step, 1)
            v.wait_ge(ZA.step, 5)
            v.tensor_scalar(s_all[0:64, :], s_all[0:64, :], s_red[0:64, 3:4], None, ALU.mult).then_inc(ZA.step, 1)
            v.wait_ge(ZA.step, 6)
            for g in range(NG):
                ins = v.tensor_scalar(s_dg[0:64, 64 * g:64 * g + 64], ident[0:64, 0:64],
                                      s_all[0:64, 384 + g:385 + g], None, ALU.mult)
                if g:
                    ins.then_inc(ZA.step, 1)
            v.wait_ge(ZA.moved, 11)
            v.tensor_copy(s_pT, acc[:, 1, 0:192]).then_inc(ZA.step, 1)
            v.tensor_copy(s_D[0:NS, :], acc[0:NS, 2, 0:192]).then_inc(ZA.step, 1)
            for n in range(PIECES // 2, PIECES):
                aout_first_dve(v, n)
            v.wait_ge(ZA.pe, STEPS_A + 1)
            for h in range(2):
                v.tensor_copy(s_of[HD * h:HD * h + HD, :],
                              acc[HD * h:HD * h + HD, 3, 0:64].rearrange("p (n h) -> p n h", h=2)[:, :, h]) \
                    .then_inc(ZA.step, 1)
            v.wait_ge(ZA.step, 12)
            v.wait_ge(ZA.act, 2)
            v.tensor_tensor(xl[:, 0:4, SEQ:T], s_of.rearrange("p (c s) -> p c s", s=NS),
                            xh[:, 0:4, SEQ:T].bitcast(F32), ALU.subtract).then_inc(ZA.fin, 1)

        def sample_a_act(act):
            split_ahead(act, U_AOUT)
            act.wait_ge(SA.o_lo, A_PAIRS)
            for b in range(2 * NG):
                if b == 0:
                    split_ahead(act, U_AOUT + 1)
                act.wait_ge(ZA.moved, NG + b + 1)
                act.copy(s_kvn[0:NS, CROW * b:CROW * b + CROW], aux[0:NS, 0, :]).then_inc(ZA.kept, 1)
            split_ahead(act, U_AOUT + 2)
            act.wait_ge(ZA.step, 4)
            act.activation(s_all[0:64, :], s_all[0:64, :], ACT.Exp, bias=s_red[0:64, 1:2], scale=SCALE,
                           accum_out=s_red[0:64, 2:3]).then_inc(ZA.act, 1)
            act.wait_ge(ZA.step, 12)
            act.copy(xh[:, 0:4, SEQ:T], s_of.rearrange("p (c s) -> p c s", s=NS)).then_inc(ZA.act, 1)

        NH = 2 * B_CHUNKS
        b_kt, b_qb, b_prod, b_stc, b_all, b_pT, b_dg, b_D, b_kvn, b_red, b_of, b_rows = carve(
            NS * P, P, P, P, 130, P, P, P, 256, 8, 64, 256)
        b_k, b_v = rope[:, 0, 0:NS * P], rope[:, 1, 0:NS * P]
        b_cols, b_new = carve(10 * T, 10 * NS, 256)[1:]
        b_cols = b_cols.rearrange("p (c s) -> p c s", s=NS)
        b_qb = b_qb.rearrange("p (h s) -> p h s", s=NS)
        b_of = b_of.rearrange("p (c s) -> p c s", s=NS)

        def sample_b_sp(sp):
            sp.dma_start(b_cols, scratch[A_CHUNKS:46, :, SEQ:T].rearrange("c p t -> p c t")).then_inc(ZB.cols, 16)
            sp.dma_start(b_new.rearrange("p (c t) -> p c t", c=2),
                         scratch[A_CHUNKS:A_CHUNKS + 2, :, SEQ - P:SEQ].rearrange("c p t -> p c t")) \
                .then_inc(ZB.cols, 16)
            for w, x in enumerate((b_k, b_v)):
                sp.dma_start(x.rearrange("p (s c) -> p s c", s=NS),
                             a["cache_b_kv"][:, w].rearrange("s w h d -> w s (h d)")).then_inc(ZB.cache[w], 16)
            sp.wait_ge(ZB.kt, 2)
            for w in range(2):
                sp.dma_start(outs["b_kv_sample"][:, w, P - 1].rearrange("s h d -> s (h d)"),
                             b_kvn[0:NS, P * w:P * w + P]).then_inc(ZB.out, 16)
                sp.dma_start(outs["b_kv_prompt"][0, w].rearrange("t h d -> t (h d)"),
                             b_rows[:, P * w:P * w + P]).then_inc(ZB.out, 16)

        def sample_b_pe(pe):
            nb = len(MB.batches)
            pe.wait_ge(SB.sc_exp, 2 * nb * B_CHUNKS)
            pe.wait_ge(SB.o_out, 2 * B_CHUNKS)
            pe.wait_ge(ZB.cols, 32)
            for w in range(2):
                mm = pe.transpose(acc[0:NS, 5, P * w:P * w + P], b_cols[:, w, :], ident)
            mm.then_inc(ZB.moved, 1)
            for w in range(2):
                mm = pe.transpose(acc[:, 4, P * w:P * w + P], b_new[:, P * w:P * w + P], ident)
            mm.then_inc(ZB.moved, 1)
            pe.wait_ge(ZB.cache[0], 16)
            for s in range(NS):
                mm = pe.transpose(acc[:, s // 4, P * (s % 4):P * (s % 4) + P], b_k[:, P * s:P * s + P], ident)
            mm.then_inc(ZB.moved, 1)
            pe.wait_ge(ZB.prep, 6)
            pe.matmul(aux[:, 1, 0:1], b_prod, ones[:, 0:1], start=True, stop=True)
            pe.wait_ge(ZB.kt, 4)
            for s in range(NS):
                mm = pe.matmul(aux[:, 0, s:s + 8 * (NH - 1) + 1:8], b_kt[:, P * s:P * s + P], b_qb[:, :, s],
                               start=True, stop=True)
            mm.then_inc(ZB.scored, 1)
            pe.wait_ge(ZB.step, 1)
            pe.transpose(acc[:, 2, 0:P], b_stc, ident).then_inc(ZB.moved, 1)
            pe.wait_ge(ZB.step, 10)
            pe.transpose(acc[:, 3, 0:P], b_all[:, 0:P], ident)
            pe.matmul(acc[0:NS, 1, 0:P], cst[:, C_E128:C_E128 + NS], b_dg, start=True, stop=True).then_inc(ZB.moved, 1)
            pe.wait_ge(ZB.step, 12)
            pe.wait_ge(ZB.cache[1], 16)
            for s in range(NS):
                pe.matmul(acc[:, 0, s:s + 8 * (NH - 1) + 1:8], b_v[:, P * s:P * s + P],
                          b_pT[:, s:s + 8 * (NH - 1) + 1:8], start=(s == 0), stop=False, skip_group_check=True)
            pe.matmul(acc[:, 0, 0:P], b_kvn[0:NS, P:2 * P], b_D[0:NS, :], start=False, stop=True,
                      skip_group_check=True).then_inc(ZB.pe, 1)

        def sample_b_dve(v):
            v.wait_ge(ZB.cols, 32)
            v.memset(b_qb, 0.0).then_inc(ZB.prep, 1)
            v.wait_ge(ZB.prep, 1)
            for kv in range(2):
                for h in range(2):
                    v.tensor_copy(b_qb[HD * kv:HD * kv + HD, 8 * kv + h:8 * kv + 8:2, :],
                                  b_cols[HD * h:HD * h + HD, 2 + 4 * kv:6 + 4 * kv, :]).then_inc(ZB.prep, 1)
            v.wait_ge(ZB.prep, 5)
            v.tensor_tensor(b_prod.rearrange("p (h s) -> p h s", s=NS), b_qb,
                            b_cols[:, 0, :].unsqueeze(1).to_broadcast([P, NH, NS]), ALU.mult).then_inc(ZB.prep, 1)
            v.wait_ge(ZB.moved, 1)
            v.tensor_copy(b_kvn[0:NS, :], acc[0:NS, 5, 0:256]).then_inc(ZB.kt, 1)
            v.wait_ge(ZB.moved, 2)
            v.tensor_copy(b_rows, acc[:, 4, 0:256]).then_inc(ZB.kt, 1)
            v.wait_ge(ZB.moved, 3)
            for half in range(2):
                v.tensor_copy(b_kt[:, 512 * half:512 * half + 512], acc[:, half, :]).then_inc(ZB.kt, 1)
            v.wait_ge(ZB.scored, 1)
            v.tensor_copy(b_stc, aux[:, 0, 0:P]).then_inc(ZB.step, 1)
            v.wait_ge(ZB.moved, 4)
            v.tensor_copy(b_all[:, 0:P], acc[:, 2, 0:P]).then_inc(ZB.step, 1)
            v.tensor_copy(b_all[:, P:P + 1], aux[:, 1, 0:1]).then_inc(ZB.step, 1)
            v.tensor_copy(b_all[:, P + 1:P + 2], sink_col[:]).then_inc(ZB.step, 1)
            v.wait_ge(ZB.step, 2)
            v.memset(b_all[:, 0:1], MASKED).then_inc(ZB.step, 1)
            v.wait_ge(ZB.step, 5)
            v.tensor_reduce(b_red[:, 0:1], b_all, AX_X, ALU.max).then_inc(ZB.step, 1)
            v.wait_ge(ZB.step, 6)
            v.tensor_scalar(b_red[:, 1:2], b_red[:, 0:1], -SCALE, None, ALU.mult).then_inc(ZB.step, 1)
            v.wait_ge(ZB.act, 1)
            v.reciprocal(b_red[:, 3:4], b_red[:, 2:3]).then_inc(ZB.step, 1)
            v.wait_ge(ZB.step, 8)
            v.tensor_scalar(b_all, b_all, b_red[:, 3:4], None, ALU.mult).then_inc(ZB.step, 1)
            v.wait_ge(ZB.step, 9)
            v.tensor_scalar(b_dg, ident, b_all[:, P:P + 1], None, ALU.mult).then_inc(ZB.step, 1)
            v.wait_ge(ZB.moved, 5)
            v.tensor_copy(b_pT, acc[:, 3, 0:P]).then_inc(ZB.step, 1)
            v.tensor_copy(b_D[0:NS, :], acc[0:NS, 1, 0:P]).then_inc(ZB.step, 1)
            v.wait_ge(ZB.pe, 1)
            for kv in range(2):
                for h in range(2):
                    v.tensor_copy(b_of[HD * h:HD * h + HD, 4 * kv:4 * kv + 4, :],
                                  acc[HD * kv:HD * kv + HD, 0, 0:P].rearrange("p (h s) -> p h s", s=NS)
                                  [:, 8 * kv + h:8 * kv + 8:2, :]).then_inc(ZB.step, 1)
            v.wait_ge(ZB.step, 16)
            v.wait_ge(ZB.act, 2)
            v.tensor_tensor(xl[:, :, SEQ:T], b_of, xh[:, :, SEQ:T].bitcast(F32), ALU.subtract).then_inc(ZB.fin, 1)

        def sample_b_act(act):
            act.wait_ge(ZB.step, 7)
            act.activation(b_all, b_all, ACT.Exp, bias=b_red[:, 1:2], scale=SCALE,
                           accum_out=b_red[:, 2:3]).then_inc(ZB.act, 1)
            act.wait_ge(ZB.step, 16)
            act.copy(xh[:, :, SEQ:T], b_of).then_inc(ZB.act, 1)

        yp = outs["y_prompt"].rearrange("b s d -> (b s) d")
        ys = outs["y_sample"].rearrange("b s d -> (b s) d")

        def rows_out_pe(pe):
            pe.wait_ge(h_added, ADDED[1] + KC * FFN_TURNS)
            for n in range(NTILE + 1):
                rows = P if n < NTILE else NS
                if n >= 3:
                    pe.wait_ge(y_set, 2 * (n - 3) + 2)
                for c in range(KC):
                    mm = pe.transpose(acc[0:rows, (2 * n + c // 4) % 6, P * (c % 4):P * (c % 4) + P],
                                      hT[:, c, P * n:P * n + rows], ident)
                mm.then_inc(y_turned, 1)

        def rows_out_dve(v):
            for n in range(NTILE + 1):
                rows = P if n < NTILE else NS
                v.wait_ge(y_turned, n + 1)
                if n >= 2:
                    v.wait_ge(y_out[n % 2], 16 * (n // 2))
                for b in range(2):
                    v.tensor_copy(y_stage[n % 2][0:rows, 512 * b:512 * b + 512], acc[0:rows, (2 * n + b) % 6, :]) \
                        .then_inc(y_set, 1)

        def rows_out_sp(sp):
            for n in range(NTILE + 1):
                sp.wait_ge(y_set, 2 * n + 2)
                if n < NTILE:
                    sp.dma_start(yp[P * n:P * n + P, :], y_stage[n % 2]).then_inc(y_out[n % 2], 16)
                else:
                    sp.dma_start(ys, y_stage[n % 2][0:NS]).then_inc(y_out[n % 2], 16)

        def copies_sp(sp):
            copy_piece(sp, 2, CACHE_PIECES[2] - 1)
            sp.dma_start(outs["b_kv_sample"][:, :, 0:P - 1].rearrange("s x w h d -> (s x) (w h d)"),
                         a["cache_b_kv"][:, :, 1:P].rearrange("s x w h d -> (s x) (w h d)")).then_inc(copied, 16)
            for l in range(2):
                sp.dma_start(outs["ffn_conv_sample"][l, :, 0], a["state_ffn_conv"][l, :, 1]).then_inc(copied, 16)
        COPIES = sum(CACHE_PIECES) + 1 + 2

        block = ctx.enter_context(nc.Block())

        @block.sync
        def _(sp):
            rows_in_sp(sp)
            conv_tables_sp(sp)
            proj_a_sp(sp)
            for k in range(2):
                sp.wait_ge(stored[k], 16 * A_CHUNKS // 2)
            with sp.Fori(0, A_PAIRS) as i:
                attn_a_sp(sp, i)
            sample_a_sp(sp)
            for n in range(5, 8):
                load(sp, wcols(w_aout, n % 4, 2 * P), U_AOUT + n)
            ffn_sp(sp, 0)
            for n in range(3):
                load(sp, wcols([a["b_w_kv"], a["b_w_kv"], w_q][n], [0, 1, 0][n]), U_KV + n)
            tails_sp(sp, 0)
            proj_b_sp(sp)
            for k in range(2):
                sp.wait_ge(stored[k], 16 * 46 // 2)
            for kv in range(2):
                attn_b_sp(sp, kv)
            sample_b_sp(sp)
            for n in range(3, KC):
                load(sp, wcols(w_bout, n), U_BOUT + n)
            copies_sp(sp)
            ffn_sp(sp, 1)
            tails_sp(sp, 1)
            rows_out_sp(sp)
            sp.wait_ge(y_out[0], 16 * 5)
            sp.wait_ge(y_out[1], 16 * 4)
            sp.wait_ge(tail_out, 16 * TAILS * 2)
            sp.wait_ge(ZA.out, 16 * 6)
            sp.wait_ge(ZB.out, 16 * 4)
            sp.wait_ge(SA.exported, 16 * 8 * A_PAIRS)
            sp.wait_ge(copied, 16 * COPIES)

        @block.gpsimd
        def _(pool):
            pool.sem_inc(lo_ready, RING)
            units_pool(pool, U_QKV, U_QKV + 2)
            norm_pool(pool, 0)
            units_pool(pool, U_QKV + 2, U_AOUT + 2)
            with pool.Fori(0, A_PAIRS) as i:
                attn_pool(pool, MA, SA, i)
            units_pool(pool, U_AOUT + 2, U_FFN0 + 2)
            norm_pool(pool, 1)
            units_pool(pool, U_FFN0 + 2, U_KV + 2)
            norm_pool(pool, 2)
            units_pool(pool, U_KV + 2, U_BQ + 2)
            norm_pool(pool, 3)
            units_pool(pool, U_BQ + 2, U_BOUT + 2)
            with pool.Fori(0, B_CHUNKS) as i:
                attn_pool(pool, MB, SB, i)
            units_pool(pool, U_BOUT + 2, U_FFN1 + 2)
            norm_pool(pool, 4)
            units_pool(pool, U_FFN1 + 2, U_END)

        @block.scalar
        def _(act):
            act.preload_act_table_set("natural_log_exp_and_others")
            counts_act(act)
            split_hi(act, U_QKV)
            split_hi(act, U_QKV + 1)
            act.wait_ge(const_set, CONSTS_SET)
            for k in range(KC):
                square_act(act, 0, k, lambda e: e.wait_ge(h_set, 2 * (NTILE + 1)))
            norm_act(act, 0)
            proj_a_act(act)
            with act.Fori(0, A_PAIRS) as i:
                attn_act(act, MA, SA, i)
            sample_a_act(act)
            aout_act(act)
            ffn_act(act, 0)
            norm_act(act, 2)
            act.wait_ge(tail_out, 16 * TAILS)
            proj_b_act(act)
            with act.Fori(0, B_CHUNKS) as i:
                attn_act(act, MB, SB, i)
            sample_b_act(act)
            bout_act(act)
            ffn_act(act, 1)

        @block.vector
        def _(v):
            v.sem_inc(chunk_out, 3 * CH)
            rows_in_dve(v)
            consts_dve(v)
            for k in range(KC):
                square_dve(v, 0, k)
            norm_dve(v, 0)
            proj_a_dve(v)
            conv_tables_dve(v)
            for k in range(2):
                v.wait_ge(stored[k], 16 * A_CHUNKS // 2)
            clear_dve(v, MA, SA)
            with v.Fori(0, A_PAIRS) as i:
                moves_dve(v, MA, SA, i, i)
                attn_dve(v, MA, SA, i)
            sample_a_dve(v)
            aout_dve(v)
            ffn_dve(v, 0)
            norm_dve(v, 2)
            proj_b_dve(v)
            for k in range(2):
                v.wait_ge(stored[k], 16 * 46 // 2)
            clear_dve(v, MB, SB)
            for kv in range(2):
                moves_dve(v, MB, SB, PAIRS_KV * kv, kv)
                with v.Fori(0, PAIRS_KV) as i:
                    attn_dve(v, MB, SB, PAIRS_KV * kv + i)
            sample_b_dve(v)
            bout_dve(v)
            ffn_dve(v, 1)
            rows_out_dve(v)

        @block.tensor
        def _(pe):
            counts_pe(pe)
            rows_in_pe(pe)
            pe.wait_ge(const_set, CONSTS_SET)
            norm_pe(pe, 0)
            proj_a_pe(pe)
            conv_tables_pe(pe)
            pe.wait_ge(SA.cleared, 1)
            with pe.Fori(0, A_PAIRS) as i:
                moves_pe(pe, MA, SA, i, i)
                attn_pe(pe, MA, SA, i, i)
            sample_a_pe(pe)
            aout_pe(pe)
            ffn_pe(pe, 0)
            proj_b_pe(pe)
            pe.wait_ge(chunk_out, 3 * (CH_B + 2 + B_CHUNKS))
            pe.wait_ge(SB.cleared, 1)
            pe.sem_inc(SB.pv, PV0[id(MB)])
            for kv in range(2):
                moves_pe(pe, MB, SB, PAIRS_KV * kv, kv)
                with pe.Fori(0, PAIRS_KV // 2) as i:
                    for e in range(2):
                        attn_pe(pe, MB, SB, PAIRS_KV * kv + 2 * i + e, kv, slot=e)
            sample_b_pe(pe)
            bout_pe(pe)
            ffn_pe(pe, 1)
            rows_out_pe(pe)


INPUTS = ["x_prompt", "x_sample", "cache_a_kv_w128", "cache_a_kv_w512", "cache_a_kv_w2048", "cache_b_kv",
          "state_ffn_conv", "attn_norm_g", "ffn_norm_g", "a_w_in", "a_q_norm_g", "a_k_norm_g", "a_w_out",
          "b_kv_norm_g", "b_w_kv", "b_k_norm_g", "b_w_q", "b_q_norm_g", "b_sinks", "b_w_out",
          "ffn_w_up", "ffn_conv_w", "ffn_conv_b", "ffn_w_down"]
OUTPUTS = [
    ("y_prompt", (1, SEQ, D)), ("y_sample", (NS, 1, D)),
    ("a_w128_prompt", (1, 1, 2, 128, 8, HD)), ("a_w128_sample", (1, NS, 2, 128, 8, HD)),
    ("a_w512_prompt", (1, 1, 2, 512, 8, HD)), ("a_w512_sample", (1, NS, 2, 512, 8, HD)),
    ("a_w2048_prompt", (1, 1, 2, SEQ, 8, HD)), ("a_w2048_sample", (1, NS, 2, 2048, 8, HD)),
    ("b_kv_prompt", (1, 2, 128, 2, HD)), ("b_kv_sample", (NS, 2, 128, 2, HD)),
    ("ffn_conv_prompt", (2, 1, 2, 2 * DFF)), ("ffn_conv_sample", (2, NS, 2, 2 * DFF)),
]


def kernel(**inputs):
    import concourse.bacc as bacc
    from concourse.bass_utils import run_bass_kernel_spmd

    nc = bacc.Bacc("TRN2", target_bir_lowering=False, num_devices=1, dynamic_dma_scratch_size=1024)
    arrays, a, outs = {}, {}, {}
    for name in INPUTS:
        arrays["in_" + name] = np.ascontiguousarray(inputs[name])
    arrays["in_consts"] = shape_constants()
    for name, x in arrays.items():
        a[name[3:]] = nc.dram_tensor(name, x.shape, F32, kind="ExternalInput").ap()
    for name, shape in OUTPUTS:
        outs[name] = nc.dram_tensor("out_" + name, shape, F32, kind="ExternalOutput").ap()
    build(nc, a, outs)
    r = run_bass_kernel_spmd(nc, [arrays], core_ids=[0])
    return tuple(r.results[0]["out_" + name] for name, _ in OUTPUTS)
```
